# Optimizing a Trainium2 kernel written in Bass

```python
import math
import jax, jax.numpy as jnp
from jax import lax
import numpy as np

D_MODEL = 2048
BATCH = 1
SEQ = 256
DEPTH = 1

PLE_DIM = 256
MIX_WIDTH = D_MODEL
LRU_WIDTH = MIX_WIDTH // 2
LRU_BLOCKS = 16
LRU_BLOCK_DIM = LRU_WIDTH // LRU_BLOCKS
CONV_WIDTH = 4
LRU_C = 8.0
HEAD_DIM = 64
N_HEADS = (MIX_WIDTH - LRU_WIDTH) // HEAD_DIM
N_KV = 4
HEADS_PER_KV = N_HEADS // N_KV
KV_W = N_KV * HEAD_DIM
CMP_LEN = 32
CMP_STRIDE = 16
CMP_HIDDEN = 256
SEL_BLOCK = 64
N_SELECT = 16
N_LOCAL_FORCED = 2
WINDOW = 512
Q_BLOCK = 128
SEL_Q_CHUNK = 32
N_BUCKETS = 32
MAX_DISTANCE = 128
D_FF = 4 * D_MODEL
NORM_EPS = 1e-6
NEG_INF = -1e30
FORCE_SCORE = 1e4

IN_SIZES = (LRU_WIDTH, LRU_WIDTH, N_HEADS * HEAD_DIM, KV_W, KV_W, KV_W, KV_W, KV_W, KV_W, 3 * N_HEADS)
IN_DIM = sum(IN_SIZES)
SPLIT_POINTS = tuple(int(v) for v in np.cumsum(IN_SIZES)[:-1])


def rms_norm(x, g):
    xf = x.astype(jnp.float32)
    y = xf * lax.rsqrt(jnp.mean(xf * xf, axis=-1, keepdims=True) + NORM_EPS)
    return (y * g.astype(jnp.float32)).astype(x.dtype)

def rel_bucket(dist):
    n = jnp.maximum(dist, 0)
    max_exact = N_BUCKETS // 2
    nf = jnp.maximum(n, 1).astype(jnp.float32)
    large = max_exact + (jnp.log(nf / max_exact) / math.log(MAX_DISTANCE / max_exact)
                         * (N_BUCKETS - max_exact)).astype(jnp.int32)
    large = jnp.minimum(large, N_BUCKETS - 1)
    return jnp.where(n < max_exact, n, large)

def rglru_mixer(u, gate_in, conv_w, conv_b, wa, ba, wx, bx, lam):
    B, S = u.shape[0], u.shape[1]
    up = jnp.pad(u, ((0, 0), (CONV_WIDTH - 1, 0), (0, 0)))
    xc = conv_b + sum(up[:, k:k + S] * conv_w[k] for k in range(CONV_WIDTH))
    xb = xc.reshape(B, S, LRU_BLOCKS, LRU_BLOCK_DIM)
    r = jax.nn.sigmoid(jnp.einsum('bsni,nij->bsnj', xb, wa) + ba).reshape(B, S, LRU_WIDTH)
    ig = jax.nn.sigmoid(jnp.einsum('bsni,nij->bsnj', xb, wx) + bx).reshape(B, S, LRU_WIDTH)
    log_a = -LRU_C * r.astype(jnp.float32) * jax.nn.softplus(-lam.astype(jnp.float32))
    a = jnp.exp(log_a)
    b = jnp.sqrt(-jnp.expm1(2.0 * log_a)) * (ig * xc).astype(jnp.float32)

    def combine(left, right):
        a1, b1 = left
        a2, b2 = right
        return a1 * a2, a2 * b1 + b2

    _, h = lax.associative_scan(combine, (a, b), axis=1)
    return h.astype(u.dtype) * jax.nn.gelu(gate_in)

def nsa_mixer(q, k_c, v_c, k_s, v_s, k_w, v_w, gates,
              pe_k, w1_k, w2_k, pe_v, w1_v, w2_v, rel_bias):
    B, S = q.shape[0], q.shape[1]
    G, R, dk = N_KV, HEADS_PER_KV, HEAD_DIM
    q = q.reshape(B, S, G, R, dk)
    k_c, v_c, k_s, v_s, k_w, v_w = [t.reshape(B, S, G, dk) for t in (k_c, v_c, k_s, v_s, k_w, v_w)]
    scale = dk ** -0.5
    pos = jnp.arange(S, dtype=jnp.int32)
    bias_tab = rel_bias.astype(jnp.float32).reshape(N_BUCKETS, G, R)

    n_cmp = (S - CMP_LEN) // CMP_STRIDE + 1
    cmp_idx = np.arange(n_cmp)[:, None] * CMP_STRIDE + np.arange(CMP_LEN)[None, :]

    def compress(t, pe, w1, w2):
        blk = t[:, cmp_idx] + pe[:, None, :]
        blk = blk.transpose(0, 1, 3, 2, 4).reshape(B, n_cmp, G, CMP_LEN * dk)
        return jax.nn.gelu(blk @ w1) @ w2

    kc = compress(k_c, pe_k, w1_k, w2_k)
    vc = compress(v_c, pe_v, w1_v, w2_v)
    cmp_end = jnp.asarray(np.arange(n_cmp) * CMP_STRIDE + CMP_LEN - 1, dtype=jnp.int32)
    dist_c = pos[:, None] - cmp_end[None, :]
    valid_c = dist_c >= 0
    bias_c = bias_tab[rel_bucket(dist_c)].transpose(2, 3, 0, 1)
    s_c = jnp.einsum('bsgrd,bngd->bgrsn', q, kc).astype(jnp.float32) * scale + bias_c
    s_c = jnp.where(valid_c, s_c, NEG_INF)
    any_c = (pos >= CMP_LEN - 1)[:, None]
    p_c = jax.nn.softmax(s_c, axis=-1) * any_c
    o_c = jnp.einsum('bgrsn,bngd->bsgrd', p_c.astype(vc.dtype), vc)

    n_sel = S // SEL_BLOCK
    ratio_sel = SEL_BLOCK // CMP_STRIDE
    ratio_cmp = CMP_LEN // CMP_STRIDE
    jj_np = np.arange(n_sel)[:, None, None]
    ci = ratio_sel * jj_np + np.arange(ratio_sel)[None, :, None] - np.arange(ratio_cmp)[None, None, :]
    jb = np.broadcast_to(jj_np, ci.shape)
    ok = (ci >= 0) & (ci < n_cmp)
    M = np.zeros((n_cmp, n_sel), np.float32)
    np.add.at(M, (ci[ok], jb[ok]), 1.0)
    imp = jnp.einsum('bgrsn,nj->bgsj', p_c, jnp.asarray(M))
    jj = jnp.arange(n_sel, dtype=jnp.int32)
    dblk = (pos // SEL_BLOCK)[:, None] - jj[None, :]
    forced = (jj[None, :] == 0) | ((dblk >= 0) & (dblk < N_LOCAL_FORCED))
    causal_blk = dblk >= 0
    imp = jnp.where(forced, FORCE_SCORE, jnp.where(causal_blk, imp, -FORCE_SCORE))
    n_top = min(N_SELECT, n_sel)
    _, sel_idx = lax.top_k(imp, n_top)

    kb = k_s.reshape(B, n_sel, SEL_BLOCK, G, dk).transpose(0, 3, 1, 2, 4)
    vb = v_s.reshape(B, n_sel, SEL_BLOCK, G, dk).transpose(0, 3, 1, 2, 4)
    n_ch = S // SEL_Q_CHUNK
    q_ch = q.reshape(B, n_ch, SEL_Q_CHUNK, G, R, dk).transpose(1, 0, 2, 3, 4, 5)
    idx_ch = sel_idx.reshape(B, G, n_ch, SEL_Q_CHUNK, n_top).transpose(2, 0, 1, 3, 4)
    pos_ch = pos.reshape(n_ch, SEL_Q_CHUNK)
    b_ar = jnp.arange(B)[:, None, None]
    g_ar = jnp.arange(G)[None, :, None]
    g_ar4 = jnp.arange(G)[None, :, None, None]
    n_keys = n_top * SEL_BLOCK
    in_blk = jnp.arange(SEL_BLOCK, dtype=jnp.int32)

    def sel_chunk(args):
        qc, ic, tc = args
        flat = ic.reshape(B, G, SEL_Q_CHUNK * n_top)
        ks = kb[b_ar, g_ar, flat].reshape(B, G, SEL_Q_CHUNK, n_keys, dk)
        vs = vb[b_ar, g_ar, flat].reshape(B, G, SEL_Q_CHUNK, n_keys, dk)
        kpos = (ic[..., None] * SEL_BLOCK + in_blk).reshape(B, G, SEL_Q_CHUNK, n_keys)
        dist = tc[None, None, :, None] - kpos
        bias = bias_tab[rel_bucket(dist), g_ar4].transpose(0, 1, 4, 2, 3)
        s = jnp.einsum('bqgrd,bgqkd->bgrqk', qc, ks).astype(jnp.float32) * scale + bias
        s = jnp.where((dist >= 0)[:, :, None], s, NEG_INF)
        pr = jax.nn.softmax(s, axis=-1)
        return jnp.einsum('bgrqk,bgqkd->bqgrd', pr.astype(vs.dtype), vs)

    o_s = lax.map(sel_chunk, (q_ch, idx_ch, pos_ch))
    o_s = o_s.transpose(1, 0, 2, 3, 4, 5).reshape(B, S, G, R, dk)

    n_qb = S // Q_BLOCK
    band = Q_BLOCK + WINDOW
    kw_pad = jnp.pad(k_w, ((0, 0), (WINDOW, 0), (0, 0), (0, 0)))
    vw_pad = jnp.pad(v_w, ((0, 0), (WINDOW, 0), (0, 0), (0, 0)))
    kj = jnp.arange(band, dtype=jnp.int32)[None, :]
    dist_w = WINDOW + jnp.arange(Q_BLOCK, dtype=jnp.int32)[:, None] - kj
    band_ok = (dist_w >= 0) & (dist_w < WINDOW)
    bias_w = bias_tab[rel_bucket(dist_w)].transpose(2, 3, 0, 1)
    q_blk = q.reshape(B, n_qb, Q_BLOCK, G, R, dk).transpose(1, 0, 2, 3, 4, 5)
    starts = jnp.arange(n_qb, dtype=jnp.int32) * Q_BLOCK

    def win_block(args):
        qb, st = args
        kw = lax.dynamic_slice_in_dim(kw_pad, st, band, axis=1)
        vw = lax.dynamic_slice_in_dim(vw_pad, st, band, axis=1)
        ok_w = band_ok & (st - WINDOW + kj >= 0)
        s = jnp.einsum('bqgrd,bkgd->bgrqk', qb, kw).astype(jnp.float32) * scale + bias_w
        s = jnp.where(ok_w, s, NEG_INF)
        pr = jax.nn.softmax(s, axis=-1)
        return jnp.einsum('bgrqk,bkgd->bqgrd', pr.astype(vw.dtype), vw)

    o_w = lax.map(win_block, (q_blk, starts))
    o_w = o_w.transpose(1, 0, 2, 3, 4, 5).reshape(B, S, G, R, dk)

    gt = jax.nn.sigmoid(gates).reshape(B, S, G, R, 3)
    o = gt[..., 0:1] * o_c + gt[..., 1:2] * o_s + gt[..., 2:3] * o_w
    return o.reshape(B, S, N_HEADS * dk)

def first_inputs(seed: int = 0) -> dict:
    key = jax.random.key(seed)
    ks = jax.random.split(key, 32)
    f32 = jnp.float32

    def nrm(k, shape, scale):
        return jax.random.normal(k, shape, f32) * scale

    def gain(k, shape):
        return 1.0 + 0.05 * jax.random.normal(k, shape, f32)

    a0 = jax.random.uniform(ks[10], (DEPTH, LRU_WIDTH), f32, 0.9, 0.999)
    return {
        "x": nrm(ks[0], (BATCH, SEQ, D_MODEL), 1.0),
        "p": nrm(ks[1], (DEPTH, BATCH, SEQ, PLE_DIM), 1.0),
        "norm_mix_pre": gain(ks[2], (DEPTH, D_MODEL)),
        "norm_mix_post": gain(ks[3], (DEPTH, D_MODEL)),
        "norm_mlp_pre": gain(ks[4], (DEPTH, D_MODEL)),
        "norm_mlp_post": gain(ks[5], (DEPTH, D_MODEL)),
        "w_in": nrm(ks[6], (DEPTH, D_MODEL, IN_DIM), D_MODEL ** -0.5),
        "conv_w": nrm(ks[7], (DEPTH, CONV_WIDTH, LRU_WIDTH), CONV_WIDTH ** -0.5),
        "conv_b": nrm(ks[8], (DEPTH, LRU_WIDTH), 0.02),
        "lru_wa": nrm(ks[9], (DEPTH, LRU_BLOCKS, LRU_BLOCK_DIM, LRU_BLOCK_DIM), LRU_BLOCK_DIM ** -0.5),
        "lru_ba": nrm(ks[11], (DEPTH, LRU_BLOCKS, LRU_BLOCK_DIM), 0.02),
        "lru_wx": nrm(ks[12], (DEPTH, LRU_BLOCKS, LRU_BLOCK_DIM, LRU_BLOCK_DIM), LRU_BLOCK_DIM ** -0.5),
        "lru_bx": nrm(ks[13], (DEPTH, LRU_BLOCKS, LRU_BLOCK_DIM), 0.02),
        "lru_lambda": jnp.log(a0 / (1.0 - a0)),
        "cmp_pe_k": nrm(ks[14], (DEPTH, CMP_LEN, HEAD_DIM), 0.1),
        "cmp_w1_k": nrm(ks[15], (DEPTH, CMP_LEN * HEAD_DIM, CMP_HIDDEN), (CMP_LEN * HEAD_DIM) ** -0.5),
        "cmp_w2_k": nrm(ks[16], (DEPTH, CMP_HIDDEN, HEAD_DIM), CMP_HIDDEN ** -0.5),
        "cmp_pe_v": nrm(ks[17], (DEPTH, CMP_LEN, HEAD_DIM), 0.1),
        "cmp_w1_v": nrm(ks[18], (DEPTH, CMP_LEN * HEAD_DIM, CMP_HIDDEN), (CMP_LEN * HEAD_DIM) ** -0.5),
        "cmp_w2_v": nrm(ks[19], (DEPTH, CMP_HIDDEN, HEAD_DIM), CMP_HIDDEN ** -0.5),
        "rel_bias": nrm(ks[20], (N_BUCKETS, N_HEADS), 0.1),
        "gnorm_lru": gain(ks[21], (DEPTH, LRU_WIDTH)),
        "gnorm_nsa": gain(ks[22], (DEPTH, N_HEADS * HEAD_DIM)),
        "w_out": nrm(ks[23], (DEPTH, MIX_WIDTH, D_MODEL), MIX_WIDTH ** -0.5),
        "mlp_w1": nrm(ks[24], (DEPTH, D_MODEL, D_FF), D_MODEL ** -0.5),
        "mlp_w2": nrm(ks[25], (DEPTH, D_FF, D_MODEL), D_FF ** -0.5),
        "ple_gate": nrm(ks[26], (DEPTH, D_MODEL, D_MODEL), D_MODEL ** -0.5),
        "ple_proj": nrm(ks[27], (DEPTH, PLE_DIM, D_MODEL), PLE_DIM ** -0.5),
    }

def first_block(x, p, norm_mix_pre, norm_mix_post, norm_mlp_pre, norm_mlp_post, w_in,
              conv_w, conv_b, lru_wa, lru_ba, lru_wx, lru_bx, lru_lambda,
              cmp_pe_k, cmp_w1_k, cmp_w2_k, cmp_pe_v, cmp_w1_v, cmp_w2_v, rel_bias,
              gnorm_lru, gnorm_nsa, w_out, mlp_w1, mlp_w2, ple_gate, ple_proj):
    h = x
    for i in range(DEPTH):
        a = rms_norm(h, norm_mix_pre[i])
        z = a @ w_in[i]
        u, g_lru, q, kc, vc, ksel, vsel, kw, vw, gts = jnp.split(z, SPLIT_POINTS, axis=-1)
        y_lru = rglru_mixer(u, g_lru, conv_w[i], conv_b[i], lru_wa[i], lru_ba[i],
                            lru_wx[i], lru_bx[i], lru_lambda[i])
        y_nsa = nsa_mixer(q, kc, vc, ksel, vsel, kw, vw, gts,
                          cmp_pe_k[i], cmp_w1_k[i], cmp_w2_k[i],
                          cmp_pe_v[i], cmp_w1_v[i], cmp_w2_v[i], rel_bias)
        y = jnp.concatenate([rms_norm(y_lru, gnorm_lru[i]), rms_norm(y_nsa, gnorm_nsa[i])], axis=-1)
        h = h + rms_norm(y @ w_out[i], norm_mix_post[i])
        f = jnp.square(jax.nn.relu(rms_norm(h, norm_mlp_pre[i]) @ mlp_w1[i])) @ mlp_w2[i]
        h = h + rms_norm(f, norm_mlp_post[i])
        h = h + jax.nn.sigmoid(h @ ple_gate[i]) * (p[i] @ ple_proj[i])
    return h


DEPTH_2 = 2

N_EVEN = (DEPTH_2 + 1) // 2
N_ODD = DEPTH_2 // 2

SB_HEADS = 8
SB_HEAD_DIM = 128
SB_WIDTH = SB_HEADS * SB_HEAD_DIM
SB_BLOCK = 128
GLA_HEADS = 8
GLA_DK = 64
GLA_DV = 128
GLA_K_WIDTH = GLA_HEADS * GLA_DK
GLA_V_WIDTH = GLA_HEADS * GLA_DV
GLA_GATE_RANK = 16
GLA_GATE_TAU = 16.0
GLA_CHUNK = 64
IN_SPLITS = [SB_WIDTH, 2 * SB_WIDTH, 3 * SB_WIDTH,
             3 * SB_WIDTH + GLA_K_WIDTH,
             3 * SB_WIDTH + 2 * GLA_K_WIDTH,
             3 * SB_WIDTH + 2 * GLA_K_WIDTH + GLA_V_WIDTH,
             3 * SB_WIDTH + 2 * GLA_K_WIDTH + 2 * GLA_V_WIDTH]
IN_WIDTH = 3 * SB_WIDTH + 2 * GLA_K_WIDTH + 2 * GLA_V_WIDTH + GLA_GATE_RANK
MIX_WIDTH_2 = SB_WIDTH + GLA_V_WIDTH
S5_GROUP = 16
S5_GROUPS = D_MODEL // S5_GROUP
S5_STATE = 64
S5_DT_MIN = 1e-3
S5_DT_MAX = 1e-1
D_FF_2 = ((8 * D_MODEL + 3 * 256 - 1) // (3 * 256)) * 256


def rms_norm_2(x, g):
    xf = x.astype(jnp.float32)
    return xf * lax.rsqrt(jnp.mean(xf * xf, axis=-1, keepdims=True) + NORM_EPS) * g.astype(jnp.float32)

def split_heads(t, n_heads):
    b_, l_, w_ = t.shape
    return t.reshape(b_, l_, n_heads, w_ // n_heads).transpose(0, 2, 1, 3)

def merge_heads(t):
    b_, h_, l_, d_ = t.shape
    return t.transpose(0, 2, 1, 3).reshape(b_, l_, h_ * d_)

def stick_breaking_attention(q, k, v):
    b_, h_, L, d = q.shape
    nblk = L // SB_BLOCK
    scale = d ** -0.5
    q_blocks = q.reshape(b_, h_, nblk, SB_BLOCK, d).transpose(2, 0, 1, 3, 4)
    starts = jnp.arange(nblk, dtype=jnp.int32) * SB_BLOCK
    kpos = jnp.arange(L, dtype=jnp.int32)

    def one_block(args):
        qb, start = args
        qpos = start + jnp.arange(SB_BLOCK, dtype=jnp.int32)
        mask = kpos[None, :] < qpos[:, None]
        z = jnp.einsum('bhqd,bhkd->bhqk', qb, k) * scale
        log_keep = jnp.where(mask, jax.nn.log_sigmoid(-z), 0.0)
        later = lax.cumsum(log_keep, axis=3, reverse=True) - log_keep
        w = jnp.where(mask, jnp.exp(jax.nn.log_sigmoid(z) + later), 0.0)
        return jnp.einsum('bhqk,bhkd->bhqd', w, v)

    out = lax.map(one_block, (q_blocks, starts))
    return out.transpose(1, 2, 0, 3, 4).reshape(b_, h_, L, d)

def gla_chunked(q, k, v, log_a):
    b_, h_, L, dk = q.shape
    dv = v.shape[-1]
    nc = L // GLA_CHUNK

    def to_chunks(t):
        return t.reshape(b_, h_, nc, GLA_CHUNK, t.shape[-1]).transpose(2, 0, 1, 3, 4)

    tpos = jnp.arange(GLA_CHUNK)
    incl = (tpos[None, :] <= tpos[:, None])[:, :, None]

    def step(S, xs):
        qc, kc, vc, lac = xs
        cum = jnp.cumsum(lac, axis=2)
        cum_last = cum[:, :, -1:, :]
        inter = jnp.einsum('bhtd,bhde->bhte', qc * jnp.exp(cum), S)
        diff = cum[:, :, :, None, :] - cum[:, :, None, :, :]
        decay = jnp.exp(jnp.where(incl, diff, -jnp.inf))
        scores = jnp.einsum('bhtsd,bhsd->bhts', qc[:, :, :, None, :] * decay, kc)
        intra = jnp.einsum('bhts,bhse->bhte', scores, vc)
        S_new = jnp.exp(cum_last[:, :, 0, :, None]) * S + jnp.einsum(
            'bhsd,bhse->bhde', kc * jnp.exp(cum_last - cum), vc)
        return S_new, inter + intra

    S0 = jnp.zeros((b_, h_, dk, dv), jnp.float32)
    _, out = lax.scan(step, S0, (to_chunks(q), to_chunks(k), to_chunks(v), to_chunks(log_a)))
    return out.transpose(1, 2, 0, 3, 4).reshape(b_, h_, L, dv)

def sb_gla_mixer(h, w_in, w_gate_up, b_gate, gla_norm_gain, w_out):
    proj = (h @ w_in).astype(jnp.float32)
    sb_q, sb_k, sb_v, g_q, g_k, g_v, g_r, g_lr = jnp.split(proj, IN_SPLITS, axis=-1)
    o_sb = stick_breaking_attention(split_heads(sb_q, SB_HEADS),
                                    split_heads(sb_k, SB_HEADS),
                                    split_heads(sb_v, SB_HEADS))
    o_sb = merge_heads(o_sb)
    gate_logits = g_lr @ w_gate_up.astype(jnp.float32) + b_gate.astype(jnp.float32)
    log_a = jax.nn.log_sigmoid(gate_logits) / GLA_GATE_TAU
    o_gla = gla_chunked(split_heads(g_q, GLA_HEADS) * (GLA_DK ** -0.5),
                        split_heads(g_k, GLA_HEADS),
                        split_heads(g_v, GLA_HEADS),
                        split_heads(log_a, GLA_HEADS))
    o_gla = o_gla * lax.rsqrt(jnp.mean(o_gla * o_gla, axis=-1, keepdims=True) + NORM_EPS)
    o_gla = merge_heads(o_gla) * gla_norm_gain.astype(jnp.float32) * jax.nn.silu(g_r)
    return jnp.concatenate([o_sb, o_gla], axis=-1) @ w_out

def s5_mixer(h, lam_re, lam_im, log_step, b_re, b_im, c_re, c_im, d_skip, w_glu):
    b_, L, _ = h.shape
    u = h.astype(jnp.float32).reshape(b_, L, S5_GROUPS, S5_GROUP)
    lam_re = lam_re.astype(jnp.float32)
    lam_im = lam_im.astype(jnp.float32)
    dt = jnp.exp(log_step.astype(jnp.float32))[:, None]
    mag = jnp.exp(dt * lam_re)
    ang = dt * lam_im
    lb_re, lb_im = mag * jnp.cos(ang), mag * jnp.sin(ang)
    den = lam_re * lam_re + lam_im * lam_im
    nr, ni = lb_re - 1.0, lb_im
    cr = (nr * lam_re + ni * lam_im) / den
    ci = (ni * lam_re - nr * lam_im) / den
    b_re = b_re.astype(jnp.float32)
    b_im = b_im.astype(jnp.float32)
    bb_re = cr[..., None] * b_re - ci[..., None] * b_im
    bb_im = cr[..., None] * b_im + ci[..., None] * b_re
    bu_re = jnp.einsum('blgh,gph->blgp', u, bb_re)
    bu_im = jnp.einsum('blgh,gph->blgp', u, bb_im)
    a_re = jnp.broadcast_to(lb_re, (1, L) + lb_re.shape)
    a_im = jnp.broadcast_to(lb_im, (1, L) + lb_im.shape)

    def combine(e1, e2):
        a1r, a1i, x1r, x1i = e1
        a2r, a2i, x2r, x2i = e2
        return (a1r * a2r - a1i * a2i,
                a1r * a2i + a1i * a2r,
                a2r * x1r - a2i * x1i + x2r,
                a2r * x1i + a2i * x1r + x2i)

    _, _, s_re, s_im = lax.associative_scan(combine, (a_re, a_im, bu_re, bu_im), axis=1)
    y = (jnp.einsum('ghp,blgp->blgh', c_re.astype(jnp.float32), s_re)
         - jnp.einsum('ghp,blgp->blgh', c_im.astype(jnp.float32), s_im)
         + d_skip.astype(jnp.float32).reshape(S5_GROUPS, S5_GROUP) * u)
    y = jax.nn.gelu(y.reshape(b_, L, D_MODEL), approximate=False)
    val, gate = jnp.split(y @ w_glu, 2, axis=-1)
    return val * jax.nn.sigmoid(gate)

def swiglu_ffn(h, w_ffn_in, w_ffn_out):
    gate, up = jnp.split(h @ w_ffn_in, 2, axis=-1)
    return (jax.nn.silu(gate) * up) @ w_ffn_out

def second_inputs(seed: int = 0) -> dict:
    key = jax.random.key(seed)
    ks = jax.random.split(key, 20)
    f32 = jnp.float32
    n = lambda k, shape, s: jax.random.normal(k, shape, f32) * s
    x = jax.random.normal(ks[0], (BATCH, SEQ, D_MODEL), f32)
    norm_gains = 1.0 + n(ks[1], (DEPTH_2, 4, D_MODEL), 0.02)
    w_in = n(ks[2], (N_EVEN, D_MODEL, IN_WIDTH), D_MODEL ** -0.5)
    w_gate_up = n(ks[3], (N_EVEN, GLA_GATE_RANK, GLA_K_WIDTH), GLA_GATE_RANK ** -0.5)
    b_gate = n(ks[4], (N_EVEN, GLA_K_WIDTH), 0.1)
    gla_norm_gain = 1.0 + n(ks[5], (N_EVEN, GLA_V_WIDTH), 0.02)
    w_out = n(ks[6], (N_EVEN, MIX_WIDTH_2, D_MODEL), MIX_WIDTH_2 ** -0.5)
    s5_lambda_re = -0.5 * jnp.exp(n(ks[7], (N_ODD, S5_GROUPS, S5_STATE), 0.05))
    s5_lambda_im = (math.pi * jnp.arange(S5_STATE, dtype=f32))[None, None, :] \
        + n(ks[8], (N_ODD, S5_GROUPS, S5_STATE), 0.01)
    s5_log_step = jax.random.uniform(ks[9], (N_ODD, S5_GROUPS), f32,
                                     math.log(S5_DT_MIN), math.log(S5_DT_MAX))
    bs = (2.0 * S5_GROUP) ** -0.5
    s5_b_re = n(ks[10], (N_ODD, S5_GROUPS, S5_STATE, S5_GROUP), bs)
    s5_b_im = n(ks[11], (N_ODD, S5_GROUPS, S5_STATE, S5_GROUP), bs)
    cs = (2.0 * S5_STATE) ** -0.5
    s5_c_re = n(ks[12], (N_ODD, S5_GROUPS, S5_GROUP, S5_STATE), cs)
    s5_c_im = n(ks[13], (N_ODD, S5_GROUPS, S5_GROUP, S5_STATE), cs)
    s5_d = n(ks[14], (N_ODD, D_MODEL), 1.0)
    w_glu = n(ks[15], (N_ODD, D_MODEL, 2 * D_MODEL), D_MODEL ** -0.5)
    w_ffn_in = n(ks[16], (DEPTH_2, D_MODEL, 2 * D_FF_2), D_MODEL ** -0.5)
    w_ffn_out = n(ks[17], (DEPTH_2, D_FF_2, D_MODEL), D_FF_2 ** -0.5)
    return {"x": x, "norm_gains": norm_gains, "w_in": w_in, "w_gate_up": w_gate_up,
            "b_gate": b_gate, "gla_norm_gain": gla_norm_gain, "w_out": w_out,
            "s5_lambda_re": s5_lambda_re, "s5_lambda_im": s5_lambda_im,
            "s5_log_step": s5_log_step, "s5_b_re": s5_b_re, "s5_b_im": s5_b_im,
            "s5_c_re": s5_c_re, "s5_c_im": s5_c_im, "s5_d": s5_d, "w_glu": w_glu,
            "w_ffn_in": w_ffn_in, "w_ffn_out": w_ffn_out}

def second_block(x, norm_gains, w_in, w_gate_up, b_gate, gla_norm_gain, w_out,
              s5_lambda_re, s5_lambda_im, s5_log_step, s5_b_re, s5_b_im,
              s5_c_re, s5_c_im, s5_d, w_glu, w_ffn_in, w_ffn_out):
    h = x.astype(jnp.float32)
    for layer in range(DEPTH_2):
        g = norm_gains[layer]
        i = layer // 2
        y = rms_norm_2(h, g[0])
        if layer % 2 == 0:
            y = sb_gla_mixer(y, w_in[i], w_gate_up[i], b_gate[i], gla_norm_gain[i], w_out[i])
        else:
            y = s5_mixer(y, s5_lambda_re[i], s5_lambda_im[i], s5_log_step[i],
                         s5_b_re[i], s5_b_im[i], s5_c_re[i], s5_c_im[i], s5_d[i], w_glu[i])
        h = h + rms_norm_2(y, g[1])
        y = swiglu_ffn(rms_norm_2(h, g[2]), w_ffn_in[layer], w_ffn_out[layer])
        h = h + rms_norm_2(y, g[3])
    return h.astype(x.dtype)


def setup_inputs(seed=0):
    out = dict(first_inputs(seed))
    for name, value in second_inputs(seed + 1).items():
        if name != "x":
            out[name + "_2"] = value
    return out


def reference(
    x, p, norm_mix_pre, norm_mix_post, norm_mlp_pre, norm_mlp_post, w_in, conv_w, conv_b,
    lru_wa, lru_ba, lru_wx, lru_bx, lru_lambda, cmp_pe_k, cmp_w1_k, cmp_w2_k, cmp_pe_v,
    cmp_w1_v, cmp_w2_v, rel_bias, gnorm_lru, gnorm_nsa, w_out, mlp_w1, mlp_w2, ple_gate,
    ple_proj, norm_gains_2, w_in_2, w_gate_up_2, b_gate_2, gla_norm_gain_2, w_out_2,
    s5_lambda_re_2, s5_lambda_im_2, s5_log_step_2, s5_b_re_2, s5_b_im_2, s5_c_re_2, s5_c_im_2,
    s5_d_2, w_glu_2, w_ffn_in_2, w_ffn_out_2,
):
    x = first_block(
        x, p, norm_mix_pre, norm_mix_post, norm_mlp_pre, norm_mlp_post, w_in, conv_w, conv_b,
        lru_wa, lru_ba, lru_wx, lru_bx, lru_lambda, cmp_pe_k, cmp_w1_k, cmp_w2_k, cmp_pe_v,
        cmp_w1_v, cmp_w2_v, rel_bias, gnorm_lru, gnorm_nsa, w_out, mlp_w1, mlp_w2, ple_gate,
        ple_proj,
    )
    return second_block(
        x, norm_gains_2, w_in_2, w_gate_up_2, b_gate_2, gla_norm_gain_2, w_out_2,
        s5_lambda_re_2, s5_lambda_im_2, s5_log_step_2, s5_b_re_2, s5_b_im_2, s5_c_re_2,
        s5_c_im_2, s5_d_2, w_glu_2, w_ffn_in_2, w_ffn_out_2,
    )


_drawn_inputs = setup_inputs


def setup_inputs(seed=0):
    import zlib

    import numpy as np

    out = dict(_drawn_inputs(seed))
    spreads = {}
    factors = {'lru_ba': 8.0,
     'lru_bx': 8.0,
     'cmp_pe_k': 4.219,
     'b_gate_2': 2.683,
     'gla_norm_gain_2': 8.0,
     's5_lambda_re_2': 8.0,
     's5_b_re_2': 2.994,
     's5_b_im_2': 3.067,
     's5_c_re_2': 2.982,
     's5_c_im_2': 3.005}
    for name, (base, spread) in spreads.items():
        noise = np.random.default_rng([zlib.crc32(name.encode()), seed]).standard_normal(out[name].shape)
        drawn = base * np.exp(spread * noise) if base else spread * noise
        out[name] = __import__('jax').numpy.asarray(drawn.astype(out[name].dtype))
    for name, factor in factors.items():
        out[name] = (out[name] * factor).astype(out[name].dtype)
    return out
```

```python
import numpy as np
import math
from contextlib import ExitStack
import concourse.bass as bass
from concourse import mybir

F32 = mybir.dt.float32
FR = mybir.dt.float32r
ALU = mybir.AluOpType
ACT = mybir.ActivationFunctionType
AX = mybir.AxisListType

P = 128
T = 256
D = 2048
DT = D // P
HALF = 8
EPS = 1e-6
KB = 1024

LT = 8
NH, NG, HD = 16, 4, 64
NCMP = 15
NEG = -1e30
FF1_GROUPS = 4

FF2_GROUPS = (16, 16, 12)
SBH = 8
LEVELS = 8

def phases(plan):
    out = []
    if "mix1" in plan:
        out += [("in1", 19), ("cmp", 2), ("out1", 8)]
    if "mlp" in plan:
        for g in range(FF1_GROUPS):
            out += [(f"up1_{g}", 8), (f"down1_{g}", 8)]
    if "ple" in plan:
        out += [("proj", 1), ("gate", 8)]
    if "mix2" in plan:
        out += [("in2", 25), ("out2", 8)]
    for s, l in (("ffn0", 0), ("ffn1", 1)):
        if s == "ffn1" and "s5" in plan:
            out += [("glu", 16)]
        if s in plan:
            for g, n in enumerate(FF2_GROUPS):
                out += [(f"up2_{l}_{g}", n), (f"down2_{l}_{g}", 8)]
    at, table = 0, {}
    for name, n in out:
        table[name] = (at, at + n)
        at += n
    return table, at


COLUMNS = [("norm_mix_pre", 16), ("norm_mix_post", 16), ("norm_mlp_pre", 16), ("norm_mlp_post", 16),
           ("gnorm", 16), ("norms2", 128), ("conv_w", 32), ("conv_b", 8), ("lru_ba", 8), ("lru_bx", 8),
           ("lru_lambda", 8), ("pe_k", 16), ("pe_v", 16), ("w2_k", 256), ("w2_v", 128),
           ("b_gate", 4), ("gla_gain", 8), ("d_skip", 16), ("any_cmp", 1),
           ("lam_re", 64), ("lam_im", 64), ("log_step", 64)]
COL, NCOL = {}, 0
for _name, _n in COLUMNS:
    COL[_name] = (NCOL, NCOL + _n)
    NCOL += _n


def build(nc, plan, x_t, stream, columns, p_t, lru_w, onehot, rel_bias, toeplitz, sb_mask, gla_masks,
          gate_up, s5_b, s5_c, out):
    PH, NPAIRS = phases(plan)
    sems = {}
    ctx = ExitStack()

    def sem(name):
        if name not in sems:
            sems[name] = ctx.enter_context(nc.semaphore(name))
        return sems[name]

    BASE = 16640

    def at(name, kib, shape, dtype=F32):
        return nc.alloc_sbuf_tensor_at(name, shape, dtype, offset=BASE + int(kib * KB))

    res = at("res", 0, [P, DT, T])
    act = at("act", 16, [P, DT, 2 * T], FR)
    w_raw = at("w_raw", 48, [P, 4, HALF * P])
    w_hi = at("w_hi", 64, [P, 4, HALF * P], FR)
    w_lo = at("w_lo", 80, [P, 4, HALF * P], FR)
    low = at("low", 96, [P, 2, T])
    ev = at("ev", 98, [P, 2, T])
    fv = at("fv", 100, [P, 2, T])
    sg = at("sg", 102, [P, 2, T])
    rms = at("rms", 104, [P, T])
    ssum = at("ssum", 105, [P, T])
    rstd = at("rstd", 106, [P, T])
    cols = at("cols", 107, [P, NCOL])
    eps_col = at("eps_col", 110.5625, [P, 1])
    lru_c = at("lru_c", 110.59375, [P, LT])
    ident = at("ident", 110.75, [P, P])
    ones = at("ones", 111.25, [P, P])
    neg_ones = at("neg_ones", 111.75, [P, P])
    neg_upper = at("neg_upper", 112.25, [P, P])
    A = 112.75
    z = at("z", A, [P, 50, T])
    lru_x = at("lru_x", A + 38, [P, LT, T])
    lru_r = at("lru_r", A + 46, [P, LT, T])
    lru_i = at("lru_i", A + 54, [P, LT, T])
    lru_a = at("lru_a", A + 62, [P, LT, T])
    lru_wt = at("lru_wt", A + 70, [P, 2, LT, HD])
    bias_cmp = at("bias_cmp", A + 74, [P, 2, NH, NCMP])
    fwd_hot = at("fwd_hot", A + 70, [33, 511])
    rev_hot = at("rev_hot", A + 72, [33, 384])
    rel = at("rel", A + 73.5, [33, NH])
    rel_rows = at("rel_rows", A + 76, [NH, 384])
    blk = at("blk", A + 38, [P, 2, 16, NG * NCMP])
    blk_s = at("blk_s", A + 46, [P, 2, 16, 2 * NG * NCMP], FR)
    hid = at("hid", A + 62, [P, 2, 2, NG * NCMP])
    k_cmp = at("k_cmp", A + 63, [P, NG * NCMP])
    v_cmp = at("v_cmp", A + 64, [NCMP, NG * HD])
    v_tok = at("v_tok", A + 65, [P, 2, 2, T])
    g_tok = at("g_tok", A + 69, [P, 2, 48])
    p_cmp = at("p_cmp", A + 38, [P, 2 * NH, NCMP])
    s_att = at("s_att", A + 40, [P, 2, 384])
    pt_att = at("pt_att", A + 43, [P, 2, 384])
    pt_cmp = at("pt_cmp", A + 46, [NCMP, 2, 2, T])
    stat = at("stat", A + 50, [P, 256])
    bias = at("bias", 16, [P, NH, 384])
    ffn = at("ffn", A, [P, DT, 2 * T], FR)
    y = at("y", A + 38, [P, DT, T])
    sq = at("sq", A + 54, [P, DT, T])
    p_in = at("p_in", A + 70, [P, 2, T])
    p_s = at("p_s", A + 72, [P, 2, 2 * T], FR)
    mask_sb = at("mask_sb", A + 50, [P, 384])
    w_gu = at("w_gu", A + 52, [16, 512])
    sb_v = at("sb_v", A + 54, [P, 2, 1024])
    zs = at("zs", A + 62, [P, 2, 384])
    se = at("se", A + 65, [P, 2, 384])
    sp = at("sp", A + 68, [P, 2, 384])
    sw = at("sw", A + 71, [P, 2, 384])
    gl = at("gl", A + 8, [P, 4, T])
    cum = at("cum", A + 12, [P, 4, T])
    dif = at("dif", A + 16, [P, 4 * T])
    dec = at("dec", A + 20, [P, 4 * T])
    v_first = at("v_first", A + 16, [P, 2, 4, P])
    k_lv = at("k_lv", A + 54, [P, LEVELS, 4, P])
    q_lv = at("q_lv", A + 70, [P, LEVELS, 4, P])
    pm = at("pm", A + 86, [P, 2, 4, P])
    v_lv = at("v_lv", A + 90, [P, 2, 4, P])
    masks = at("masks", 16, [P, 10, P])
    one_row = at("one_row", 24, [P, T])
    o_rms = at("o_rms", A + 54, [P, 8, T])
    o_rstd = at("o_rstd", A + 62, [P, 8, T])
    b_lhs = at("b_lhs", A, [P, 2, DT, P])
    c_lhs = at("c_lhs", A + 16, [P, 2, 64, 32])
    u5 = at("u5", A + 32, [P, DT, T])
    st0 = at("st0", A + 48, [P, 64, 2, 64])
    st1 = at("st1", 16, [P, 64, 2, 64])
    b_dia = at("b_dia", A + 48, [P, 2, 64, 32])
    c_raw = at("c_raw", A + 64, [P, 2, 64, 16])
    s5w = at("s5w", A + 64, [P, 4, 64, 16])
    b_raw = at("b_raw", A + 80, [P, 2, 64, 16])
    lam = at("lam", A + 88, [P, 2, 2, 2, 32])
    s5t = at("s5t", A + 89, [P, 19, 64])
    prod = at("prod", A + 93.75, [P, 2, 2, 2, 32])

    def col(name, n=None):
        a, b = COL[name]
        return cols[:, a:b] if n is None else cols[:, a + n:a + n + 1]

    bank = [ctx.enter_context(nc.psum_tensor(f"bank{w}", [P, 512], F32)) for w in range(2)]
    m = [ctx.enter_context(nc.psum_tensor(f"m{n}", [P, 512], F32)) for n in range(6)]

    order = []
    if "mix1" in plan:
        order += ["in1", "lru", "nsa", "post1"]
    if "mlp" in plan:
        order += ["mlp", "post_mlp"]
    if "mix2" in plan:
        order += ["in2", "post2"]
    if "ffn0" in plan:
        order += ["ffn0", "post_ffn0"]
    if "s5" in plan:
        order += ["s5", "post_s5"]
    if "ffn1" in plan:
        order += ["ffn1", "post_ffn1"]
    NORM = {n: k for k, n in enumerate(order)}
    acts = [n for n in ["in1", "out1", "mlp", "gate", "in2", "out2", "ffn0", "glu", "ffn1"]
            if n in ("mlp", "ffn0", "ffn1") and n in plan
            or n in ("in1", "out1") and "mix1" in plan or n == "gate" and "ple" in plan
            or n in ("in2", "out2") and "mix2" in plan or n == "glu" and "s5" in plan]
    ACTS = {n: k for k, n in enumerate(acts)}
    adds = [n for n in ["post1", "post_mlp", "gate", "post2", "post_ffn0", "post_s5", "post_ffn1"]
            if n in NORM or n == "gate" and "ple" in plan]
    ADDS = {n: DT * (k + 1) for k, n in enumerate(adds)}
    before = {"in1": 0, "mlp": ADDS.get("post1", 0), "gate": ADDS.get("post_mlp", 0),
              "in2": ADDS.get("gate", 0), "ffn0": ADDS.get("post2", 0), "s5": ADDS.get("post_ffn0", 0),
              "ffn1": ADDS.get("post_s5", 0)}
    SCALED, n_ = {}, 0
    for name_ in order:
        SCALED[name_] = n_
        n_ += 8 if name_ in ("lru", "nsa") else DT
    SQUARED, n_ = {}, 0
    for name_ in order:
        if not name_.startswith("post"):
            SQUARED[name_] = n_
            n_ += 8 if name_ in ("lru", "nsa") else DT
    YSQ = {name_: k * (2 * DT + 1) for k, name_ in enumerate([n for n in order if n.startswith("post")])}
    GROUPS, f_no, y_no, last_y = [], 0, 0, {}
    for s, sizes, tag in (("mlp", (16,) * FF1_GROUPS, "1_"), ("ffn0", FF2_GROUPS, "2_0_"),
                          ("ffn1", FF2_GROUPS, "2_1_")):
        if s in plan:
            for g, n in enumerate(sizes):
                GROUPS.append((s, g, n, f"up{tag}{g}", f"down{tag}{g}", f_no, y_no))
                f_no += n
                y_no += DT if g else 0
            last_y[s] = y_no

    half_loaded = [sem(f"half_loaded{q}") for q in range(4)]
    hi_ready, lo_ready = sem("hi_ready"), sem("lo_ready")
    halves_used, low_copied, drained = sem("halves_used"), sem("low_copied"), sem("drained")
    act_hi, act_ready = sem("act_hi"), sem("act_ready")
    squared, y_squares, sum_spread = sem("squared"), sem("y_squares"), sem("sum_spread")
    root_taken, rstd_ready, scaled = sem("root_taken"), sem("rstd_ready"), sem("scaled")
    res_added = sem("res_added")
    f_val, f_hi, f_ready, y_acc = sem("f_val"), sem("f_hi"), sem("f_ready"), sem("y_acc")
    gate_ready = sem("gate_ready")
    scan_step = [sem(f"scan_step{h}") for h in range(2)]
    consts, setup = sem("consts"), sem("setup")
    PRIME = 2
    NCONST = 16 * (5 if "mix1" in plan else 2)

    def x_piece(k):
        return sem(f"x_loaded{k // 4}"), 16

    def stream_ready(name):
        return lambda k: (res_added, before[name] - DT + k + 1) if before[name] else x_piece(k)

    def split_pair(i, step, evacuate, last=False):
        step(i, 3)
        if not last:
            step(i + 1, 0)
        evacuate(i, 0)
        if not last:
            step(i + 1, 1)
            step(i + 1, 2)
        evacuate(i, 1)

    def run_phase(eng, name, step, evacuate, unroll=False):
        a, b = PH[name]
        end = b == NPAIRS
        if unroll:
            for i in range(a, b):
                split_pair(i, step, evacuate, i == NPAIRS - 1)
            return
        if a == 0:
            split_pair(0, step, evacuate)
            a = 1
        with eng.Fori(a, b - 1 if end else b) as i:
            split_pair(i, step, evacuate)
        if end:
            split_pair(b - 1, step, evacuate, True)

    def window(t, tile, p0, l2):
        v = t[p0:p0 + 64, tile, :].rearrange("p (n l) -> p n l", l=16)
        lo_ = v[:, 0:NCMP, l2:16:2].rearrange("p n l -> p l n")
        hi_ = v[:, 1:NCMP + 1, l2:16:2].rearrange("p n l -> p l n")
        return lo_, hi_

    def tokens(ap, size, second):
        v = ap.rearrange("p (n b) -> p n b", b=size)
        return v[:, :, size // 2:size] if second else v[:, :, 0:size // 2]

    block = ctx.enter_context(nc.Block())

    @block.sync
    def _(sp_eng):
        def load(i, q):
            sp_eng.dma_start(w_raw[:, q, :], stream[4 * i + q, :, :]).then_inc(half_loaded[q], 16)
        for q in range(4):
            load(0, q)
        with sp_eng.Fori(1, NPAIRS) as i:
            for q in range(4):
                sp_eng.wait_ge(lo_ready, 4 * i + (q - 3))
                load(i, q)
        for k in range(0, DT, 4):
            sp_eng.wait_ge(res_added, ADDS[adds[-1]] - DT + k + 4)
            sp_eng.dma_start(out.rearrange("(k p) t -> p k t", p=P)[:, k:k + 4, :], res[:, k:k + 4, :]).then_inc(sem("stored"), 16)
        sp_eng.wait_ge(sem("stored"), 64)

    @block.scalar
    def _(s):
        a = nc.scalar.activation
        for k in range(0, DT, 4):
            s.dma_start(res[:, k:k + 4, :], x_t.rearrange("(k p) t -> p k t", p=P)[:, k:k + 4, :]).then_inc(x_piece(k)[0], 16)
        s.dma_start(cols[:, :], columns).then_inc(consts, 16)
        s.dma_start(neg_upper[:, :], sb_mask[:, 384:512]).then_inc(consts, 16)
        if "mix1" in plan:
            s.dma_start(fwd_hot[:, :], onehot[:, 0:511]).then_inc(consts, 16)
            s.dma_start(rev_hot[:, :], onehot[:, 511:895]).then_inc(consts, 16)
            s.dma_start(rel[0:32, :], rel_bias).then_inc(consts, 16)

        def hi(i, q):
            s.wait_ge(half_loaded[q], 16 * (i + 1))
            if not (isinstance(i, int) and i == 0):
                s.wait_ge(halves_used, 4 * i + (q - 3))
            a(w_hi[:, q, :], w_raw[:, q, :], ACT.Copy).then_inc(hi_ready, 1)

        def copy_low(i, w, n=T):
            s.wait_ge(halves_used, 4 * i + (2 * w + 2))
            a(low[:, w, 0:n], bank[w][:, n:2 * n], ACT.Copy).then_inc(low_copied, 1)

        def norm(name, src, kt, sq_t, width, ready):
            n = NORM[name]
            for k in range(kt if ready else 0):
                s.wait_ge(*ready(k))
                a(sq_t[:, k, :], src[:, k, :], ACT.Square).then_inc(squared, 1)
            s.wait_ge(sum_spread, n + 1)
            a(rms[:, :], m[5][:, 0:T], ACT.Sqrt, bias=eps_col[:, :], scale=1.0 / width).then_inc(root_taken, 1)

        def act_high(name, src, ready):
            for k in range(DT):
                s.wait_ge(*ready(k))
                a(act[:, k, 0:T], src[:, k, :], ACT.Copy).then_inc(act_hi, 1)

        def scaled_ready(name, first=0):
            return lambda k: (scaled, SCALED[name] + k + 1)

        for q in range(3):
            hi(0, q)

        s.wait_ge(setup, 5)
        s.wait_ge(consts, NCONST)
        if "mix1" in plan:
            s.wait_ge(sem("setup_mm"), 1)
            a(rel_rows[:, :], m[0][0:NH, 0:384], ACT.Copy).then_inc(sem("setup_cp"), 1)
            a(bias_cmp[:, :, :, :].rearrange("p b h n -> p b n h"),
              m[1][:, 0:480].rearrange("p (b n h) -> p b n h", b=2, n=NCMP), ACT.Copy).then_inc(sem("setup_cp"), 1)
            s.wait_ge(sem("setup_cp"), 2)
            s.dma_start(toeplitz, rel_rows[:, :].unsqueeze(1).to_broadcast([NH, P, 384])).then_inc(sem("toep_out"), 16)
            s.wait_ge(sem("lam_neg"), 1)
            a(stat[:, 24:32], stat[:, 8:16], ACT.Exp).then_inc(sem("lam_exp"), 1)
            norm("in1", res, DT, sq, D, stream_ready("in1"))
            act_high("in1", sq, scaled_ready("in1"))
            run_phase(s, "in1", hi, copy_low)
            s.wait_ge(halves_used, 4 * PH["in1"][1])
            s.wait_ge(sem("toep_out"), 16)
            for lo_c, hi_c, off in ((128, 384, 127), (0, 128, 255)):
                src = bass.AP(toeplitz.tensor, off, [[383, P], [384 * P, NH], [1, hi_c - lo_c]])
                s.dma_start(bias[:, :, lo_c:hi_c], src).then_inc(sem("bias_loaded"), 16)
            s.dma_start(lru_wt[:, :, :, :], lru_w).then_inc(sem("lru_loaded"), 16)
            for j in range(LT):
                s.wait_ge(sem("lru_mm"), j + 1)
                a(lru_r[:, j, :], m[j % 2][:, 0:T], ACT.Sigmoid, bias=col("lru_ba", j)).then_inc(sem("lru_sig"), 1)
                a(lru_i[:, j, :], m[j % 2][:, T:2 * T], ACT.Sigmoid, bias=col("lru_bx", j)).then_inc(sem("lru_sig"), 1)
            s.wait_ge(sem("lru_vec"), 1)
            a(lru_a[:, :, :], lru_r[:, :, :], ACT.Exp).then_inc(sem("lru_act"), 1)
            s.wait_ge(sem("lru_act"), 1)
            a(lru_r[:, :, :], lru_r[:, :, :], ACT.Tanh, scale=-1.0).then_inc(sem("lru_act"), 1)
            s.wait_ge(sem("lru_vec"), 3)
            a(lru_r[:, :, :], z[:, 0:LT, :], ACT.Sqrt).then_inc(sem("lru_act"), 1)
            a(z[:, LT:2 * LT, :], z[:, LT:2 * LT, :], ACT.Gelu_apprx_tanh).then_inc(sem("lru_act"), 1)
            s.wait_ge(drained, 2 * PH["in1"][1])
            s.wait_ge(sem("lru_vec"), 13)
            for g in range(NG):
                for l2 in range(2):
                    for part, src in enumerate(window(z, 26 + g // 2, 64 * (g % 2), l2)):
                        a(blk[64 * l2:64 * l2 + 64, 1, 8 * part:8 * part + 8, g * NCMP:(g + 1) * NCMP],
                          src, ACT.Copy).then_inc(sem("blk_v"), 1)
            for kv in range(2):
                s.wait_ge(sem("blk_pe"), kv + 1)
                a(blk_s[:, kv, :, 0:60], blk[:, kv, :, :], ACT.Copy).then_inc(sem("blk_hi"), 1)

            def cmp_low(i, w):
                copy_low(i, w, 60)
                s.wait_ge(drained, 2 * i + w + 1)
                a(hid[:, i - PH["cmp"][0], w, :], ev[:, w, 0:60], ACT.Gelu_apprx_tanh).then_inc(sem("hid_ready"), 1)
            run_phase(s, "cmp", hi, cmp_low, unroll=True)
            s.wait_ge(sem("cmp_mm"), 1)
            a(k_cmp[:, :], m[0][:, 0:60], ACT.Copy).then_inc(sem("cmp_cp"), 1)
            a(v_cmp[:, :], m[1][0:NCMP, 0:256], ACT.Copy).then_inc(sem("cmp_cp"), 1)
            a(z[0:48, 36, :], z[0:48, 36, :], ACT.Sigmoid).then_inc(sem("gate_sig"), 1)
            s.wait_ge(sem("tok_mm"), 1)
            for tb in range(2):
                a(v_tok[:, tb, :, :], m[2 + tb][:, :].rearrange("p (a f) -> p a f", a=2), ACT.Copy).then_inc(sem("tok_cp"), 1)
            s.wait_ge(sem("tok_mm"), 2)
            a(g_tok[:, :, :], m[4][:, 0:96].rearrange("p (b c) -> p b c", b=2), ACT.Copy).then_inc(sem("tok_cp"), 1)
            s.wait_ge(sem("cmp_vec"), 3)
            a(p_cmp[:, :, :], p_cmp[:, :, :], ACT.Exp).then_inc(sem("cmp_exp"), 1)

            def att_exp(it):
                s.wait_ge(sem("att_max"), it + 1)
                b = it % 2
                a(s_att[:, b, 0:128], s_att[:, b, 0:128], ACT.Exp, bias=stat[:, 64 + 8 * b:65 + 8 * b],
                  accum_out=stat[:, 96 + 8 * b:97 + 8 * b])
                a(s_att[:, b, 128:384], s_att[:, b, 128:384], ACT.Exp, bias=stat[:, 65 + 8 * b:66 + 8 * b],
                  accum_out=stat[:, 97 + 8 * b:98 + 8 * b]).then_inc(sem("att_exp"), 1)

            def att_copy(it):
                b = it % 2
                if it % 4 == 0:
                    s.wait_ge(sem("pct_mm"), it // 4 + 1)
                    a(pt_cmp[:, (it // 4) % 2, :, :], m[5][0:NCMP, :].rearrange("n (h t) -> n h t", h=2),
                      ACT.Copy).then_inc(sem("pct_cp"), 1)
                s.wait_ge(sem("pt_mm"), it + 1)
                a(pt_att[:, b, :], m[2 + b][:, 0:384], ACT.Copy).then_inc(sem("pt_cp"), 1)
                if it % 4 == 3:
                    s.wait_ge(sem("pv_mm"), it + 1)
                    a(z[:, 8 + it // 4, :], m[4][:, 0:T], ACT.Copy).then_inc(sem("o_cp"), 1)
            s.wait_ge(sem("lru_vec"), 13)
            for it in range(33):
                if it < 32:
                    att_exp(it)
                if it >= 1:
                    att_copy(it - 1)
            norm("lru", z[:, 0:8, :], 8, z[:, 16:24, :], LT * P, lambda k: (sem("o_cp"), 8))
            for k in range(8):
                s.wait_ge(scaled, SCALED["lru"] + k + 1)
                a(act[:, k, 0:T], z[:, 16 + k, :], ACT.Copy).then_inc(act_hi, 1)
            norm("nsa", z[:, 8:16, :], 8, z[:, 24:32, :], LT * P, lambda k: (sem("o_cp"), 8))
            for k in range(8):
                s.wait_ge(scaled, SCALED["nsa"] + k + 1)
                a(act[:, 8 + k, 0:T], z[:, 24 + k, :], ACT.Copy).then_inc(act_hi, 1)
            run_phase(s, "out1", hi, copy_low)
            norm("post1", y, DT, sq, D, None)

        def up1_low(i, w):
            copy_low(i, w)
            s.wait_ge(f_val, 2 * (i - cur[1]) + (w + cur[2] + 1))
            a(ffn[:, 2 * (i - cur[1]) + w, 0:T], fv[:, w, :], ACT.Copy).then_inc(f_hi, 1)

        def up2_low(i, w):
            copy_low(i, w)
            if w == 0:
                s.wait_ge(drained, 2 * i + 1)
                a(sg[:, 0, :], ev[:, 0, :], ACT.Silu).then_inc(gate_ready, 1)
            else:
                s.wait_ge(f_val, (i - cur[1]) + (cur[2] + 1))
                a(ffn[:, i - cur[1], 0:T], fv[:, 0, :], ACT.Copy).then_inc(f_hi, 1)

        def feed_forward(layer, name, up_low):
            norm(name, res, DT, sq, D, stream_ready(name))
            act_high(name, sq, scaled_ready(name))
            for (s_, g, n, up, down, f0, y0) in GROUPS:
                if s_ == layer:
                    cur[:] = [n, PH[up][0], f0]
                    run_phase(s, up, hi, up_low)
                    run_phase(s, down, hi, copy_low)
            norm("post_" + name, y, DT, sq, D, None)
        cur = [0, 0, 0]
        if "mlp" in plan:
            feed_forward("mlp", "mlp", up1_low)
        if "ple" in plan:
            s.dma_start(p_in[:, :, :], p_t.rearrange("(k p) t -> p k t", p=P)).then_inc(sem("p_loaded"), 16)
            s.wait_ge(sem("p_loaded"), 16)
            a(p_s[:, :, 0:T], p_in[:, :, :], ACT.Copy).then_inc(sem("p_hi"), 1)
            act_high("gate", res, stream_ready("gate"))
            i0 = PH["proj"][0]
            hi(i0, 3)
            for mt in range(DT):
                if mt % 4 == 3:
                    s.wait_ge(halves_used, 4 * i0 + mt // 4 + 1)
                else:
                    s.wait_ge(sem("proj_mm"), mt + 1 - mt // 4)
                a(low[:, mt % 2, :], bank[mt % 2][:, T:2 * T], ACT.Copy).then_inc(low_copied if mt % 8 == 7 else sem("proj_low"), 1)
            for q in range(3):
                hi(i0 + 1, q)

            def gate_low(i, w):
                copy_low(i, w)
                s.wait_ge(drained, 2 * i + (w + 1))
                s.wait_ge(sem("ple_used"), 2 * (i - PH["gate"][0]) + (w + 1))
                a(sg[:, w, :], ev[:, w, :], ACT.Sigmoid).then_inc(gate_ready, 1)
            run_phase(s, "gate", hi, gate_low)
        if "mix2" in plan:
            s.wait_ge(res_added, before["in2"]) if before["in2"] else None
            s.dma_start(mask_sb[:, :], sb_mask[:, 0:384]).then_inc(sem("mix2_loaded"), 16)
            s.dma_start(w_gu[:, :], gate_up).then_inc(sem("mix2_loaded"), 16)
            norm("in2", res, DT, sq, D, stream_ready("in2"))
            act_high("in2", sq, scaled_ready("in2"))
            run_phase(s, "in2", hi, copy_low)
            s.wait_ge(halves_used, 4 * PH["in2"][1])
            s.dma_start(masks[:, :, :], gla_masks).then_inc(sem("masks_loaded"), 16)
            for n in range(4):
                s.wait_ge(sem("sbv_mm"), n + 1)
                a(sb_v[:, n // 2, 512 * (n % 2):512 * (n % 2) + 512], m[n][:, :], ACT.Copy).then_inc(sem("sbv_cp"), 1)
            for h in range(SBH + 1):
                if h < SBH:
                    s.wait_ge(sem("sb_z"), h + 1)
                    a(se[:, h % 2, :], se[:, h % 2, :], ACT.Exp).then_inc(sem("sb_exp"), 1)
                    s.wait_ge(sem("sb_exp"), h + 1)
                    a(se[:, h % 2, :], se[:, h % 2, :], ACT.Ln, bias=1.0).then_inc(sem("sb_ln"), 1)
                if h >= 1:
                    s.wait_ge(sem("sb_ex"), h)
                    a(sw[:, (h - 1) % 2, :], sw[:, (h - 1) % 2, :], ACT.Exp).then_inc(sem("sb_w"), 1)
                    s.wait_ge(sem("sb_o"), h)
                    a(z[:, h - 1, :], m[4 + (h - 1) % 2][:, 0:T], ACT.Copy).then_inc(sem("sb_cp"), 1)
            s.wait_ge(sem("gla_n"), 1)
            a(dec[:, :], dif[:, :], ACT.Exp).then_inc(sem("gla_e"), 1)
            s.wait_ge(sem("gla_e"), 1)
            a(dec[:, :], dec[:, :], ACT.Ln, bias=1.0).then_inc(sem("gla_e"), 1)
            for l in range(LEVELS):
                s.wait_ge(sem("lv_dif"), l + 1)
                a(dec[:, :], dif[:, :], ACT.Exp, scale=1.0 / 16.0).then_inc(sem("lv_exp"), 1)
            for it in range(3 * 8):
                n = 2 if it % 3 == 2 else 4
                s.wait_ge(sem("gv_mm"), it + 1)
                if it >= 2:
                    s.wait_ge(sem("go_step"), it - 1)
                a(v_lv[:, it % 2, 0:n, :], m[2 + it % 2][:, 0:128 * n].rearrange("p (n c) -> p n c", n=n),
                  ACT.Copy).then_inc(sem("gv_cp"), 1)
                if it % 3 == 0 and it:
                    h = it // 3 - 1
                    s.wait_ge(sem("go_step"), 3 * h + 3)
                    a(z[:, 8 + h, :], m[4 + h % 2][:, 0:T], ACT.Copy).then_inc(sem("go_cp"), 1)
            s.wait_ge(sem("go_step"), 24)
            a(z[:, 15, :], m[5][:, 0:T], ACT.Copy).then_inc(sem("go_cp"), 1)
            s.wait_ge(sem("go_cp"), 8)
            a(o_rms[:, :, :], z[:, 8:16, :], ACT.Square).then_inc(sem("gn_sq"), 1)
            s.wait_ge(sem("gn_mm"), 4)
            for n in range(4):
                a(o_rms[:, 2 * n:2 * n + 2, :], m[n][:, :].rearrange("p (k t) -> p k t", k=2), ACT.Sqrt,
                  bias=eps_col[:, :], scale=1.0 / P).then_inc(sem("gn_rt"), 1)
            a(z[:, 40:48, :], z[:, 40:48, :], ACT.Silu).then_inc(sem("gn_si"), 1)
            act_high("out2", z, lambda k: (sem("sb_cp"), 8) if k < 8 else (sem("gn_y"), k - 7))
            run_phase(s, "out2", hi, copy_low)
            norm("post2", y, DT, sq, D, None)
        if "ffn0" in plan:
            feed_forward("ffn0", "ffn0", up2_low)
        if "s5" in plan:
            if before["s5"]:
                s.wait_ge(res_added, before["s5"])
            s.dma_start(b_raw[:, :, :, :], s5_b).then_inc(sem("s5_loaded"), 16)
            s.dma_start(c_raw[:, :, :, :], s5_c).then_inc(sem("s5_loaded"), 16)
            norm("s5", res, DT, u5, D, stream_ready("s5"))
            a(s5t[:, 0, :], col("log_step"), ACT.Exp).then_inc(sem("s5_par"), 1)
            s.wait_ge(sem("s5_ang"), 1)
            a(s5t[:, 3, :], s5t[:, 1, :], ACT.Exp).then_inc(sem("s5_par"), 1)
            s.wait_ge(sem("s5_ang"), 2)
            a(s5t[:, 6:8, :], s5t[:, 4:6, :], ACT.Sin).then_inc(sem("s5_par"), 1)
            for n in range(8):
                s.wait_ge(sem("blhs_mm"), n + 1)
                a(b_lhs[:, n // 4, 4 * (n % 4):4 * (n % 4) + 4, :], m[n % 4][:, :].rearrange("p (k c) -> p k c", k=4),
                  ACT.Copy).then_inc(sem("blhs_cp"), 1)
            for tb in range(4):
                if tb >= 2:
                    s.wait_ge(sem("y5_mm"), 2 * (tb - 1))
                    for h in range(2):
                        s.wait_ge(scan_step[h], 3 * (64 * (tb - 1)))
                if tb == 0:
                    s.wait_ge(sem("blhs_mm"), 8)
                st = (st0, st1)[tb % 2]
                for n in range(16):
                    bb, i = n // 4, n % 4
                    s.wait_ge(sem("bu_mm"), 16 * tb + n + 1)
                    a(st[:, :, :, 16 * bb + i:16 * bb + 16:4], m[i][:, :].rearrange("p (k r t) -> p t r k", k=4, r=2),
                      ACT.Copy).then_inc(sem("bu_cp"), 1)
            for k in range(4):
                s.wait_ge(sem("y5_add"), 8)
                a(u5[:, 4 * k:4 * k + 4, :], u5[:, 4 * k:4 * k + 4, :], ACT.Gelu).then_inc(sem("y5_gelu"), 1)
            act_high("glu", u5, lambda k: (sem("y5_gelu"), k // 4 + 1))

            def glu_low(i, w):
                copy_low(i, w)
                if w == 0:
                    s.wait_ge(drained, 2 * i + 1)
                    a(sg[:, 0, :], ev[:, 0, :], ACT.Sigmoid).then_inc(gate_ready, 1)
            run_phase(s, "glu", hi, glu_low)
            norm("post_s5", y, DT, sq, D, None)
        if "ffn1" in plan:
            feed_forward("ffn1", "ffn1", up2_low)

    GATES, n_ = {}, 0
    for name_ in PH:
        GATES[name_] = n_
        if name_ == "gate":
            n_ += 16
        if name_ == "glu" or name_.startswith("up2"):
            n_ += PH[name_][1] - PH[name_][0]

    @block.vector
    def _(v):
        e = nc.vector
        steps = [0]

        def chain(ins):
            steps[0] += 1
            ins.then_inc(sem("dve_chain"), 1)
            v.wait_ge(sem("dve_chain"), steps[0])

        def lo(i, q):
            v.wait_ge(hi_ready, 4 * i + (q + 1))
            e.tensor_tensor(w_lo[:, q, :], w_raw[:, q, :], w_hi[:, q, :].bitcast(F32), ALU.subtract).then_inc(lo_ready, 1)

        def drain(i, w, dst, n=T):
            v.wait_ge(low_copied, 2 * i + (w + 1))
            e.tensor_tensor(dst, bank[w][:, 0:n], low[:, w, 0:n], ALU.add).then_inc(drained, 1)

        def norm(name, src, kt, gain, dst):
            n = NORM[name]
            v.wait_ge(root_taken, n + 1)
            e.reciprocal(rstd[:, :], rms[:, :]).then_inc(rstd_ready, 1)
            v.wait_ge(rstd_ready, n + 1)
            for k in range(kt):
                e.scalar_tensor_tensor(dst[:, k, :], src[:, k, :], gain(k), rstd[:, :],
                                       ALU.mult, ALU.mult).then_inc(scaled, 1)

        e.memset(rel[32:33, :], NEG).then_inc(setup, 1)
        v.wait_ge(setup, 5)
        v.wait_ge(consts, NCONST)
        for q in range(3):
            lo(0, q)

        def store(name, dst, first=0):
            def evacuate(i, w):
                drain(i, w, dst[:, 2 * (i - PH[name][0]) + w, :])
            return evacuate

        if "mix1" in plan:
            c8 = lambda n: stat[:, 8 * n:8 * n + 8]
            chain(e.tensor_scalar(c8(0), col("lru_lambda"), -1.0, None, ALU.mult))
            chain(e.tensor_tensor(c8(1), c8(0), col("lru_lambda"), ALU.min))
            e.tensor_scalar(c8(2), c8(0), 0.0, None, ALU.max).then_inc(sem("lam_neg"), 1)
            v.wait_ge(sem("lam_exp"), 1)
            chain(e.tensor_scalar(c8(4), c8(3), 2.0, None, ALU.add))
            chain(e.reciprocal(c8(5), c8(4)))
            chain(e.tensor_tensor(c8(4), c8(3), c8(5), ALU.mult))
            chain(e.tensor_tensor(c8(5), c8(4), c8(4), ALU.mult))
            chain(e.tensor_scalar(c8(6), c8(5), 1.0 / 17, 1.0 / 15, ALU.mult, ALU.add))
            for k in (13, 11, 9, 7, 5, 3, 1):
                chain(e.tensor_tensor(c8(6), c8(6), c8(5), ALU.mult))
                chain(e.tensor_scalar(c8(6), c8(6), 1.0 / k, None, ALU.add))
            chain(e.tensor_tensor(c8(6), c8(6), c8(4), ALU.mult))
            chain(e.scalar_tensor_tensor(c8(6), c8(6), 2.0, c8(2), ALU.mult, ALU.add))
            chain(e.tensor_scalar(lru_c[:, :], c8(6), -8.0, None, ALU.mult))
            norm("in1", res, DT, lambda k: col("norm_mix_pre", k), sq)
            run_phase(v, "in1", lo, store("in1", z))
            v.wait_ge(drained, 2 * PH["in1"][1])
            for j in range(LT):
                e.tensor_scalar(lru_x[:, j, :], z[:, j, :], cols[:, COL["conv_w"][0] + 24 + j:COL["conv_w"][0] + 25 + j],
                                col("conv_b", j), ALU.mult, ALU.add).then_inc(sem("lru_conv"), 1)
            for s_ in (1, 2, 3):
                for j in range(LT):
                    v.wait_ge(sem("lru_conv"), 8 * (s_ - 1) + j + 1)
                    c0 = COL["conv_w"][0] + 8 * (3 - s_) + j
                    e.scalar_tensor_tensor(lru_x[:, j, s_:T], z[:, j, 0:T - s_], cols[:, c0:c0 + 1], lru_x[:, j, s_:T],
                                           ALU.mult, ALU.add).then_inc(sem("lru_conv"), 1)
            vec = sem("lru_vec")
            v.wait_ge(sem("lru_sig"), 16)
            e.tensor_tensor(lru_r[:, :, :], lru_r[:, :, :], lru_c[:, :].unsqueeze(2).to_broadcast([P, LT, T]),
                            ALU.mult).then_inc(vec, 1)
            v.wait_ge(sem("lru_act"), 1)
            e.tensor_tensor(z[:, 0:LT, :], lru_a[:, :, :], lru_a[:, :, :], ALU.mult).then_inc(vec, 1)
            v.wait_ge(sem("lru_act"), 2)
            v.wait_ge(vec, 2)
            e.scalar_tensor_tensor(z[:, 0:LT, :], z[:, 0:LT, :], 1.0, lru_r[:, :, :], ALU.add, ALU.mult).then_inc(vec, 1)
            v.wait_ge(sem("lru_act"), 3)
            v.wait_ge(sem("lru_ix"), 1)
            e.tensor_tensor(lru_x[:, :, :], lru_x[:, :, :], lru_r[:, :, :], ALU.mult).then_inc(vec, 1)
            v.wait_ge(vec, 4)
            for j in range(LT):
                e.tensor_tensor_scan(lru_i[:, j, :], lru_a[:, j, :], lru_x[:, j, :], 0.0, ALU.mult, ALU.add).then_inc(vec, 1)
            v.wait_ge(sem("lru_act"), 4)
            v.wait_ge(vec, 12)
            e.tensor_tensor(z[:, 0:LT, :], lru_i[:, :, :], z[:, LT:2 * LT, :], ALU.mult).then_inc(vec, 1)
            v.wait_ge(vec, 13)
            for g in range(NG):
                for l2 in range(2):
                    for part, src in enumerate(window(z, 24 + g // 2, 64 * (g % 2), l2)):
                        e.tensor_copy(blk[64 * l2:64 * l2 + 64, 0, 8 * part:8 * part + 8, g * NCMP:(g + 1) * NCMP],
                                      src).then_inc(sem("blk_k"), 1)
            for kv, name in enumerate(("pe_k", "pe_v")):
                v.wait_ge(sem("blk_k" if kv == 0 else "blk_v"), 16)
                e.tensor_tensor(blk[:, kv, :, :], blk[:, kv, :, :], col(name).unsqueeze(2).to_broadcast([P, 16, 60]),
                                ALU.add).then_inc(sem("blk_pe"), 1)
            for kv in range(2):
                v.wait_ge(sem("blk_hi"), kv + 1)
                e.tensor_tensor(blk_s[:, kv, :, 60:120], blk[:, kv, :, :], blk_s[:, kv, :, 0:60].bitcast(F32),
                                ALU.subtract).then_inc(sem("blk_ready"), 1)
            run_phase(v, "cmp", lo, lambda i, w: drain(i, w, ev[:, w, 0:60], 60), unroll=True)
            v.wait_ge(sem("cmp_scores"), 1)
            pc = p_cmp[:, :, :]
            for h in range(2):
                chain(e.scalar_tensor_tensor(p_cmp[:, h:32:2, :], m[h][:, 0:240].rearrange("p (j n) -> p j n", n=NCMP), HD ** -0.5,
                                             bias_cmp[:, :, :, :].rearrange("p b h n -> p (b h) n")[:, h:32:2, :],
                                             ALU.mult, ALU.add))
            e.tensor_reduce(stat[:, 0:32], pc, AX.X, ALU.max).then_inc(sem("cmp_vec"), 1)
            v.wait_ge(sem("cmp_vec"), 1)
            e.tensor_tensor(pc, pc, stat[:, 0:32].unsqueeze(2).to_broadcast([P, 32, NCMP]), ALU.subtract).then_inc(sem("cmp_vec"), 2)
            v.wait_ge(sem("cmp_exp"), 1)
            chain(e.tensor_reduce(stat[:, 0:32], pc, AX.X, ALU.add))
            chain(e.reciprocal(stat[:, 32:64], stat[:, 0:32]))
            v.wait_ge(sem("tok_cp"), 3)
            chain(e.tensor_scalar(g_tok[:, 0, 0:16], g_tok[:, 0, 0:16], col("any_cmp"), None, ALU.mult))
            chain(e.tensor_tensor(stat[:, 0:32].rearrange("p (b h) -> p b h", b=2), stat[:, 32:64].rearrange("p (b h) -> p b h", b=2),
                                  g_tok[:, :, 0:16], ALU.mult))
            e.tensor_tensor(pc, pc, stat[:, 0:32].unsqueeze(2).to_broadcast([P, 32, NCMP]), ALU.mult).then_inc(sem("cmp_p"), 1)
            v.wait_ge(sem("bias_loaded"), 32)

            def att_scores(it):
                b, hh = it % 2, it // 2
                v.wait_ge(sem("s_mm"), it + 1)
                if it >= 2:
                    v.wait_ge(sem("pt_mm"), it - 1)
                e.scalar_tensor_tensor(s_att[:, b, :], m[b][:, 0:384], HD ** -0.5, bias[:, hh, :], ALU.mult, ALU.add).then_inc(sem("s_bias"), 1)
                v.wait_ge(sem("s_bias"), it + 1)
                chain(e.tensor_reduce(stat[:, 80 + 8 * b:81 + 8 * b], s_att[:, b, 0:128], AX.X, ALU.max))
                chain(e.tensor_reduce(stat[:, 81 + 8 * b:82 + 8 * b], s_att[:, b, 128:384], AX.X, ALU.max))
                e.tensor_scalar(stat[:, 64 + 8 * b:66 + 8 * b], stat[:, 80 + 8 * b:82 + 8 * b], -1.0, None, ALU.mult).then_inc(sem("att_max"), 1)

            def att_scale(it):
                b, hh, at_ = it % 2, it // 2, it % 2
                v.wait_ge(sem("att_exp"), it + 1)
                chain(e.reciprocal(stat[:, 112 + 8 * b:114 + 8 * b], stat[:, 96 + 8 * b:98 + 8 * b]))
                chain(e.tensor_tensor(stat[:, 128 + 8 * b:130 + 8 * b].unsqueeze(2), stat[:, 112 + 8 * b:114 + 8 * b].unsqueeze(2),
                                      g_tok[:, :, 16 * (1 + at_) + hh:16 * (1 + at_) + hh + 1], ALU.mult))
                e.tensor_scalar(s_att[:, b, 0:128], s_att[:, b, 0:128], stat[:, 128 + 8 * b:129 + 8 * b], None, ALU.mult)
                e.tensor_scalar(s_att[:, b, 128:384], s_att[:, b, 128:384], stat[:, 129 + 8 * b:130 + 8 * b], None, ALU.mult).then_inc(sem("att_p"), 1)
            for it in range(33):
                if it < 32:
                    att_scores(it)
                if it >= 1:
                    att_scale(it - 1)
            norm("lru", z[:, 0:8, :], 8, lambda k: col("gnorm", k), z[:, 16:24, :])
            norm("nsa", z[:, 8:16, :], 8, lambda k: col("gnorm", 8 + k), z[:, 24:32, :])
            run_phase(v, "out1", lo, store("out1", y))
            norm("post1", y, DT, lambda k: col("norm_mix_post", k), sq)

        def up1(i, w):
            drain(i, w, ev[:, w, :])
            v.wait_ge(drained, 2 * i + (w + 1))
            v.wait_ge(f_ready, 2 * (i - cur[1]) + (w + cur[2] + 1))
            e.scalar_tensor_tensor(fv[:, w, :], ev[:, w, :], 0.0, ev[:, w, :], ALU.max, ALU.mult).then_inc(f_val, 1)

        def up2(i, w):
            drain(i, w, ev[:, w, :])
            if w == 1:
                v.wait_ge(drained, 2 * i + 2)
                v.wait_ge(gate_ready, (i - cur[1]) + (cur[4] + 1))
                v.wait_ge(f_ready, (i - cur[1]) + (cur[2] + PRIME))
                e.tensor_tensor(fv[:, 0, :], sg[:, 0, :], ev[:, 1, :], ALU.mult).then_inc(f_val, 1)

        def down_more(i, w):
            v.wait_ge(y_acc, 2 * (i - cur[1]) + (w + cur[3] + 1))
            drain(i, w, ev[:, w, :])

        cur = [0, 0, 0, 0, 0]

        def feed_forward(layer, name, up_fn, gain, post_gain):
            norm(name, res, DT, gain, sq)
            for (s_, g, n, up, down, f0, y0) in GROUPS:
                if s_ == layer:
                    v.wait_ge(y_acc, PRIME + y0)
                    cur[:] = [n, PH[up][0], f0, y0, GATES[up]]
                    run_phase(v, up, lo, up_fn)
                    cur[1] = PH[down][0]
                    run_phase(v, down, lo, down_more if g else store(down, y))
            norm("post_" + name, y, DT, post_gain, sq)

        def gain2(layer, which):
            return lambda k: col("norms2", 64 * layer + 16 * which + k)

        if "mlp" in plan:
            feed_forward("mlp", "mlp", up1, lambda k: col("norm_mlp_pre", k), lambda k: col("norm_mlp_post", k))
        if "ple" in plan:
            v.wait_ge(sem("p_hi"), 1)
            e.tensor_tensor(p_s[:, :, T:2 * T], p_in[:, :, :], p_s[:, :, 0:T].bitcast(F32), ALU.subtract).then_inc(sem("p_ready"), 1)

            i0 = PH["proj"][0]
            lo(i0, 3)
            for mt in range(DT):
                if mt % 8 == 7:
                    v.wait_ge(low_copied, 2 * i0 + mt // 8 + 1)
                else:
                    v.wait_ge(sem("proj_low"), mt + 1 - mt // 8)
                e.tensor_tensor(y[:, mt, :], bank[mt % 2][:, 0:T], low[:, mt % 2, :],
                                ALU.add).then_inc(drained if mt % 8 == 7 else sem("proj_y"), 1)
            for q in range(3):
                lo(i0 + 1, q)

            def gate(i, w):
                drain(i, w, ev[:, w, :])
            run_phase(v, "gate", lo, gate)
        if "mix2" in plan:
            norm("in2", res, DT, gain2(0, 0), sq)
            run_phase(v, "in2", lo, store("in2", z))
            v.wait_ge(sem("mix2_loaded"), 32)
            v.wait_ge(drained, 2 * PH["in2"][1])
            for h in range(SBH + 1):
                if h < SBH:
                    v.wait_ge(sem("sb_s"), h + 1)
                    b = h % 2
                    if h >= 2:
                        v.wait_ge(sem("sb_ex"), h - 1)
                    e.scalar_tensor_tensor(zs[:, b, :], m[b][:, 0:384], 128 ** -0.5, mask_sb[:, :], ALU.mult, ALU.add).then_inc(sem("sb_zs"), 1)
                    v.wait_ge(sem("sb_zs"), h + 1)
                    e.scalar_tensor_tensor(se[:, b, :], zs[:, b, :], -1.0, zs[:, b, :], ALU.mult, ALU.min).then_inc(sem("sb_z"), 1)
                if h >= 1:
                    b = (h - 1) % 2
                    v.wait_ge(sem("sb_u"), h)
                    if h >= 3:
                        v.wait_ge(sem("sb_o"), h - 2)
                    e.tensor_tensor(sw[:, b, :], m[2 + b][:, 0:384], zs[:, b, :], ALU.add).then_inc(sem("sb_ex"), 1)
                if h < SBH:
                    b = h % 2
                    v.wait_ge(sem("sb_ln"), h + 1)
                    if h >= 2:
                        v.wait_ge(sem("sb_u"), h - 1)
                    e.scalar_tensor_tensor(sp[:, b, :], zs[:, b, :], 0.0, se[:, b, :], ALU.max, ALU.add).then_inc(sem("sb_sp"), 1)
            v.wait_ge(sem("gl_mm"), 1)
            for k in range(4):
                e.tensor_scalar(gl[:, k, :], m[k // 2][:, T * (k % 2):T * (k % 2) + T], col("b_gate", k), None, ALU.add).then_inc(sem("gla_gl"), 1)
            v.wait_ge(sem("gla_gl"), 4)
            glf = gl[:, :, :].rearrange("p k t -> p (k t)")
            e.scalar_tensor_tensor(dif[:, :], glf, -1.0, glf, ALU.mult, ALU.min).then_inc(sem("gla_n"), 1)
            v.wait_ge(sem("gla_e"), 2)
            chain(e.scalar_tensor_tensor(glf, glf, 0.0, dec[:, :], ALU.min, ALU.subtract))
            v.wait_ge(sem("one_row"), 1)
            for k in range(4):
                e.tensor_tensor_scan(cum[:, k, :], one_row[:, :], gl[:, k, :], 0.0, ALU.mult, ALU.add).then_inc(sem("gla_cum"), 1)
            v.wait_ge(sem("gla_cum"), 4)
            zq = z[:, 24:28, :].rearrange("p k t -> p (k t)")
            zk = z[:, 28:32, :].rearrange("p k t -> p (k t)")
            v.wait_ge(sem("sb_cp"), 8)
            for l in range(LEVELS):
                size = 2 << l
                half = size // 2
                cv = cum[:, :, :].rearrange("p k t -> p (k t)").rearrange("p (n b) -> p n b", b=size)
                if l:
                    v.wait_ge(sem("lv_exp"), l)
                chain(e.tensor_tensor(dif[:, :].rearrange("p (n b) -> p n b", b=size), cv,
                                      cv[:, :, half - 1:half].to_broadcast([P, 1024 // size, size]), ALU.subtract))
                e.scalar_tensor_tensor(dif[:, :], dif[:, :], -1.0, dif[:, :], ALU.mult, ALU.min).then_inc(sem("lv_dif"), 1)
                v.wait_ge(sem("lv_exp"), l + 1)
                for dst, src, second in ((k_lv, zk, False), (q_lv, zq, True)):
                    e.tensor_tensor(dst[:, l, :, :].rearrange("p k c -> p (k c)").rearrange("p (n b) -> p n b", b=half),
                                    tokens(src, size, second), tokens(dec[:, :], size, second), ALU.mult).then_inc(sem("lv_done"), 1)
            v.wait_ge(sem("masks_loaded"), 16)
            for it in range(24):
                n = 2 if it % 3 == 2 else 4
                s0 = 4 * (it % 3)
                v.wait_ge(sem("gs_mm"), it + 1)
                if it >= 2:
                    v.wait_ge(sem("go_step"), it - 1)
                e.scalar_tensor_tensor(pm[:, it % 2, 0:n, :].rearrange("p n c -> p (n c)"), m[it % 2][:, 0:128 * n], 0.125,
                                       masks[:, s0:s0 + n, :].rearrange("p n c -> p (n c)"), ALU.mult, ALU.mult).then_inc(sem("pm_done"), 1)
            for n in range(4):
                v.wait_ge(sem("gn_rt"), n + 1)
                e.reciprocal(o_rstd[:, 2 * n:2 * n + 2, :], o_rms[:, 2 * n:2 * n + 2, :]).then_inc(sem("gn_rs"), 1)
                v.wait_ge(sem("gn_rs"), n + 1)
                for k in (2 * n, 2 * n + 1):
                    e.scalar_tensor_tensor(z[:, 8 + k, :], z[:, 8 + k, :], col("gla_gain", k), o_rstd[:, k, :],
                                           ALU.mult, ALU.mult).then_inc(sem("gn_o"), 1)
            run_phase(v, "out2", lo, store("out2", y))
            norm("post2", y, DT, gain2(0, 1), sq)
        if "ffn0" in plan:
            feed_forward("ffn0", "ffn0", up2, gain2(0, 2), gain2(0, 3))
        if "s5" in plan:
            norm("s5", res, DT, gain2(1, 0), u5)
            t5 = lambda n: s5t[:, n, :]
            TT = lambda o, x, y_, op: chain(e.tensor_tensor(t5(o), x, y_, op))
            TS = lambda o, x, a_, op0, b_=None, op1=ALU.bypass: chain(e.tensor_scalar(t5(o), t5(x), a_, b_, op0, op1))
            v.wait_ge(sem("s5_par"), 1)
            e.tensor_tensor(t5(1), t5(0), col("lam_re"), ALU.mult).then_inc(sem("s5_ang"), 1)
            TT(2, t5(0), col("lam_im"), ALU.mult)
            MAGIC = 12582912.0
            TS(8, 2, 1.0 / (2 * math.pi), ALU.mult)
            TS(8, 8, MAGIC, ALU.add)
            TS(8, 8, MAGIC, ALU.subtract)
            two_pi = 2 * math.pi
            c1 = 6.28125
            c2 = float(np.float32(round((two_pi - c1) * 2 ** 21) / 2 ** 21))
            c3 = float(np.float32(two_pi - c1 - c2))
            for c in (c1, c2, c3):
                chain(e.scalar_tensor_tensor(t5(2), t5(8), -c, t5(2), ALU.mult, ALU.add))
            TS(9, 2, math.pi / 2, ALU.add)
            TS(10, 9, math.pi, ALU.is_gt, -two_pi, ALU.mult)
            TT(5, t5(9), t5(10), ALU.add)
            TS(5, 5, 3.1415925, ALU.min, -3.1415925, ALU.max)
            chain(e.tensor_scalar(t5(4), t5(2), 3.1415925, -3.1415925, ALU.min, ALU.max))
            e.tensor_copy(t5(10), t5(5)).then_inc(sem("s5_ang"), 1)
            v.wait_ge(sem("s5_par"), 3)
            TT(11, t5(3), t5(7), ALU.mult)
            TT(12, t5(3), t5(6), ALU.mult)
            for r in range(2):
                halves = lambda n: t5(n).rearrange("p (h g) -> p h g", h=2)
                chain(e.tensor_copy(lam[:, :, 0, r, :], halves(11)))
                chain(e.tensor_scalar(lam[:, :, 1, r, :], halves(12), 1.0 - 2.0 * r, None, ALU.mult))
            TT(13, col("lam_re"), col("lam_re"), ALU.mult)
            TT(14, col("lam_im"), col("lam_im"), ALU.mult)
            TT(13, t5(13), t5(14), ALU.add)
            chain(e.reciprocal(t5(14), t5(13)))
            TS(15, 11, 1.0, ALU.subtract)
            TT(16, t5(15), col("lam_re"), ALU.mult)
            TT(17, t5(12), col("lam_im"), ALU.mult)
            TT(16, t5(16), t5(17), ALU.add)
            TT(16, t5(16), t5(14), ALU.mult)
            TT(18, t5(12), col("lam_re"), ALU.mult)
            TT(17, t5(15), col("lam_im"), ALU.mult)
            TT(18, t5(18), t5(17), ALU.subtract)
            TT(18, t5(18), t5(14), ALU.mult)
            v.wait_ge(sem("s5_loaded"), 32)
            v.wait_ge(sem("s5_zero"), 2)
            for r, f in ((0, 1.0), (1, -1.0)):
                for h_ in range(2):
                    e.tensor_scalar(c_lhs[64 * h_:64 * h_ + 64, r, :, 16 * h_:16 * h_ + 16],
                                    c_raw[64 * h_:64 * h_ + 64, r, :, :], f, None, ALU.mult).then_inc(sem("c_done"), 1)
            v.wait_ge(sem("c_done"), 4)
            wide = lambda n: t5(n).unsqueeze(2).to_broadcast([P, 64, 16])
            for r in range(2):
                chain(e.tensor_tensor(s5w[:, 0, :, :], b_raw[:, r, :, :], wide(16), ALU.mult))
                chain(e.tensor_tensor(s5w[:, 1, :, :], b_raw[:, 1 - r, :, :], wide(18), ALU.mult))
                for h_ in range(2):
                    pr = slice(64 * h_, 64 * h_ + 64)
                    e.tensor_tensor(b_dia[pr, r, :, 16 * h_:16 * h_ + 16], s5w[pr, 0, :, :], s5w[pr, 1, :, :],
                                    ALU.add if r else ALU.subtract).then_inc(sem("b_done"), 1)
                v.wait_ge(sem("b_done"), 2 * r + 2)

            def y_add(tb):
                for n in range(2):
                    v.wait_ge(sem("y5_mm"), 2 * tb + n + 1)
                    v.wait_ge(sem("y5_skip"), tb + 1)
                    e.tensor_tensor(u5[:, 8 * n:8 * n + 8, 64 * tb:64 * tb + 64], u5[:, 8 * n:8 * n + 8, 64 * tb:64 * tb + 64],
                                    m[4 + n][:, :].rearrange("p (k t) -> p k t", k=8), ALU.add).then_inc(sem("y5_add"), 1)
            def scan(st, t, prev, n):
                for step in range(3):
                    for h in range(2):
                        if not (isinstance(n, int) and n + step == 0):
                            v.wait_ge(scan_step[h], n + step)
                        g = slice(32 * h, 32 * h + 32)
                        now = st[:, t, :, g]
                        if step == 0:
                            ins = e.tensor_tensor(prod[:, h, :, :, :], lam[:, h, :, :, :],
                                                  prev[:, :, g].unsqueeze(1).to_broadcast([P, 2, 2, 32]), ALU.mult)
                        elif step == 1:
                            ins = e.tensor_tensor(now, now, prod[:, h, 0, :, :], ALU.add)
                        else:
                            ins = e.tensor_tensor(now, now, prod[:, h, 1, ::-1, :], ALU.add)
                        ins.then_inc(scan_step[h], 1)
            for tb in range(4):
                st, prev = ((st0, st1), (st1, st0))[tb % 2]
                v.wait_ge(sem("bu_cp"), 16 * tb + 16)
                if tb:
                    scan(st, 0, prev[:, 63, :, :], 3 * (64 * tb - 1))
                for t in range(1, 64):
                    scan(st, t, st[:, t - 1, :, :], 3 * (64 * tb + t - 1))
                if tb:
                    y_add(tb - 1)
            y_add(3)

            def glu(i, w):
                drain(i, w, ev[:, w, :])
                if w == 1:
                    v.wait_ge(drained, 2 * i + 2)
                    v.wait_ge(gate_ready, (i - PH["glu"][0]) + (GATES["glu"] + 1))
                    e.tensor_tensor(y[:, i - PH["glu"][0], :], sg[:, 0, :], ev[:, 1, :], ALU.mult).then_inc(sem("glu_y"), 1)
            run_phase(v, "glu", lo, glu)
            norm("post_s5", y, DT, gain2(1, 1), sq)
        if "ffn1" in plan:
            feed_forward("ffn1", "ffn1", up2, gain2(1, 2), gain2(1, 3))

    @block.gpsimd
    def _(g):
        e = nc.gpsimd
        e.memset(ones[:, :], 1.0).then_inc(setup, 1)
        e.memset(neg_ones[:, :], -1.0).then_inc(setup, 1)
        e.memset(eps_col[:, :], EPS).then_inc(setup, 1)
        e.memset(ident[:, :], 0.0).then_inc(sem("ident0"), 1)
        g.wait_ge(sem("ident0"), 1)
        e.affine_select(out=ident[:, :], in_=ident[:, :], compare_op=ALU.not_equal, fill=1.0, base=0,
                        pattern=[[-1, P]], channel_multiplier=1).then_inc(setup, 1)
        e.memset(fv[:, 0, 0:2], 0.0).then_inc(f_ready, PRIME)
        e.memset(fv[:, 0, 2:4], 0.0).then_inc(y_acc, PRIME)
        e.memset(fv[:, 0, 4:6], 0.0).then_inc(sem("ple_used"), PRIME)

        def act_low(name, src):
            for k in range(DT):
                g.wait_ge(act_hi, DT * ACTS[name] + k + 1)
                e.tensor_tensor(act[:, k, T:2 * T], src(k), act[:, k, 0:T].bitcast(F32), ALU.subtract).then_inc(act_ready, 1)

        def add_residual(name):
            for k in range(DT):
                g.wait_ge(scaled, SCALED[name] + k + 1)
                e.tensor_tensor(res[:, k, :], res[:, k, :], sq[:, k, :], ALU.add).then_inc(res_added, 1)

        def square_sum(name, begin, ready):
            g.wait_ge(sum_spread, NORM[name])
            e.memset(ssum[:, :], 0.0).then_inc(y_squares, 1)
            for i in range(DT // 2):
                for w in range(2):
                    begin(i, w)
                    g.wait_ge(*ready(i, w))
                    e.tensor_tensor(sq[:, 2 * i + w, :], y[:, 2 * i + w, :], y[:, 2 * i + w, :], ALU.mult).then_inc(y_squares, 1)
                    g.wait_ge(y_squares, 4 * i + (YSQ[name] + 2 * w + 2))
                    e.tensor_tensor(ssum[:, :], ssum[:, :], sq[:, 2 * i + w, :], ALU.add).then_inc(y_squares, 1)

        for k in range(0, DT, 4):
            g.wait_ge(*x_piece(k))
        if "mix1" in plan:
            act_low("in1", lambda k: sq[:, k, :])
            g.wait_ge(sem("lru_sig"), 16)
            e.tensor_tensor(lru_x[:, :, :], lru_x[:, :, :], lru_i[:, :, :], ALU.mult).then_inc(sem("lru_ix"), 1)
            act_low("out1", lambda k: z[:, 16 + k, :])
            square_sum("post1", lambda i, w: None, lambda i, w: (drained, 2 * i + (2 * PH["out1"][0] + w + 1)))
            add_residual("post1")

        def feed_forward(layer, name, paired):
            act_low(name, lambda k: sq[:, k, :])
            for (s_, gr, n, up, down, f0, y0) in GROUPS:
                if s_ != layer:
                    continue

                def f_low(tile, w):
                    g.wait_ge(f_hi, f0 + 1 + tile)
                    e.tensor_tensor(ffn[:, tile, T:2 * T], fv[:, w, :], ffn[:, tile, 0:T].bitcast(F32), ALU.subtract).then_inc(f_ready, 1)
                if paired:
                    with g.Fori(0, n) as i:
                        f_low(i, 0)
                else:
                    with g.Fori(0, n // 2) as i:
                        f_low(2 * i, 0)
                        f_low(2 * i + 1, 1)

                def accumulate(i, w):
                    g.wait_ge(drained, 2 * i + (2 * PH[down][0] + w + 1))
                    e.tensor_tensor(y[:, 2 * i + w, :], y[:, 2 * i + w, :], ev[:, w, :], ALU.add).then_inc(y_acc, 1)
                if y0 + DT == last_y[layer] and gr:
                    square_sum("post_" + name, accumulate, lambda i, w: (y_acc, 2 * i + (PRIME + y0 + w + 1)))
                elif gr:
                    with g.Fori(0, DT // 2) as i:
                        for w in range(2):
                            accumulate(i, w)
            add_residual("post_" + name)
        if "mlp" in plan:
            feed_forward("mlp", "mlp", False)
        if "ple" in plan:
            act_low("gate", lambda k: res[:, k, :])
            with g.Fori(0, DT // 2) as i:
                for w in range(2):
                    g.wait_ge(gate_ready, 2 * i + (GATES["gate"] + w + 1))
                    e.tensor_tensor(y[:, 2 * i + w, :], y[:, 2 * i + w, :], sg[:, w, :], ALU.mult).then_inc(sem("ple_used"), 1)
                    g.wait_ge(sem("ple_used"), 2 * i + (PRIME + w + 1))
                    e.tensor_tensor(res[:, 2 * i + w, :], res[:, 2 * i + w, :], y[:, 2 * i + w, :], ALU.add).then_inc(res_added, 1)
        if "mix2" in plan:
            act_low("in2", lambda k: sq[:, k, :])
            g.wait_ge(halves_used, 4 * PH["in2"][1])
            e.memset(one_row[:, :], 1.0).then_inc(sem("one_row"), 1)
            g.wait_ge(sem("lv_done"), 2 * LEVELS)
            for it in range(24):
                h, r = it // 3, it % 3
                if it >= 2:
                    g.wait_ge(sem("gv_mm"), it - 1)
                for n in range(2 if r == 0 else 0, 2 if r == 2 else 4):
                    last = e.tensor_copy(v_first[:, it % 2, n, :].rearrange("p (n b) -> p n b", b=1 << (4 * r + n - 2)),
                                         tokens(z[:, 32 + h, :], 2 << (4 * r + n - 2), False))
                last.then_inc(sem("v_first_ready"), 1)
            g.wait_ge(sem("gn_si"), 1)
            for k in range(8):
                g.wait_ge(sem("gn_o"), k + 1)
                e.tensor_tensor(z[:, 8 + k, :], z[:, 8 + k, :], z[:, 40 + k, :], ALU.mult).then_inc(sem("gn_y"), 1)
            act_low("out2", lambda k: z[:, k, :])
            square_sum("post2", lambda i, w: None, lambda i, w: (drained, 2 * i + (2 * PH["out2"][0] + w + 1)))
            add_residual("post2")
        if "ffn0" in plan:
            feed_forward("ffn0", "ffn0", True)
        if "s5" in plan:
            if before["s5"]:
                g.wait_ge(res_added, before["s5"])
            e.memset(c_lhs[:, :, :, :], 0.0).then_inc(sem("s5_zero"), 1)
            e.memset(b_dia[:, :, :, :], 0.0).then_inc(sem("s5_zero"), 1)
            for tb in range(4):
                g.wait_ge(sem("bu_mm"), 16 * tb + 16)
                e.tensor_tensor(u5[:, :, 64 * tb:64 * tb + 64], u5[:, :, 64 * tb:64 * tb + 64],
                                col("d_skip").unsqueeze(2).to_broadcast([P, DT, 64]), ALU.mult).then_inc(sem("y5_skip"), 1)
            act_low("glu", lambda k: u5[:, k, :])
            square_sum("post_s5", lambda i, w: None, lambda i, w: (sem("glu_y"), 2 * i + (w + 1)))
            add_residual("post_s5")
        if "ffn1" in plan:
            feed_forward("ffn1", "ffn1", True)

    @block.tensor
    def _(pe):
        mm = nc.tensor.matmul

        def unit(i, w, x, kt, n=T, tile_ready=None):
            if not (isinstance(i, int) and i == 0):
                pe.wait_ge(drained, 2 * i + (w - 1))
            hk = kt // 2
            for h in range(2):
                q = 2 * w + h
                pe.wait_ge(lo_ready, 4 * i + (q + 1))
                for k in range(hk):
                    wt = slice(k * P, (k + 1) * P)
                    if tile_ready:
                        pe.wait_ge(*tile_ready(h * hk + k))
                    mm(bank[w][:, 0:2 * n], w_hi[:, q, wt], x(h * hk + k, 0, 2 * n), start=(h == 0 and k == 0), stop=False)
                    last = mm(bank[w][:, n:2 * n], w_lo[:, q, wt], x(h * hk + k, 0, n), start=False,
                              stop=(h == 1 and k == hk - 1))
                last.then_inc(halves_used, 1)

        def gemm(name, x, kt, tile_ready):
            start, end = PH[name]
            unit(start, 0, x, kt, tile_ready=tile_ready)
            unit(start, 1, x, kt)
            with pe.Fori(start + 1, end) as i:
                for w in range(2):
                    unit(i, w, x, kt)

        x_act = lambda k, a_, b_: act[:, k, a_:b_]
        x_ffn = lambda k, a_, b_: ffn[:, k, a_:b_]

        def norm(name, squares=None, kt=DT):
            if squares is None:
                pe.wait_ge(y_squares, YSQ[name] + 2 * DT + 1)
                mm(m[5][:, 0:T], ones[:, :], ssum[:, :], start=True, stop=True).then_inc(sum_spread, 1)
                return
            for k in range(kt):
                pe.wait_ge(squared, SQUARED[name] + k + 1)
                last = mm(m[5][:, 0:T], ones[:, :], squares[:, k, :], start=(k == 0), stop=(k == kt - 1))
            last.then_inc(sum_spread, 1)

        def act_tile(name):
            return lambda k: (act_ready, DT * ACTS[name] + k + 1)

        pe.wait_ge(setup, 5)
        pe.wait_ge(consts, NCONST)
        if "mix1" in plan:
            mm(m[0][0:NH, 0:384], rel[:, :], rev_hot[:, :], start=True, stop=True)
            for b in range(2):
                for n in range(NCMP):
                    s0 = 224 + 128 * b - 16 * n
                    last = mm(m[1][:, (b * NCMP + n) * NH:(b * NCMP + n + 1) * NH], fwd_hot[:, s0:s0 + 128], rel[:, :], start=True, stop=True)
            last.then_inc(sem("setup_mm"), 1)
            norm("in1", sq)
            gemm("in1", x_act, 16, act_tile("in1"))
            pe.wait_ge(sem("lru_loaded"), 16)
            for j in range(LT):
                pe.wait_ge(sem("lru_conv"), 24 + j + 1)
                if j >= 2:
                    pe.wait_ge(sem("lru_sig"), 2 * (j - 1))
                for wx in range(2):
                    for h in range(2):
                        pr = slice(64 * h, 64 * h + 64)
                        last = mm(m[j % 2][pr, wx * T:(wx + 1) * T], lru_wt[pr, wx, j, :], lru_x[pr, j, :], start=True, stop=True)
                last.then_inc(sem("lru_mm"), 1)
            for kv in range(2):
                pe.wait_ge(sem("blk_ready"), kv + 1)
                for w in range(2):
                    unit(PH["cmp"][0] + kv, w, lambda k, a_, b_, kv=kv: blk_s[:, kv, k, a_:b_], 16, 60)
            pe.wait_ge(sem("hid_ready"), 4)
            w2k, w2v = COL["w2_k"][0], COL["w2_v"][0]
            for f in range(2):
                mm(m[0][:, 0:60], cols[:, w2k + 128 * f:w2k + 128 * f + 128], hid[:, 0, f, :], start=(f == 0), stop=(f == 1))
            for g_ in range(NG):
                for f in range(2):
                    last = mm(m[1][0:NCMP, 64 * g_:64 * g_ + 64], hid[:, 1, f, g_ * NCMP:(g_ + 1) * NCMP],
                              cols[:, w2v + 64 * f:w2v + 64 * f + 64], start=(f == 0), stop=(f == 1))
            last.then_inc(sem("cmp_mm"), 1)
            for tb in range(2):
                for at_, tile in enumerate((30, 34)):
                    for f in range(2):
                        last = nc.tensor.transpose(m[2 + tb][:, 256 * at_ + 128 * f:256 * at_ + 128 * f + 128],
                                                   z[:, tile + f, 128 * tb:128 * tb + 128], ident[:, :])
            last.then_inc(sem("tok_mm"), 1)
            pe.wait_ge(sem("gate_sig"), 1)
            for tb in range(2):
                last = nc.tensor.transpose(m[4][:, 48 * tb:48 * tb + 48], z[0:48, 36, 128 * tb:128 * tb + 128], ident[0:48, 0:48])
            last.then_inc(sem("tok_mm"), 1)
            pe.wait_ge(sem("cmp_cp"), 2)
            for b in range(2):
                for hh in range(NH):
                    j, h = hh // 2, hh % 2
                    g_ = 2 * (j // 4) + h
                    pr = slice(64 * h, 64 * h + 64)
                    last = mm(m[h][:, (8 * b + j) * NCMP:(8 * b + j + 1) * NCMP], z[pr, 16 + j, 128 * b:128 * b + 128],
                              k_cmp[pr, g_ * NCMP:(g_ + 1) * NCMP], start=True, stop=True)
            last.then_inc(sem("cmp_scores"), 1)
            pe.wait_ge(sem("cmp_p"), 1)

            def scores(it):
                hh, at_ = it // 2, it % 2
                j, h = hh // 2, hh % 2
                pr, kt = slice(64 * h, 64 * h + 64), (28, 32)[at_] + j // 4
                if it >= 2:
                    pe.wait_ge(sem("s_bias"), it - 1)
                mm(m[it % 2][:, 128:384], z[pr, 16 + j, 128:256], z[pr, kt, :], start=True, stop=True)
                mm(m[it % 2][:, 0:128], z[pr, 16 + j, 0:128], z[pr, kt, 0:128], start=True, stop=True).then_inc(sem("s_mm"), 1)

            def cmp_weights(j):
                if j >= 1:
                    pe.wait_ge(sem("pct_cp"), j)
                for h in range(2):
                    for b in range(2):
                        last = nc.tensor.transpose(m[5][0:NCMP, T * h + 128 * b:T * h + 128 * b + 128],
                                                   p_cmp[:, 16 * b + 2 * j + h, :], ident[:, :])
                last.then_inc(sem("pct_mm"), 1)

            def transposes(it):
                b = it % 2
                pe.wait_ge(sem("att_p"), it + 1)
                if it >= 2:
                    pe.wait_ge(sem("pt_cp"), it - 1)
                for n in range(3):
                    last = nc.tensor.transpose(m[2 + b][:, 128 * n:128 * n + 128], s_att[:, b, 128 * n:128 * n + 128], ident[:, :])
                last.then_inc(sem("pt_mm"), 1)

            def results(it):
                b, hh, at_ = it % 2, it // 2, it % 2
                j, h = hh // 2, hh % 2
                g_ = 2 * (j // 4) + h
                o = m[4][64 * h:64 * h + 64, :]
                if at_ == 0:
                    if h == 0:
                        pe.wait_ge(sem("pct_cp"), j + 1)
                        if j:
                            pe.wait_ge(sem("o_cp"), j)
                    mm(o[:, 0:T], v_cmp[:, 64 * g_:64 * g_ + 64], pt_cmp[:, j % 2, h, :], start=True, stop=False)
                pe.wait_ge(sem("pt_cp"), it + 1)
                mm(o[:, 0:T], v_tok[:, 0, at_, 64 * g_:64 * g_ + 64], pt_att[:, b, 0:T], start=False, stop=False)
                last = mm(o[:, 128:T], v_tok[:, 1, at_, 64 * g_:64 * g_ + 64], pt_att[:, b, T:384], start=False, stop=(at_ == 1))
                last.then_inc(sem("pv_mm"), 1)
            for it in range(34):
                if it < 32:
                    scores(it)
                if 1 <= it <= 32:
                    if (it - 1) % 4 == 0:
                        cmp_weights((it - 1) // 4)
                    transposes(it - 1)
                if it >= 2:
                    results(it - 2)
            norm("lru", z[:, 16:24, :], 8)
            norm("nsa", z[:, 24:32, :], 8)
            gemm("out1", x_act, 16, act_tile("out1"))
            norm("post1")

        def feed_forward(layer, name):
            norm(name, sq)
            for (s_, g_, n, up, down, f0, y0) in GROUPS:
                if s_ != layer:
                    continue
                gemm(up, x_act, 16, act_tile(name))
                gemm(down, x_ffn, n, lambda k: (f_ready, PRIME + f0 + k + 1))
            norm("post_" + name)
        if "mlp" in plan:
            feed_forward("mlp", "mlp")
        if "ple" in plan:
            pe.wait_ge(sem("p_ready"), 1)
            i0 = PH["proj"][0]
            if i0:
                pe.wait_ge(drained, 2 * i0)
            for mt in range(DT):
                q = mt // 4
                pe.wait_ge(lo_ready, 4 * i0 + q + 1)
                if mt >= 2:
                    if (mt - 2) % 8 == 7:
                        pe.wait_ge(drained, 2 * i0 + 1)
                    else:
                        pe.wait_ge(sem("proj_y"), mt - 1 - (mt >= 9))
                for k in range(2):
                    wt = slice((2 * (mt % 4) + k) * P, (2 * (mt % 4) + k + 1) * P)
                    mm(bank[mt % 2][:, :], w_hi[:, q, wt], p_s[:, k, :], start=(k == 0), stop=False)
                    last = mm(bank[mt % 2][:, T:2 * T], w_lo[:, q, wt], p_s[:, k, 0:T], start=False, stop=(k == 1))
                last.then_inc(halves_used if mt % 4 == 3 else sem("proj_mm"), 1)
            gemm("gate", x_act, 16, act_tile("gate"))
        if "mix2" in plan:
            norm("in2", sq)
            gemm("in2", x_act, 16, act_tile("in2"))
            pe.wait_ge(drained, 2 * PH["in2"][1])
            for n in range(4):
                for k in range(4):
                    last = nc.tensor.transpose(m[n][:, 128 * k:128 * k + 128],
                                               z[:, 16 + 4 * (n % 2) + k, 128 * (n // 2):128 * (n // 2) + 128], ident[:, :])
                last.then_inc(sem("sbv_mm"), 1)
            pe.wait_ge(sem("sbv_cp"), 4)
            for h in range(SBH + 1):
                if h < SBH:
                    if h >= 2:
                        pe.wait_ge(sem("sb_zs"), h - 1)
                    mm(m[h % 2][:, 0:T], z[:, 8 + h, 0:128], z[:, h, :], start=True, stop=True)
                    mm(m[h % 2][:, T:384], z[:, 8 + h, 128:T], z[:, h, 128:T], start=True, stop=True).then_inc(sem("sb_s"), 1)
                if h >= 1:
                    b = (h - 1) % 2
                    pe.wait_ge(sem("sb_sp"), h)
                    if h >= 3:
                        pe.wait_ge(sem("sb_ex"), h - 2)
                    mm(m[2 + b][:, 0:T], neg_upper[:, :], sp[:, b, 0:T], start=True, stop=False)
                    mm(m[2 + b][:, 128:T], neg_ones[:, :], sp[:, b, T:384], start=False, stop=True)
                    mm(m[2 + b][:, T:384], neg_upper[:, :], sp[:, b, T:384], start=True, stop=True).then_inc(sem("sb_u"), 1)
                    pe.wait_ge(sem("sb_w"), h)
                    if h >= 3:
                        pe.wait_ge(sem("sb_cp"), h - 2)
                    hv = slice(128 * (h - 1), 128 * h)
                    mm(m[4 + b][:, 0:T], sb_v[:, 0, hv], sw[:, b, 0:T], start=True, stop=False)
                    mm(m[4 + b][:, 128:T], sb_v[:, 1, hv], sw[:, b, T:384], start=False, stop=True).then_inc(sem("sb_o"), 1)
            pe.wait_ge(sem("sb_cp"), 8)
            for k in range(4):
                last = mm(m[k // 2][:, T * (k % 2):T * (k % 2) + T], w_gu[:, 128 * k:128 * k + 128], z[0:16, 48, :], start=True, stop=True)
            last.then_inc(sem("gl_mm"), 1)
            pe.wait_ge(sem("lv_done"), 2 * LEVELS)

            def gla_scores(it):
                h, r = it // 3, it % 3
                tl, pr = h // 2, slice(64 * (h % 2), 64 * (h % 2) + 64)
                if it >= 2:
                    pe.wait_ge(sem("pm_done"), it - 1)
                for n in range(2 if r == 2 else 4):
                    o = m[it % 2][:, 128 * n:128 * n + 128]
                    if r == 0 and n < 2:
                        tk = slice(128 * n, 128 * n + 128)
                        last = mm(o, z[pr, 28 + tl, tk], z[pr, 24 + tl, tk], start=True, stop=True)
                    else:
                        l = 4 * r + n - 2
                        last = mm(o, k_lv[pr, l, tl, :], q_lv[pr, l, tl, :], start=True, stop=True)
                last.then_inc(sem("gs_mm"), 1)
                if it >= 2:
                    pe.wait_ge(sem("gv_cp"), it - 1)
                pe.wait_ge(sem("v_first_ready"), it + 1)
                for n in range(2 if r == 2 else 4):
                    o = m[2 + it % 2][:, 128 * n:128 * n + 128]
                    if r == 0 and n < 2:
                        src = z[:, 32 + h, 128 * n:128 * n + 128]
                    else:
                        src = v_first[:, it % 2, n, :]
                    last = nc.tensor.transpose(o, src, ident[:, :])
                last.then_inc(sem("gv_mm"), 1)

            def gla_results(it):
                h, r = it // 3, it % 3
                o = m[4 + h % 2]
                pe.wait_ge(sem("pm_done"), it + 1)
                pe.wait_ge(sem("gv_cp"), it + 1)
                if r == 0 and h >= 2:
                    pe.wait_ge(sem("go_cp"), h - 1)
                for n in range(2 if r == 2 else 4):
                    if r == 0 and n < 2:
                        dst = o[:, 128 * n:128 * n + 128]
                    else:
                        dst = tokens(o[:, 0:T], 2 << (4 * r + n - 2), True)
                    last = mm(dst, v_lv[:, it % 2, n, :], pm[:, it % 2, n, :], start=(r == 0 and n == 0), stop=(r == 2 and n == 1))
                last.then_inc(sem("go_step"), 1)
            for it in range(25):
                if it < 24:
                    gla_scores(it)
                if it >= 1:
                    gla_results(it - 1)
            pe.wait_ge(sem("gn_sq"), 1)
            for n in range(4):
                mm(m[n][:, :], ones[:, :], o_rms[:, 2 * n:2 * n + 2, :].rearrange("p k t -> p (k t)"), start=True, stop=True).then_inc(sem("gn_mm"), 1)
            gemm("out2", x_act, 16, act_tile("out2"))
            norm("post2")
        if "ffn0" in plan:
            feed_forward("ffn0", "ffn0")
        if "s5" in plan:
            norm("s5", u5)
            pe.wait_ge(sem("b_done"), 4)
            for n in range(8):
                if n >= 4:
                    pe.wait_ge(sem("blhs_cp"), n - 3)
                for k in range(4):
                    kt = 4 * (n % 4) + k
                    last = nc.tensor.transpose(m[n % 4][:, 128 * k:128 * k + 128],
                                               b_dia[:, n // 4, 4 * kt:4 * kt + 4, :].rearrange("p a c -> p (a c)"), ident[:, :])
                last.then_inc(sem("blhs_mm"), 1)
            pe.wait_ge(sem("blhs_cp"), 8)
            pe.wait_ge(scaled, SCALED["s5"] + DT)

            def inputs(tb):
                for n in range(16):
                    bb, i = n // 4, n % 4
                    if tb or n >= 4:
                        pe.wait_ge(sem("bu_cp"), 16 * tb + n - 3)
                    pr = slice(32 * i, 32 * i + 32)
                    for k in range(4):
                        for r in range(2):
                            last = mm(m[i][:, 128 * k + 64 * r:128 * k + 64 * r + 64], b_lhs[pr, r, 4 * bb + k, :],
                                      u5[pr, 4 * bb + k, 64 * tb:64 * tb + 64], start=True, stop=True)
                    last.then_inc(sem("bu_mm"), 1)

            def outputs(tb):
                st = (st0, st1)[tb % 2]
                for h in range(2):
                    pe.wait_ge(scan_step[h], 3 * (64 * tb + 63))
                for n in range(2):
                    if tb:
                        pe.wait_ge(sem("y5_add"), 2 * (tb - 1) + n + 1)
                    for k in range(8):
                        for i in range(4):
                            pair = 4 * (8 * n + k) + i
                            for r in range(2):
                                last = mm(m[4 + n][32 * i:32 * i + 32, 64 * k:64 * k + 64], c_lhs[:, r, pair, :],
                                          st[:, :, r, pair], start=(r == 0), stop=(r == 1))
                    last.then_inc(sem("y5_mm"), 1)
            inputs(0)
            for tb in range(4):
                if tb < 3:
                    inputs(tb + 1)
                outputs(tb)
            gemm("glu", x_act, 16, act_tile("glu"))
            norm("post_s5")
        if "ffn1" in plan:
            feed_forward("ffn1", "ffn1")
    ctx.close()


def tiles(w):
    k, n = w.shape
    return w.reshape(k // P, P, n // P, P).transpose(2, 1, 0, 3)


def weight_stream(plan, w):
    table, pairs = phases(plan)
    out = np.zeros((pairs * 4, P, HALF, P), np.float32)

    def put(name, units):
        at = table[name][0] * 4
        for u in units:
            kt = u.shape[1] // 2
            out[at, :, 0:kt] = u[:, :kt]
            out[at + 1, :, 0:kt] = u[:, kt:]
            at += 2
        assert at <= table[name][1] * 4

    def pad(a, n):
        full = np.zeros((a.shape[0], n), np.float32)
        full[:, :a.shape[1]] = a
        return full

    if "mix1" in plan:
        put("in1", tiles(pad(w["in1"], 38 * P)))
        put("cmp", np.concatenate([tiles(w["cmp_k"]), tiles(w["cmp_v"])]))
        put("out1", tiles(w["out1"]))
    if "mlp" in plan:
        up, down = tiles(w["up1"]), tiles(w["down1"])
        for g in range(FF1_GROUPS):
            put(f"up1_{g}", up[16 * g:16 * g + 16])
            put(f"down1_{g}", down[:, :, 16 * g:16 * g + 16])
    if "ple" in plan:
        pj = tiles(w["proj"])
        put("proj", pj.reshape(2, 8, P, 2, P).transpose(0, 2, 1, 3, 4).reshape(2, P, 16, P))
        put("gate", tiles(w["gate"]))
    if "mix2" in plan:
        put("in2", tiles(pad(w["in2"], 50 * P)))
        put("out2", tiles(w["out2"]))
    for s, l in (("ffn0", 0), ("ffn1", 1)):
        if s in plan:
            up, down = tiles(w["up2"][l]), tiles(w["down2"][l])
            n_ff = up.shape[0] // 2
            up = up.reshape(2, n_ff, P, DT, P).transpose(1, 0, 2, 3, 4)
            f = 0
            for g, n in enumerate(FF2_GROUPS):
                put(f"up2_{l}_{g}", up[f:f + n].reshape(2 * n, P, DT, P))
                put(f"down2_{l}_{g}", down[:, :, f:f + n])
                f += n
    if "glu" in table:
        put("glu", tiles(w["glu"]).reshape(2, DT, P, DT, P)[::-1].transpose(1, 0, 2, 3, 4).reshape(2 * DT, P, DT, P))
    return out.reshape(pairs * 4, P, HALF * P)


def bucket(dist):
    n = np.maximum(dist, 0)
    nf = np.maximum(n, 1).astype(np.float32)
    large = 16 + (np.log(nf / 16) / math.log(8) * 16).astype(np.int32)
    return np.where(n < 16, n, np.minimum(large, 31))


def one_hot(dist):
    out = np.zeros((33, len(dist)), np.float32)
    ahead = dist < 0
    out[bucket(dist), np.arange(len(dist))] = ~ahead
    out[32] = ahead
    return out


PLAN = ("mix1", "mlp", "ple", "mix2", "ffn0", "s5", "ffn1")


def kernel(plan=PLAN, **inputs):
    import concourse.bacc as bacc
    from concourse.bass_utils import run_bass_kernel_spmd as run

    a = {k: np.asarray(v) for k, v in inputs.items()}
    heads = [4 * (2 * gp + half) + r for gp in range(2) for r in range(4) for half in range(2)]
    head_cols = np.concatenate([np.arange(64 * h, 64 * h + 64) for h in heads])
    w_in = a["w_in"][0]
    parts = np.split(w_in, np.cumsum([1024, 1024, 1024] + [256] * 6), axis=1)
    gates = parts[9].reshape(D, NH, 3)[:, heads, :].transpose(0, 2, 1).reshape(D, 48)
    w1 = np.concatenate([parts[0], parts[1], parts[2][:, head_cols], *parts[3:9], gates], axis=1)
    w_out = np.concatenate([a["w_out"][0][:1024], a["w_out"][0][1024:][head_cols]], axis=0)
    w = {"in1": w1, "cmp_k": a["cmp_w1_k"][0], "cmp_v": a["cmp_w1_v"][0], "out1": w_out,
         "up1": a["mlp_w1"][0], "down1": a["mlp_w2"][0], "proj": a["ple_proj"][0], "gate": a["ple_gate"][0],
         "in2": a["w_in_2"][0], "out2": a["w_out_2"][0], "glu": a["w_glu_2"][0],
         "up2": a["w_ffn_in_2"], "down2": a["w_ffn_out_2"]}

    cols = np.zeros((P, NCOL), np.float32)

    def put(name, v):
        cols[:, COL[name][0]:COL[name][1]] = v

    by_tile = lambda v: v.reshape(-1, P).T
    for name in ("norm_mix_pre", "norm_mix_post", "norm_mlp_pre", "norm_mlp_post"):
        put(name, by_tile(a[name][0]))
    put("gnorm", by_tile(np.concatenate([a["gnorm_lru"][0], a["gnorm_nsa"][0][head_cols]])))
    put("norms2", by_tile(a["norm_gains_2"].reshape(-1)))
    put("conv_w", by_tile(a["conv_w"][0].reshape(-1)))
    put("conv_b", by_tile(a["conv_b"][0]))
    put("lru_ba", by_tile(a["lru_ba"][0].reshape(-1)))
    put("lru_bx", by_tile(a["lru_bx"][0].reshape(-1)))
    put("lru_lambda", by_tile(a["lru_lambda"][0]))
    put("pe_k", by_tile(a["cmp_pe_k"][0].reshape(-1)))
    put("pe_v", by_tile(a["cmp_pe_v"][0].reshape(-1)))
    w2k = a["cmp_w2_k"][0].reshape(2, P, HD).transpose(1, 0, 2)
    put("w2_k", np.stack([w2k, w2k], axis=2).reshape(P, 256))
    put("w2_v", a["cmp_w2_v"][0].reshape(2, P, HD).transpose(1, 0, 2).reshape(P, 128))
    put("b_gate", by_tile(a["b_gate_2"][0]))
    put("gla_gain", by_tile(a["gla_norm_gain_2"][0]))
    put("d_skip", by_tile(a["s5_d_2"][0]))
    put("any_cmp", (np.arange(P) >= 31).astype(np.float32)[:, None])
    two = lambda v: v.reshape(64, 2, 64).transpose(1, 2, 0).reshape(P, 64)
    put("lam_re", two(a["s5_lambda_re_2"][0]))
    put("lam_im", two(a["s5_lambda_im_2"][0]))
    put("log_step", np.repeat(a["s5_log_step_2"][0].reshape(64, 2).T[:, None, :], 64, axis=1).reshape(P, 64))

    lru = np.stack([a["lru_wa"][0], a["lru_wx"][0]]).reshape(2, LT, 2, HD, HD).transpose(2, 3, 0, 1, 4).reshape(P, 2, LT, HD)
    hot = np.concatenate([one_hot(np.arange(511) - 255), one_hot(255 - np.arange(384))], axis=1)
    key, query = np.arange(P)[:, None], np.arange(P)[None, :]
    strict = np.where(key < query, 0.0, NEG).astype(np.float32)
    sb = np.concatenate([strict, np.zeros((P, P), np.float32), strict, -(key >= query).astype(np.float32)], axis=1)
    eye = np.eye(P, dtype=np.float32)
    gla = np.stack([eye, eye] + [(key // (1 << l) == query // (1 << l)).astype(np.float32) for l in range(LEVELS)], axis=1)
    s5b = np.stack([a[k][0].reshape(64, 2, 64, 16).transpose(1, 2, 0, 3).reshape(P, 64, 16) for k in ("s5_b_re_2", "s5_b_im_2")], axis=1)
    s5c = np.stack([a[k][0].reshape(64, 2, 16, 64).transpose(1, 3, 0, 2).reshape(P, 64, 16) for k in ("s5_c_re_2", "s5_c_im_2")], axis=1)

    arrays = {
        "x_t": a["x"][0].T, "stream": weight_stream(plan, w), "columns": cols, "p_t": a["p"][0, 0].T,
        "lru_w": lru, "onehot": hot, "rel_bias": a["rel_bias"][:, heads], "sb_mask": sb, "gla_masks": gla,
        "gate_up": a["w_gate_up_2"][0], "s5_b": s5b, "s5_c": s5c,
    }
    arrays = {k: np.ascontiguousarray(v) for k, v in arrays.items()}
    nc = bacc.Bacc("TRN2", target_bir_lowering=False, num_devices=1)
    args = {k: nc.dram_tensor(k, v.shape, mybir.dt.from_np(v.dtype), kind="ExternalInput").ap() for k, v in arrays.items()}
    args["toeplitz"] = nc.dram_tensor("toeplitz", (NH, P, 384), F32, kind="Internal").ap()
    out = nc.dram_tensor("out", (D, T), F32, kind="ExternalOutput").ap()
    build(nc, plan, out=out, **args)
    r = run(nc, [arrays], core_ids=[0])
    return np.ascontiguousarray(r.results[0]["out"].T)[None]
```

```python
import numpy as np
import math
from contextlib import ExitStack
import concourse.bass as bass
from concourse import mybir

F32 = mybir.dt.float32
FR = mybir.dt.float32r
ALU = mybir.AluOpType
ACT = mybir.ActivationFunctionType
AX = mybir.AxisListType

P = 128
T = 256
D = 2048
DT = D // P
HALF = 8
EPS = 1e-6
KB = 1024

LT = 8
NH, NG, HD = 16, 4, 64
NCMP = 15
NEG = -1e30
FF1_GROUPS = 4

FF2_GROUPS = (16, 16, 12)
SBH = 8
LEVELS = 8

def phases(plan):
    out = []
    if "mix1" in plan:
        out += [("in1", 19), ("cmp", 2), ("out1", 8)]
    if "mlp" in plan:
        for g in range(FF1_GROUPS):
            out += [(f"up1_{g}", 8), (f"down1_{g}", 8)]
    if "ple" in plan:
        out += [("proj", 1), ("gate", 8)]
    if "mix2" in plan:
        out += [("in2", 25), ("out2", 8)]
    for s, l in (("ffn0", 0), ("ffn1", 1)):
        if s == "ffn1" and "s5" in plan:
            out += [("glu", 16)]
        if s in plan:
            for g, n in enumerate(FF2_GROUPS):
                out += [(f"up2_{l}_{g}", n), (f"down2_{l}_{g}", 8)]
    at, table = 0, {}
    for name, n in out:
        table[name] = (at, at + n)
        at += n
    return table, at


COLUMNS = [("norm_mix_pre", 16), ("norm_mix_post", 16), ("norm_mlp_pre", 16), ("norm_mlp_post", 16),
           ("gnorm", 16), ("norms2", 128), ("conv_w", 32), ("conv_b", 8), ("lru_ba", 8), ("lru_bx", 8),
           ("lru_lambda", 8), ("pe_k", 16), ("pe_v", 16), ("w2_k", 256), ("w2_v", 128),
           ("b_gate", 4), ("gla_gain", 8), ("d_skip", 16), ("any_cmp", 1),
           ("lam_re", 64), ("lam_im", 64), ("log_step", 64)]
COL, NCOL = {}, 0
for _name, _n in COLUMNS:
    COL[_name] = (NCOL, NCOL + _n)
    NCOL += _n


def build(nc, plan, x_t, stream, columns, p_t, lru_w, onehot, rel_bias, toeplitz, sb_mask, gla_masks,
          gate_up, s5_b, s5_c, out):
    PH, NPAIRS = phases(plan)
    sems = {}
    ctx = ExitStack()

    def sem(name):
        if name not in sems:
            sems[name] = ctx.enter_context(nc.semaphore(name))
        return sems[name]

    BASE = 16640

    def at(name, kib, shape, dtype=F32):
        return nc.alloc_sbuf_tensor_at(name, shape, dtype, offset=BASE + int(kib * KB))

    res = at("res", 0, [P, DT, T])
    act = at("act", 16, [P, DT, 2 * T], FR)
    w_raw = at("w_raw", 48, [P, 4, HALF * P])
    w_hi = at("w_hi", 64, [P, 4, HALF * P], FR)
    w_lo = at("w_lo", 80, [P, 4, HALF * P], FR)
    low = at("low", 96, [P, 2, T])
    ev = at("ev", 98, [P, 2, T])
    fv = at("fv", 100, [P, 2, T])
    sg = at("sg", 102, [P, 2, T])
    rms = at("rms", 104, [P, T])
    ssum = at("ssum", 105, [P, T])
    rstd = at("rstd", 106, [P, T])
    cols = at("cols", 107, [P, NCOL])
    eps_col = at("eps_col", 110.5625, [P, 1])
    lru_c = at("lru_c", 110.59375, [P, LT])
    ident = at("ident", 110.75, [P, P])
    ones = at("ones", 111.25, [P, P])
    neg_ones = at("neg_ones", 111.75, [P, P])
    neg_upper = at("neg_upper", 112.25, [P, P])
    A = 112.75
    z = at("z", A, [P, 50, T])
    lru_x = at("lru_x", A + 38, [P, LT, T])
    lru_r = at("lru_r", A + 46, [P, LT, T])
    lru_i = at("lru_i", A + 54, [P, LT, T])
    lru_a = at("lru_a", A + 62, [P, LT, T])
    lru_wt = at("lru_wt", A + 70, [P, 2, LT, HD])
    bias_cmp = at("bias_cmp", A + 74, [P, 2, NH, NCMP])
    fwd_hot = at("fwd_hot", A + 70, [33, 511])
    rev_hot = at("rev_hot", A + 72, [33, 384])
    rel = at("rel", A + 73.5, [33, NH])
    rel_rows = at("rel_rows", A + 76, [NH, 384])
    blk = at("blk", A + 78, [P, 2, 16, NG * NCMP])
    blk_s = at("blk_s", A + 46, [P, 2, 16, 2 * NG * NCMP], FR)
    hid = at("hid", A + 62, [P, 2, 2, NG * NCMP])
    k_cmp = at("k_cmp", A + 63, [P, NG * NCMP])
    v_cmp = at("v_cmp", A + 64, [NCMP, NG * HD])
    v_tok = at("v_tok", A + 65, [P, 2, 2, T])
    g_tok = at("g_tok", A + 69, [P, 2, 48])
    p_cmp = at("p_cmp", A + 38, [P, 2 * NH, NCMP])
    s_att = at("s_att", A + 40, [P, 2, 2, 384])
    pt_att = at("pt_att", A + 51, [P, 2, 2, 384])
    lru_n = at("lru_n", A + 78, [P, LT, T])
    pt_cmp = at("pt_cmp", A + 46, [NCMP, 2, 2, T])
    stat = at("stat", A + 50, [P, 256])
    bias = at("bias", 16, [P, NH, 384])
    ffn = at("ffn", A, [P, DT, 2 * T], FR)
    y = at("y", A + 38, [P, DT, T])
    sq = at("sq", A + 54, [P, DT, T])
    p_in = at("p_in", A + 70, [P, 2, T])
    p_s = at("p_s", A + 72, [P, 2, 2 * T], FR)
    mask_sb = at("mask_sb", A + 50, [P, 384])
    w_gu = at("w_gu", A + 52, [16, 512])
    sb_v = at("sb_v", A + 54, [P, 2, 1024])
    zs = at("zs", A + 62, [P, 2, 2, 384])
    se = at("se", A + 68, [P, 2, 2, 384])
    sp = at("sp", A + 74, [P, 2, 384])
    sw = at("sw", A + 77, [P, 2, 384])
    gl = at("gl", 24, [P, 4, T])
    cum = at("cum", 28, [P, 4, T])
    dif = at("dif", A + 16, [P, 4 * T])
    dec = at("dec", A + 20, [P, 4 * T])
    dif1 = at("dif1", A + 86, [P, 4 * T])
    dec1 = at("dec1", A + 90, [P, 4 * T])
    v_first = at("v_first", A + 16, [P, 2, 4, P])
    k_lv = at("k_lv", A + 54, [P, LEVELS, 4, P])
    q_lv = at("q_lv", A + 70, [P, LEVELS, 4, P])
    pm = at("pm", A + 86, [P, 2, 4, P])
    v_lv = at("v_lv", A + 90, [P, 2, 4, P])
    masks = at("masks", 96, [P, 10, P])
    one_row = at("one_row", 101, [P, T])
    o_rms = at("o_rms", A + 20, [P, 2, T])
    o_rstd = at("o_rstd", A + 22, [P, 2, T])
    b_raw = at("b_raw", A + 24, [P, 2, 64, 16])
    b_tmp = at("b_tmp", A + 32, [P, 64, 16])
    b_dia = at("b_dia", A + 54, [P, 2, 64, 32])
    b_lhs = at("b_lhs", A + 70, [P, 2, DT, P])
    lam = at("lam", A + 88, [P, 2, 2, 2, 32])
    s5t = at("s5t", A + 89, [P, 19, 64])
    prod = at("prod", A + 93.75, [P, 2, 2, 2, 32])
    c_raw = at("c_raw", A, [P, 2, 64, 16])
    c_lhs = at("c_lhs", A + 32, [P, 2, 64, 32])
    u5 = at("u5", A + 54, [P, DT, T])
    st0 = at("st0", A, [P, 64, 2, 64])
    st1 = at("st1", 16, [P, 64, 2, 64])

    def col(name, n=None):
        a, b = COL[name]
        return cols[:, a:b] if n is None else cols[:, a + n:a + n + 1]

    bank = [ctx.enter_context(nc.psum_tensor(f"bank{w}", [P, 512], F32)) for w in range(2)]
    m = [ctx.enter_context(nc.psum_tensor(f"m{n}", [P, 512], F32)) for n in range(6)]

    order = []
    if "mix1" in plan:
        order += ["in1", "lru", "nsa", "post1"]
    if "mlp" in plan:
        order += ["mlp", "post_mlp"]
    if "mix2" in plan:
        order += ["in2", "post2"]
    if "ffn0" in plan:
        order += ["ffn0", "post_ffn0"]
    if "s5" in plan:
        order += ["s5", "post_s5"]
    if "ffn1" in plan:
        order += ["ffn1", "post_ffn1"]
    NORM = {n: k for k, n in enumerate(order)}
    acts = [n for n in ["in1", "out1", "mlp", "gate", "in2", "out2", "ffn0", "glu", "ffn1"]
            if n in ("mlp", "ffn0", "ffn1") and n in plan
            or n in ("in1", "out1") and "mix1" in plan or n == "gate" and "ple" in plan
            or n in ("in2", "out2") and "mix2" in plan or n == "glu" and "s5" in plan]
    ACTS = {n: k for k, n in enumerate(acts)}
    adds = [n for n in ["post1", "post_mlp", "gate", "post2", "post_ffn0", "post_s5", "post_ffn1"]
            if n in NORM or n == "gate" and "ple" in plan]
    ADDS = {n: DT * (k + 1) for k, n in enumerate(adds)}
    before = {"in1": 0, "mlp": ADDS.get("post1", 0), "gate": ADDS.get("post_mlp", 0),
              "in2": ADDS.get("gate", 0), "ffn0": ADDS.get("post2", 0), "s5": ADDS.get("post_ffn0", 0),
              "ffn1": ADDS.get("post_s5", 0)}
    SCALED, n_ = {}, 0
    for name_ in order:
        SCALED[name_] = n_
        n_ += 8 if name_ in ("lru", "nsa") else DT
    SQUARED, n_ = {}, 0
    for name_ in order:
        if not name_.startswith("post"):
            SQUARED[name_] = n_
            n_ += 8 if name_ in ("lru", "nsa") else DT
    YSQ = {name_: k * (2 * DT + 1) for k, name_ in enumerate([n for n in order if n.startswith("post")])}
    GROUPS, f_no, y_no, last_y = [], 0, 0, {}
    for s, sizes, tag in (("mlp", (16,) * FF1_GROUPS, "1_"), ("ffn0", FF2_GROUPS, "2_0_"),
                          ("ffn1", FF2_GROUPS, "2_1_")):
        if s in plan:
            for g, n in enumerate(sizes):
                GROUPS.append((s, g, n, f"up{tag}{g}", f"down{tag}{g}", f_no, y_no))
                f_no += n
                y_no += DT if g else 0
            last_y[s] = y_no

    half_loaded = [sem(f"half_loaded{q}") for q in range(4)]
    hi_ready, lo_ready = sem("hi_ready"), sem("lo_ready")
    halves_used, low_copied, drained = sem("halves_used"), sem("low_copied"), sem("drained")
    act_hi, act_ready = sem("act_hi"), sem("act_ready")
    squared, y_squares, sum_spread = sem("squared"), sem("y_squares"), sem("sum_spread")
    root_taken, rstd_ready, scaled = sem("root_taken"), sem("rstd_ready"), sem("scaled")
    res_added = sem("res_added")
    f_val, f_hi, f_ready, y_acc = sem("f_val"), sem("f_hi"), sem("f_ready"), sem("y_acc")
    gate_ready = sem("gate_ready")
    scan_step = [sem(f"scan_step{h}") for h in range(2)]
    consts, setup = sem("consts"), sem("setup")
    PRIME = 2
    NCONST = 16 * (5 if "mix1" in plan else 2)

    def x_piece(k):
        return sem(f"x_loaded{k // 4}"), 16

    def stream_ready(name):
        return lambda k: (res_added, before[name] - DT + k + 1) if before[name] else x_piece(k)

    def split_pair(i, step, evacuate, last=False):
        step(i, 3)
        if not last:
            step(i + 1, 0)
        evacuate(i, 0)
        if not last:
            step(i + 1, 1)
            step(i + 1, 2)
        evacuate(i, 1)

    def run_phase(eng, name, step, evacuate, unroll=False, behind=None):
        a, b = PH[name]
        end = b == NPAIRS
        if behind:
            looped = LT if a == 0 else 0
            if looped:
                split_pair(0, step, evacuate)
                with eng.Fori(1, looped) as i:
                    split_pair(i, step, evacuate)

            def with_more(i, w):
                evacuate(i, w)
                behind(2 * (i - a) + w)
            for i in range(a + looped, b):
                split_pair(i, step, with_more)
            return
        if unroll:
            for i in range(a, b):
                split_pair(i, step, evacuate, i == NPAIRS - 1)
            return
        if a == 0:
            split_pair(0, step, evacuate)
            a = 1
        with eng.Fori(a, b - 1 if end else b) as i:
            split_pair(i, step, evacuate)
        if end:
            split_pair(b - 1, step, evacuate, True)

    def window(t, tile, p0, l2):
        v = t[p0:p0 + 64, tile, :].rearrange("p (n l) -> p n l", l=16)
        lo_ = v[:, 0:NCMP, l2:16:2].rearrange("p n l -> p l n")
        hi_ = v[:, 1:NCMP + 1, l2:16:2].rearrange("p n l -> p l n")
        return lo_, hi_

    def tokens(ap, size, second):
        v = ap.rearrange("p (n b) -> p n b", b=size)
        return v[:, :, size // 2:size] if second else v[:, :, 0:size // 2]

    block = ctx.enter_context(nc.Block())

    @block.sync
    def _(sp_eng):
        def load(i, q):
            sp_eng.dma_start(w_raw[:, q, :], stream[4 * i + q, :, :]).then_inc(half_loaded[q], 16)
        for q in range(4):
            load(0, q)
        with sp_eng.Fori(1, NPAIRS) as i:
            for q in range(4):
                sp_eng.wait_ge(lo_ready, 4 * i + (q - 3))
                load(i, q)
        for k in range(0, DT, 4):
            sp_eng.wait_ge(res_added, ADDS[adds[-1]] - DT + k + 4)
            sp_eng.dma_start(out.rearrange("(k p) t -> p k t", p=P)[:, k:k + 4, :], res[:, k:k + 4, :]).then_inc(sem("stored"), 16)
        sp_eng.wait_ge(sem("stored"), 64)

    @block.scalar
    def _(s):
        a = nc.scalar.activation
        for k in range(0, DT, 4):
            s.dma_start(res[:, k:k + 4, :], x_t.rearrange("(k p) t -> p k t", p=P)[:, k:k + 4, :]).then_inc(x_piece(k)[0], 16)
        s.dma_start(cols[:, :], columns).then_inc(consts, 16)
        s.dma_start(neg_upper[:, :], sb_mask[:, 384:512]).then_inc(consts, 16)
        if "mix1" in plan:
            s.dma_start(fwd_hot[:, :], onehot[:, 0:511]).then_inc(consts, 16)
            s.dma_start(rev_hot[:, :], onehot[:, 511:895]).then_inc(consts, 16)
            s.dma_start(rel[0:32, :], rel_bias).then_inc(consts, 16)

        def hi(i, q):
            s.wait_ge(half_loaded[q], 16 * (i + 1))
            if not (isinstance(i, int) and i == 0):
                s.wait_ge(halves_used, 4 * i + (q - 3))
            a(w_hi[:, q, :], w_raw[:, q, :], ACT.Copy).then_inc(hi_ready, 1)

        def copy_low(i, w, n=T):
            s.wait_ge(halves_used, 4 * i + (2 * w + 2))
            a(low[:, w, 0:n], bank[w][:, n:2 * n], ACT.Copy).then_inc(low_copied, 1)

        def norm(name, src, kt, sq_t, width, ready):
            n = NORM[name]
            for k in range(kt if ready else 0):
                s.wait_ge(*ready(k))
                a(sq_t[:, k, :], src[:, k, :], ACT.Square).then_inc(squared, 1)
            s.wait_ge(sum_spread, n + 1)
            a(rms[:, :], m[5][:, 0:T], ACT.Sqrt, bias=eps_col[:, :], scale=1.0 / width).then_inc(root_taken, 1)

        def act_high(name, src, ready):
            for k in range(DT):
                s.wait_ge(*ready(k))
                a(act[:, k, 0:T], src[:, k, :], ACT.Copy).then_inc(act_hi, 1)

        def scaled_ready(name, first=0):
            return lambda k: (scaled, SCALED[name] + k + 1)

        for q in range(3):
            hi(0, q)

        s.wait_ge(setup, 5)
        s.wait_ge(consts, NCONST)
        if "mix1" in plan:
            s.wait_ge(sem("setup_mm"), 1)
            a(rel_rows[:, :], m[0][0:NH, 0:384], ACT.Copy).then_inc(sem("setup_cp"), 1)
            a(bias_cmp[:, :, :, :].rearrange("p b h n -> p b n h"),
              m[1][:, 0:480].rearrange("p (b n h) -> p b n h", b=2, n=NCMP), ACT.Copy).then_inc(sem("setup_cp"), 1)
            s.wait_ge(sem("setup_cp"), 2)
            s.dma_start(toeplitz, rel_rows[:, :].unsqueeze(1).to_broadcast([NH, P, 384])).then_inc(sem("toep_out"), 16)
            s.dma_start(lru_wt[:, :, :, :], lru_w).then_inc(sem("lru_loaded"), 16)
            s.wait_ge(sem("lam_neg"), 1)
            a(stat[:, 24:32], stat[:, 8:16], ACT.Exp).then_inc(sem("lam_exp"), 1)
            norm("in1", res, DT, sq, D, stream_ready("in1"))
            act_high("in1", sq, scaled_ready("in1"))

            def value_blocks(g):
                for l2 in range(2):
                    for part, src in enumerate(window(z, 26 + g // 2, 64 * (g % 2), l2)):
                        a(blk[64 * l2:64 * l2 + 64, 1, 8 * part:8 * part + 8, g * NCMP:(g + 1) * NCMP],
                          src, ACT.Copy).then_inc(sem("blk_v"), 1)

            def lru_behind(u):
                j = u - 19
                if 0 <= j < LT:
                    s.wait_ge(sem("lru_mm"), j + 1)
                    a(lru_r[:, j, :], m[j % 2][:, 0:T], ACT.Sigmoid, bias=col("lru_ba", j)).then_inc(sem("lru_sig"), 1)
                    a(lru_i[:, j, :], m[j % 2][:, T:2 * T], ACT.Sigmoid, bias=col("lru_bx", j)).then_inc(sem("lru_sig"), 1)
                if u == 28:
                    s.wait_ge(sem("lru_vec"), 1)
                    a(lru_a[:, :, :], lru_r[:, :, :], ACT.Exp).then_inc(sem("lru_act"), 1)
                if u == 29:
                    s.wait_ge(sem("lru_act"), 1)
                    a(lru_r[:, :, :], lru_r[:, :, :], ACT.Tanh, scale=-1.0).then_inc(sem("lru_act"), 1)
                if u in (30, 31):
                    s.wait_ge(drained, 28)
                    value_blocks(2 * (u - 30))
                    value_blocks(2 * (u - 30) + 1)
                if u == 32:
                    s.wait_ge(sem("lru_vec"), 3)
                    a(lru_r[:, :, :], z[:, 0:LT, :], ACT.Sqrt).then_inc(sem("lru_act"), 1)
                if u == 33:
                    a(z[:, LT:2 * LT, :], z[:, LT:2 * LT, :], ACT.Gelu_apprx_tanh).then_inc(sem("lru_act"), 1)
            run_phase(s, "in1", hi, copy_low, behind=lru_behind)
            s.wait_ge(drained, 37)
            a(z[0:48, 36, :], z[0:48, 36, :], ACT.Sigmoid).then_inc(sem("gate_sig"), 1)
            s.wait_ge(halves_used, 4 * PH["in1"][1])
            s.wait_ge(sem("toep_out"), 16)
            for lo_c, hi_c, off in ((128, 384, 127), (0, 128, 255)):
                src = bass.AP(toeplitz.tensor, off, [[383, P], [384 * P, NH], [1, hi_c - lo_c]])
                s.dma_start(bias[:, :, lo_c:hi_c], src).then_inc(sem("bias_loaded"), 16)
            s.wait_ge(sem("lru_vec"), 13)
            for kv in range(2):
                s.wait_ge(sem("blk_pe"), kv + 1)
                a(blk_s[:, kv, :, 0:60], blk[:, kv, :, :], ACT.Copy).then_inc(sem("blk_hi"), 1)

            s.wait_ge(sem("tok_mm"), 1)
            for tb in range(2):
                a(v_tok[:, tb, :, :], m[2 + tb][:, :].rearrange("p (a f) -> p a f", a=2), ACT.Copy).then_inc(sem("tok_cp"), 1)
            s.wait_ge(sem("tok_mm"), 2)
            a(g_tok[:, :, :], m[4][:, 0:96].rearrange("p (b c) -> p b c", b=2), ACT.Copy).then_inc(sem("tok_cp"), 1)

            def cmp_low(i, w):
                copy_low(i, w, 60)
                s.wait_ge(drained, 2 * i + w + 1)
                a(hid[:, i - PH["cmp"][0], w, :], ev[:, w, 0:60], ACT.Gelu_apprx_tanh).then_inc(sem("hid_ready"), 1)
            run_phase(s, "cmp", hi, cmp_low, unroll=True)
            s.wait_ge(sem("cmp_mm"), 1)
            a(k_cmp[:, :], m[0][:, 0:60], ACT.Copy).then_inc(sem("cmp_cp"), 1)
            a(v_cmp[:, :], m[1][0:NCMP, 0:256], ACT.Copy).then_inc(sem("cmp_cp"), 1)
            for k in range(8):
                a(lru_n[:, k, :], z[:, k, :], ACT.Square).then_inc(squared, 1)
            s.wait_ge(sem("cmp_vec"), 3)
            a(p_cmp[:, :, :], p_cmp[:, :, :], ACT.Exp).then_inc(sem("cmp_exp"), 1)
            norm("lru", z, 8, lru_n, LT * P, None)

            def att_exp(hh):
                s.wait_ge(sem("att_max"), hh + 1)
                b = hh % 2
                for at_ in range(2):
                    for qb, c in enumerate((slice(0, 128), slice(128, 384))):
                        n = 8 * b + 2 * qb + at_
                        last = a(s_att[:, b, at_, c], s_att[:, b, at_, c], ACT.Exp, bias=stat[:, 64 + n:65 + n],
                                 accum_out=stat[:, 96 + n:97 + n])
                last.then_inc(sem("att_exp"), 1)

            def att_copy(hh):
                if hh % 2 == 0:
                    s.wait_ge(sem("pct_mm"), hh // 2 + 1)
                    a(pt_cmp[:, (hh // 2) % 2, :, :], m[5][0:NCMP, :].rearrange("n (h t) -> n h t", h=2),
                      ACT.Copy).then_inc(sem("pct_cp"), 1)
                for at_ in range(2):
                    s.wait_ge(sem("pt_mm"), 2 * hh + at_ + 1)
                    a(pt_att[:, hh % 2, at_, :], m[2 + at_][:, 0:384], ACT.Copy).then_inc(sem("pt_cp"), 1)

            def att_result(j):
                s.wait_ge(sem("pv_mm"), 2 * j + 2)
                a(z[:, 8 + j, :], (m[4], bank[0])[j % 2][:, 0:T], ACT.Copy).then_inc(sem("o_cp"), 1)
            s.wait_ge(sem("lru_vec"), 13)
            for it in range(NH + 3):
                if it < NH:
                    att_exp(it)
                if 1 <= it <= NH:
                    att_copy(it - 1)
                if it >= 4 and it % 2 == 0:
                    att_result(it // 2 - 2)
            for k in range(8):
                s.wait_ge(scaled, SCALED["lru"] + k + 1)
                a(act[:, k, 0:T], lru_n[:, k, :], ACT.Copy).then_inc(act_hi, 1)
            norm("nsa", z[:, 8:16, :], 8, z[:, 24:32, :], LT * P, lambda k: (sem("o_cp"), 8))
            for k in range(8):
                s.wait_ge(scaled, SCALED["nsa"] + k + 1)
                a(act[:, 8 + k, 0:T], z[:, 24 + k, :], ACT.Copy).then_inc(act_hi, 1)
            run_phase(s, "out1", hi, copy_low)
            norm("post1", y, DT, sq, D, None)

        def up1_low(i, w):
            copy_low(i, w)
            s.wait_ge(f_val, 2 * (i - cur[1]) + (w + cur[2] + 1))
            a(ffn[:, 2 * (i - cur[1]) + w, 0:T], fv[:, w, :], ACT.Copy).then_inc(f_hi, 1)

        def up2_low(i, w):
            copy_low(i, w)
            if w == 0:
                s.wait_ge(drained, 2 * i + 1)
                a(sg[:, 0, :], ev[:, 0, :], ACT.Silu).then_inc(gate_ready, 1)
            else:
                s.wait_ge(f_val, (i - cur[1]) + (cur[2] + 1))
                a(ffn[:, i - cur[1], 0:T], fv[:, 0, :], ACT.Copy).then_inc(f_hi, 1)

        def feed_forward(layer, name, up_low):
            norm(name, res, DT, sq, D, stream_ready(name))
            act_high(name, sq, scaled_ready(name))
            for (s_, g, n, up, down, f0, y0) in GROUPS:
                if s_ == layer:
                    cur[:] = [n, PH[up][0], f0]
                    run_phase(s, up, hi, up_low, behind=s5_behind if s_ == "ffn0" and g == 2 and "s5" in plan else None)
                    run_phase(s, down, hi, copy_low)
            norm("post_" + name, y, DT, sq, D, None)
        cur = [0, 0, 0]

        def s5_behind(u):
            if u == 0:
                if "ffn0" in plan:
                    s.wait_ge(halves_used, 4 * PH["up2_0_2"][0])
                s.dma_start(b_raw[:, :, :, :], s5_b).then_inc(sem("s5_loaded"), 16)
                a(s5t[:, 0, :], col("log_step"), ACT.Exp).then_inc(sem("s5_par"), 1)
            if u == 1:
                s.wait_ge(sem("s5_ang"), 1)
                a(s5t[:, 3, :], s5t[:, 1, :], ACT.Exp).then_inc(sem("s5_par"), 1)
            if u == 3:
                s.wait_ge(sem("s5_ang"), 2)
                a(s5t[:, 6:8, :], s5t[:, 4:6, :], ACT.Sin).then_inc(sem("s5_par"), 1)
            n = u - 15
            if 0 <= n < 8:
                s.wait_ge(sem("blhs_mm"), n + 1)
                a(b_lhs[:, n // 4, 4 * (n % 4):4 * (n % 4) + 4, :], m[n % 4][:, :].rearrange("p (k c) -> p k c", k=4),
                  ACT.Copy).then_inc(sem("blhs_cp"), 1)
        if "mlp" in plan:
            feed_forward("mlp", "mlp", up1_low)
        if "ple" in plan:
            s.dma_start(p_in[:, :, :], p_t.rearrange("(k p) t -> p k t", p=P)).then_inc(sem("p_loaded"), 16)
            s.wait_ge(sem("p_loaded"), 16)
            a(p_s[:, :, 0:T], p_in[:, :, :], ACT.Copy).then_inc(sem("p_hi"), 1)
            act_high("gate", res, stream_ready("gate"))
            i0 = PH["proj"][0]
            hi(i0, 3)
            for mt in range(DT):
                if mt % 4 == 3:
                    s.wait_ge(halves_used, 4 * i0 + mt // 4 + 1)
                else:
                    s.wait_ge(sem("proj_mm"), mt + 1 - mt // 4)
                a(low[:, mt % 2, :], bank[mt % 2][:, T:2 * T], ACT.Copy).then_inc(low_copied if mt % 8 == 7 else sem("proj_low"), 1)
            for q in range(3):
                hi(i0 + 1, q)

            def gate_low(i, w):
                copy_low(i, w)
                s.wait_ge(drained, 2 * i + (w + 1))
                s.wait_ge(sem("ple_used"), 2 * (i - PH["gate"][0]) + (w + 1))
                a(sg[:, w, :], ev[:, w, :], ACT.Sigmoid).then_inc(gate_ready, 1)
            run_phase(s, "gate", hi, gate_low)
        if "mix2" in plan:
            s.wait_ge(res_added, before["in2"]) if before["in2"] else None
            s.dma_start(mask_sb[:, :], sb_mask[:, 0:384]).then_inc(sem("mix2_loaded"), 16)
            s.dma_start(w_gu[:, :], gate_up).then_inc(sem("mix2_loaded"), 16)
            norm("in2", res, DT, sq, D, stream_ready("in2"))
            act_high("in2", sq, scaled_ready("in2"))
            run_phase(s, "in2", hi, copy_low)
            s.wait_ge(drained, 2 * PH["in2"][1])
            s.dma_start(masks[:, :, :], gla_masks).then_inc(sem("masks_loaded"), 16)
            a(z[:, 40:48, :], z[:, 40:48, :], ACT.Silu).then_inc(sem("gn_si"), 1)
            for n in range(4):
                s.wait_ge(sem("sbv_mm"), n + 1)
                a(sb_v[:, n // 2, 512 * (n % 2):512 * (n % 2) + 512], m[n][:, :], ACT.Copy).then_inc(sem("sbv_cp"), 1)

            def sb_exp(n):
                s.wait_ge(sem("sb_z"), n + 1)
                a(se[:, n % 2, :, :], se[:, n % 2, :, :], ACT.Exp).then_inc(sem("sb_exp"), 1)

            def sb_log(n):
                s.wait_ge(sem("sb_exp"), n + 1)
                a(se[:, n % 2, :, :], se[:, n % 2, :, :], ACT.Ln, bias=1.0).then_inc(sem("sb_ln"), 1)
            sb_exp(0)
            s.wait_ge(sem("gla_n"), 1)
            a(dec[:, :], dif[:, :], ACT.Exp).then_inc(sem("gla_e"), 1)
            sb_log(0)
            s.wait_ge(sem("gla_e"), 1)
            a(dec[:, :], dec[:, :], ACT.Ln, bias=1.0).then_inc(sem("gla_e"), 1)
            for n in range(SBH // 2):
                if n + 1 < SBH // 2:
                    sb_exp(n + 1)
                s.wait_ge(sem("sb_ex"), 2 * n + 2)
                a(sw[:, :, :], sw[:, :, :], ACT.Exp).then_inc(sem("sb_w"), 1)
                if n + 1 < SBH // 2:
                    sb_log(n + 1)
                for j in range(2):
                    s.wait_ge(sem("sb_o"), 2 * n + j + 1)
                    a(z[:, 2 * n + j, :], m[4 + j][:, 0:T], ACT.Copy).then_inc(sem("sb_cp"), 1)
            for l in range(LEVELS):
                s.wait_ge(sem("lv_dif"), l + 1)
                if l >= 2:
                    s.wait_ge(sem("lv_done"), 2 * (l - 1))
                a((dec, dec1)[l % 2][:, :], (dif, dif1)[l % 2][:, :], ACT.Exp, scale=1.0 / 16.0).then_inc(sem("lv_exp"), 1)
            for k in range(8):
                a(act[:, k, 0:T], z[:, k, :], ACT.Copy).then_inc(act_hi, 1)
            s.wait_ge(sem("lv_done"), 2 * LEVELS)

            def head_result(h):
                s.wait_ge(sem("go_step"), 3 * h + 3)
                a(z[:, 8 + h, :], m[4 + h % 2][:, 0:T], ACT.Copy).then_inc(sem("go_cp"), 1)
                s.wait_ge(sem("go_cp"), h + 1)
                if h >= 2:
                    s.wait_ge(sem("gn_rs"), h - 1)
                a(o_rms[:, h % 2, :], z[:, 8 + h, :], ACT.Square).then_inc(sem("gn_sq"), 1)

            def head_root(h):
                s.wait_ge(sem("gn_mm"), h + 1)
                a(o_rms[:, h % 2, :], bank[h % 2][:, 0:T], ACT.Sqrt, bias=eps_col[:, :], scale=1.0 / P).then_inc(sem("gn_rt"), 1)
            for it in range(3 * 8):
                n = 2 if it % 3 == 2 else 4
                s.wait_ge(sem("gv_mm"), it + 1)
                if it >= 2:
                    s.wait_ge(sem("go_step"), it - 1)
                a(v_lv[:, it % 2, 0:n, :], m[2 + it % 2][:, 0:128 * n].rearrange("p (n c) -> p n c", n=n),
                  ACT.Copy).then_inc(sem("gv_cp"), 1)
                if it % 3 == 0 and it:
                    head_result(it // 3 - 1)
                if it % 3 == 1 and it >= 4:
                    head_root(it // 3 - 1)
            head_result(7)
            head_root(7)
            for k in range(8):
                s.wait_ge(sem("gn_y"), k + 1)
                a(act[:, 8 + k, 0:T], z[:, 8 + k, :], ACT.Copy).then_inc(act_hi, 1)
            run_phase(s, "out2", hi, copy_low)
            norm("post2", y, DT, sq, D, None)
        if "ffn0" in plan:
            feed_forward("ffn0", "ffn0", up2_low)
        if "s5" in plan:
            if before["s5"]:
                s.wait_ge(res_added, before["s5"])
            else:
                for u in range(24):
                    s5_behind(u)
            s.dma_start(c_raw[:, :, :, :], s5_c).then_inc(sem("c_loaded"), 16)
            norm("s5", res, DT, u5, D, stream_ready("s5"))
            for tb in range(4):
                if tb >= 2:
                    s.wait_ge(sem("y5_mm"), 2 * (tb - 1))
                    for h in range(2):
                        s.wait_ge(scan_step[h], 3 * (64 * (tb - 1)))
                if tb == 0:
                    s.wait_ge(sem("c_done"), 4)
                st = (st0, st1)[tb % 2]
                for n in range(16):
                    bb, i = n // 4, n % 4
                    s.wait_ge(sem("bu_mm"), 16 * tb + n + 1)
                    a(st[:, :, :, 16 * bb + i:16 * bb + 16:4], m[i][:, :].rearrange("p (k r t) -> p t r k", k=4, r=2),
                      ACT.Copy).then_inc(sem("bu_cp"), 1)
            for k in range(4):
                s.wait_ge(sem("y5_add"), 8)
                a(u5[:, 4 * k:4 * k + 4, :], u5[:, 4 * k:4 * k + 4, :], ACT.Gelu).then_inc(sem("y5_gelu"), 1)
            act_high("glu", u5, lambda k: (sem("y5_gelu"), k // 4 + 1))

            def glu_low(i, w):
                copy_low(i, w)
                if w == 0:
                    s.wait_ge(drained, 2 * i + 1)
                    a(sg[:, 0, :], ev[:, 0, :], ACT.Sigmoid).then_inc(gate_ready, 1)
            run_phase(s, "glu", hi, glu_low)
            norm("post_s5", y, DT, sq, D, None)
        if "ffn1" in plan:
            feed_forward("ffn1", "ffn1", up2_low)

    GATES, n_ = {}, 0
    for name_ in PH:
        GATES[name_] = n_
        if name_ == "gate":
            n_ += 16
        if name_ == "glu" or name_.startswith("up2"):
            n_ += PH[name_][1] - PH[name_][0]

    @block.vector
    def _(v):
        e = nc.vector
        steps = [0]

        def chain(ins):
            steps[0] += 1
            ins.then_inc(sem("dve_chain"), 1)
            v.wait_ge(sem("dve_chain"), steps[0])

        def lo(i, q):
            v.wait_ge(hi_ready, 4 * i + (q + 1))
            e.tensor_tensor(w_lo[:, q, :], w_raw[:, q, :], w_hi[:, q, :].bitcast(F32), ALU.subtract).then_inc(lo_ready, 1)

        def drain(i, w, dst, n=T):
            v.wait_ge(low_copied, 2 * i + (w + 1))
            e.tensor_tensor(dst, bank[w][:, 0:n], low[:, w, 0:n], ALU.add).then_inc(drained, 1)

        def norm(name, src, kt, gain, dst):
            n = NORM[name]
            v.wait_ge(root_taken, n + 1)
            e.reciprocal(rstd[:, :], rms[:, :]).then_inc(rstd_ready, 1)
            v.wait_ge(rstd_ready, n + 1)
            for k in range(kt):
                e.scalar_tensor_tensor(dst[:, k, :], src[:, k, :], gain(k), rstd[:, :],
                                       ALU.mult, ALU.mult).then_inc(scaled, 1)

        e.memset(rel[32:33, :], NEG).then_inc(setup, 1)
        v.wait_ge(setup, 5)
        v.wait_ge(consts, NCONST)
        for q in range(3):
            lo(0, q)

        def store(name, dst, first=0):
            def evacuate(i, w):
                drain(i, w, dst[:, 2 * (i - PH[name][0]) + w, :])
            return evacuate

        if "mix1" in plan:
            c8 = lambda n: stat[:, 8 * n:8 * n + 8]
            chain(e.tensor_scalar(c8(0), col("lru_lambda"), -1.0, None, ALU.mult))
            chain(e.tensor_tensor(c8(1), c8(0), col("lru_lambda"), ALU.min))
            e.tensor_scalar(c8(2), c8(0), 0.0, None, ALU.max).then_inc(sem("lam_neg"), 1)
            v.wait_ge(sem("lam_exp"), 1)
            chain(e.tensor_scalar(c8(4), c8(3), 2.0, None, ALU.add))
            chain(e.reciprocal(c8(5), c8(4)))
            chain(e.tensor_tensor(c8(4), c8(3), c8(5), ALU.mult))
            chain(e.tensor_tensor(c8(5), c8(4), c8(4), ALU.mult))
            chain(e.tensor_scalar(c8(6), c8(5), 1.0 / 17, 1.0 / 15, ALU.mult, ALU.add))
            for k in (13, 11, 9, 7, 5, 3, 1):
                chain(e.tensor_tensor(c8(6), c8(6), c8(5), ALU.mult))
                chain(e.tensor_scalar(c8(6), c8(6), 1.0 / k, None, ALU.add))
            chain(e.tensor_tensor(c8(6), c8(6), c8(4), ALU.mult))
            chain(e.scalar_tensor_tensor(c8(6), c8(6), 2.0, c8(2), ALU.mult, ALU.add))
            chain(e.tensor_scalar(lru_c[:, :], c8(6), -8.0, None, ALU.mult))
            norm("in1", res, DT, lambda k: col("norm_mix_pre", k), sq)
            vec = sem("lru_vec")

            def lru_behind(u):
                j = u - 16
                if 0 <= j < LT:
                    v.wait_ge(drained, j + 1)
                    e.tensor_scalar(lru_x[:, j, :], z[:, j, :], cols[:, COL["conv_w"][0] + 24 + j:COL["conv_w"][0] + 25 + j],
                                    col("conv_b", j), ALU.mult, ALU.add).then_inc(sem("lru_conv"), 1)
                    for s_ in (1, 2, 3):
                        v.wait_ge(sem("lru_conv"), 4 * j + s_)
                        c0 = COL["conv_w"][0] + 8 * (3 - s_) + j
                        e.scalar_tensor_tensor(lru_x[:, j, s_:T], z[:, j, 0:T - s_], cols[:, c0:c0 + 1], lru_x[:, j, s_:T],
                                               ALU.mult, ALU.add).then_inc(sem("lru_conv"), 1)
                if u == 27:
                    v.wait_ge(sem("lru_sig"), 16)
                    e.tensor_tensor(lru_r[:, :, :], lru_r[:, :, :], lru_c[:, :].unsqueeze(2).to_broadcast([P, LT, T]),
                                    ALU.mult).then_inc(vec, 1)
                if u == 28:
                    v.wait_ge(drained, 26)
                    for g in range(NG):
                        for l2 in range(2):
                            for part, src in enumerate(window(z, 24 + g // 2, 64 * (g % 2), l2)):
                                e.tensor_copy(blk[64 * l2:64 * l2 + 64, 0, 8 * part:8 * part + 8, g * NCMP:(g + 1) * NCMP],
                                              src).then_inc(sem("blk_k"), 1)
                if u == 29:
                    v.wait_ge(sem("lru_act"), 1)
                    e.tensor_tensor(z[:, 0:LT, :], lru_a[:, :, :], lru_a[:, :, :], ALU.mult).then_inc(vec, 1)
                if u == 30:
                    v.wait_ge(sem("lru_act"), 2)
                    v.wait_ge(vec, 2)
                    e.scalar_tensor_tensor(z[:, 0:LT, :], z[:, 0:LT, :], 1.0, lru_r[:, :, :], ALU.add, ALU.mult).then_inc(vec, 1)
                if u in (31, 32):
                    v.wait_ge(sem("blk_k" if u == 31 else "blk_v"), 16)
                    e.tensor_tensor(blk[:, u - 31, :, :], blk[:, u - 31, :, :],
                                    col(("pe_k", "pe_v")[u - 31]).unsqueeze(2).to_broadcast([P, 16, 60]),
                                    ALU.add).then_inc(sem("blk_pe"), 1)
                if u == 33:
                    v.wait_ge(sem("lru_act"), 3)
                    v.wait_ge(sem("lru_ix"), 1)
                    e.tensor_tensor(lru_x[:, :, :], lru_x[:, :, :], lru_r[:, :, :], ALU.mult).then_inc(vec, 1)
                if u in (34, 35):
                    v.wait_ge(vec, 4)
                    for k in range(4 * (u - 34), 4 * (u - 34) + 4):
                        e.tensor_tensor_scan(lru_i[:, k, :], lru_a[:, k, :], lru_x[:, k, :], 0.0, ALU.mult, ALU.add).then_inc(vec, 1)
                if u == 36:
                    v.wait_ge(sem("lru_act"), 4)
                    v.wait_ge(vec, 12)
                    e.tensor_tensor(z[:, 0:LT, :], lru_i[:, :, :], z[:, LT:2 * LT, :], ALU.mult).then_inc(vec, 1)
            run_phase(v, "in1", lo, store("in1", z), behind=lru_behind)
            for kv in range(2):
                v.wait_ge(sem("blk_hi"), kv + 1)
                e.tensor_tensor(blk_s[:, kv, :, 60:120], blk[:, kv, :, :], blk_s[:, kv, :, 0:60].bitcast(F32),
                                ALU.subtract).then_inc(sem("blk_ready"), 1)
            run_phase(v, "cmp", lo, lambda i, w: drain(i, w, ev[:, w, 0:60], 60), unroll=True)
            v.wait_ge(sem("cmp_scores"), 1)
            pc = p_cmp[:, :, :]
            for h in range(2):
                chain(e.scalar_tensor_tensor(p_cmp[:, h:32:2, :], m[h][:, 0:240].rearrange("p (j n) -> p j n", n=NCMP), HD ** -0.5,
                                             bias_cmp[:, :, :, :].rearrange("p b h n -> p (b h) n")[:, h:32:2, :],
                                             ALU.mult, ALU.add))
            e.tensor_reduce(stat[:, 0:32], pc, AX.X, ALU.max).then_inc(sem("cmp_vec"), 1)
            v.wait_ge(sem("cmp_vec"), 1)
            e.tensor_tensor(pc, pc, stat[:, 0:32].unsqueeze(2).to_broadcast([P, 32, NCMP]), ALU.subtract).then_inc(sem("cmp_vec"), 2)
            v.wait_ge(sem("cmp_exp"), 1)
            chain(e.tensor_reduce(stat[:, 0:32], pc, AX.X, ALU.add))
            chain(e.reciprocal(stat[:, 32:64], stat[:, 0:32]))
            v.wait_ge(sem("tok_cp"), 3)
            chain(e.tensor_scalar(g_tok[:, 0, 0:16], g_tok[:, 0, 0:16], col("any_cmp"), None, ALU.mult))
            chain(e.tensor_tensor(stat[:, 0:32].rearrange("p (b h) -> p b h", b=2), stat[:, 32:64].rearrange("p (b h) -> p b h", b=2),
                                  g_tok[:, :, 0:16], ALU.mult))
            e.tensor_tensor(pc, pc, stat[:, 0:32].unsqueeze(2).to_broadcast([P, 32, NCMP]), ALU.mult).then_inc(sem("cmp_p"), 1)
            v.wait_ge(sem("bias_loaded"), 32)

            n_lru = NORM["lru"] + 1
            for it in range(NH + 1):
                b, o = it % 2, (it + 1) % 2
                if it < NH:
                    if it >= 2:
                        v.wait_ge(sem("pt_mm"), 2 * it - 2)
                    for at_ in range(2):
                        v.wait_ge(sem("s_mm"), 2 * it + at_ + 1)
                        e.scalar_tensor_tensor(s_att[:, b, at_, :], m[at_][:, 0:384], HD ** -0.5, bias[:, it, :], ALU.mult, ALU.add).then_inc(sem("s_bias"), 1)
                if it:
                    v.wait_ge(sem("att_exp"), it)
                    e.reciprocal(stat[:, 112 + 8 * o:116 + 8 * o], stat[:, 96 + 8 * o:100 + 8 * o]).then_inc(sem("att_inv"), 1)
                if it < NH:
                    v.wait_ge(sem("s_bias"), 2 * it + 2)
                    e.tensor_reduce(stat[:, 80 + 8 * b:82 + 8 * b], s_att[:, b, :, 0:128], AX.X, ALU.max).then_inc(sem("att_top"), 1)
                    e.tensor_reduce(stat[:, 82 + 8 * b:84 + 8 * b], s_att[:, b, :, 128:384], AX.X, ALU.max).then_inc(sem("att_top"), 1)
                if it:
                    v.wait_ge(sem("att_inv"), it)
                    e.tensor_tensor(stat[:, 128 + 8 * o:132 + 8 * o].rearrange("p (q a) -> p q a", a=2),
                                    stat[:, 112 + 8 * o:116 + 8 * o].rearrange("p (q a) -> p q a", a=2),
                                    g_tok[:, :, 15 + it:48:16], ALU.mult).then_inc(sem("att_fac"), 1)
                if it < NH:
                    v.wait_ge(sem("att_top"), 2 * it + 2)
                    e.tensor_scalar(stat[:, 64 + 8 * b:68 + 8 * b], stat[:, 80 + 8 * b:84 + 8 * b], -1.0, None, ALU.mult).then_inc(sem("att_max"), 1)
                if it:
                    v.wait_ge(sem("att_fac"), it)
                    for qb, c in enumerate((slice(0, 128), slice(128, 384))):
                        f = stat[:, 128 + 8 * o + 2 * qb:130 + 8 * o + 2 * qb]
                        e.tensor_tensor(s_att[:, o, :, c], s_att[:, o, :, c],
                                        f.unsqueeze(2).to_broadcast([P, 2, c.stop - c.start]), ALU.mult).then_inc(sem("att_p"), 1)
                if it == 3:
                    v.wait_ge(root_taken, n_lru)
                    e.reciprocal(rstd[:, :], rms[:, :]).then_inc(rstd_ready, 1)
                if 4 <= it < 12:
                    v.wait_ge(rstd_ready, n_lru)
                    e.scalar_tensor_tensor(lru_n[:, it - 4, :], z[:, it - 4, :], col("gnorm", it - 4), rstd[:, :],
                                           ALU.mult, ALU.mult).then_inc(scaled, 1)
            norm("nsa", z[:, 8:16, :], 8, lambda k: col("gnorm", 8 + k), z[:, 24:32, :])
            run_phase(v, "out1", lo, store("out1", y))
            norm("post1", y, DT, lambda k: col("norm_mix_post", k), sq)

        def up1(i, w):
            drain(i, w, ev[:, w, :])
            v.wait_ge(drained, 2 * i + (w + 1))
            v.wait_ge(f_ready, 2 * (i - cur[1]) + (w + cur[2] + 1))
            e.scalar_tensor_tensor(fv[:, w, :], ev[:, w, :], 0.0, ev[:, w, :], ALU.max, ALU.mult).then_inc(f_val, 1)

        def up2(i, w):
            drain(i, w, ev[:, w, :])
            if w == 1:
                v.wait_ge(drained, 2 * i + 2)
                v.wait_ge(gate_ready, (i - cur[1]) + (cur[4] + 1))
                v.wait_ge(f_ready, (i - cur[1]) + (cur[2] + PRIME))
                e.tensor_tensor(fv[:, 0, :], sg[:, 0, :], ev[:, 1, :], ALU.mult).then_inc(f_val, 1)

        def down_more(i, w):
            v.wait_ge(y_acc, 2 * (i - cur[1]) + (w + cur[3] + 1))
            drain(i, w, ev[:, w, :])

        cur = [0, 0, 0, 0, 0]

        def feed_forward(layer, name, up_fn, gain, post_gain):
            norm(name, res, DT, gain, sq)
            for (s_, g, n, up, down, f0, y0) in GROUPS:
                if s_ == layer:
                    v.wait_ge(y_acc, PRIME + y0)
                    cur[:] = [n, PH[up][0], f0, y0, GATES[up]]
                    run_phase(v, up, lo, up_fn, behind=s5_behind if s_ == "ffn0" and g == 2 and "s5" in plan else None)
                    cur[1] = PH[down][0]
                    run_phase(v, down, lo, down_more if g else store(down, y))
            norm("post_" + name, y, DT, post_gain, sq)

        def s5_behind(u):
            t5 = lambda n: s5t[:, n, :]
            TT = lambda o, x, y_, op: chain(e.tensor_tensor(t5(o), x, y_, op))
            TS = lambda o, x, a_, op0, b_=None, op1=ALU.bypass: chain(e.tensor_scalar(t5(o), t5(x), a_, b_, op0, op1))
            two_pi = 2 * math.pi
            if u == 0:
                v.wait_ge(sem("s5_par"), 1)
                e.tensor_tensor(t5(1), t5(0), col("lam_re"), ALU.mult).then_inc(sem("s5_ang"), 1)
                TT(2, t5(0), col("lam_im"), ALU.mult)
                TS(8, 2, 1.0 / two_pi, ALU.mult)
                TS(8, 8, 12582912.0, ALU.add)
                TS(8, 8, 12582912.0, ALU.subtract)
            if u == 1:
                c1 = 6.28125
                c2 = float(np.float32(round((two_pi - c1) * 2 ** 21) / 2 ** 21))
                c3 = float(np.float32(two_pi - c1 - c2))
                for c in (c1, c2, c3):
                    chain(e.scalar_tensor_tensor(t5(2), t5(8), -c, t5(2), ALU.mult, ALU.add))
                TS(9, 2, math.pi / 2, ALU.add)
            if u == 2:
                TS(10, 9, math.pi, ALU.is_gt, -two_pi, ALU.mult)
                TT(5, t5(9), t5(10), ALU.add)
                TS(5, 5, 3.1415925, ALU.min, -3.1415925, ALU.max)
                chain(e.tensor_scalar(t5(4), t5(2), 3.1415925, -3.1415925, ALU.min, ALU.max))
                e.tensor_copy(t5(10), t5(5)).then_inc(sem("s5_ang"), 1)
            if u == 4:
                v.wait_ge(sem("s5_par"), 3)
                TT(11, t5(3), t5(7), ALU.mult)
                TT(12, t5(3), t5(6), ALU.mult)
                for r in range(2):
                    halves = lambda n: t5(n).rearrange("p (h g) -> p h g", h=2)
                    chain(e.tensor_copy(lam[:, :, 0, r, :], halves(11)))
                    chain(e.tensor_scalar(lam[:, :, 1, r, :], halves(12), 1.0 - 2.0 * r, None, ALU.mult))
            if u == 5:
                TT(13, col("lam_re"), col("lam_re"), ALU.mult)
                TT(14, col("lam_im"), col("lam_im"), ALU.mult)
                TT(13, t5(13), t5(14), ALU.add)
                chain(e.reciprocal(t5(14), t5(13)))
                TS(15, 11, 1.0, ALU.subtract)
            if u == 6:
                TT(16, t5(15), col("lam_re"), ALU.mult)
                TT(17, t5(12), col("lam_im"), ALU.mult)
                TT(16, t5(16), t5(17), ALU.add)
                TT(16, t5(16), t5(14), ALU.mult)
            if u == 7:
                TT(18, t5(12), col("lam_re"), ALU.mult)
                TT(17, t5(15), col("lam_im"), ALU.mult)
                TT(18, t5(18), t5(17), ALU.subtract)
                TT(18, t5(18), t5(14), ALU.mult)
            r, stage = (u - 8) // 3, (u - 8) % 3
            if r in (0, 1):
                for h_ in range(2):
                    pr = slice(64 * h_, 64 * h_ + 64)
                    band = b_dia[pr, r, :, 16 * h_:16 * h_ + 16]
                    wide = lambda n: s5t[pr, n, :].unsqueeze(2).to_broadcast([64, 64, 16])
                    if stage == 0:
                        if u == 8 and h_ == 0:
                            v.wait_ge(sem("s5_loaded"), 16)
                            v.wait_ge(sem("b_zero"), 1)
                        e.tensor_tensor(band, b_raw[pr, r, :, :], wide(16), ALU.mult).then_inc(sem("b_first"), 1)
                    elif stage == 1:
                        e.tensor_tensor(b_tmp[pr, :, :], b_raw[pr, 1 - r, :, :], wide(18), ALU.mult).then_inc(sem("b_second"), 1)
                    else:
                        v.wait_ge(sem("b_first"), 2 * r + h_ + 1)
                        v.wait_ge(sem("b_second"), 2 * r + h_ + 1)
                        e.tensor_tensor(band, band, b_tmp[pr, :, :], ALU.add if r else ALU.subtract).then_inc(sem("b_done"), 1)
                if stage == 2:
                    v.wait_ge(sem("b_done"), 2 * r + 2)

        def gain2(layer, which):
            return lambda k: col("norms2", 64 * layer + 16 * which + k)

        if "mlp" in plan:
            feed_forward("mlp", "mlp", up1, lambda k: col("norm_mlp_pre", k), lambda k: col("norm_mlp_post", k))
        if "ple" in plan:
            v.wait_ge(sem("p_hi"), 1)
            e.tensor_tensor(p_s[:, :, T:2 * T], p_in[:, :, :], p_s[:, :, 0:T].bitcast(F32), ALU.subtract).then_inc(sem("p_ready"), 1)

            i0 = PH["proj"][0]
            lo(i0, 3)
            for mt in range(DT):
                if mt % 8 == 7:
                    v.wait_ge(low_copied, 2 * i0 + mt // 8 + 1)
                else:
                    v.wait_ge(sem("proj_low"), mt + 1 - mt // 8)
                e.tensor_tensor(y[:, mt, :], bank[mt % 2][:, 0:T], low[:, mt % 2, :],
                                ALU.add).then_inc(drained if mt % 8 == 7 else sem("proj_y"), 1)
            for q in range(3):
                lo(i0 + 1, q)

            def gate(i, w):
                drain(i, w, ev[:, w, :])
            run_phase(v, "gate", lo, gate)
        if "mix2" in plan:
            norm("in2", res, DT, gain2(0, 0), sq)
            run_phase(v, "in2", lo, store("in2", z))
            v.wait_ge(sem("mix2_loaded"), 32)
            v.wait_ge(drained, 2 * PH["in2"][1])
            def sb_logits(n):
                b = n % 2
                if n >= 2:
                    v.wait_ge(sem("sb_ex"), 2 * n - 2)
                for j in range(2):
                    v.wait_ge(sem("sb_s"), 2 * n + j + 1)
                    e.scalar_tensor_tensor(zs[:, b, j, :], m[j][:, 0:384], 128 ** -0.5, mask_sb[:, :], ALU.mult, ALU.add).then_inc(sem("sb_zs"), 1)
                v.wait_ge(sem("sb_zs"), 2 * n + 2)
                e.scalar_tensor_tensor(se[:, b, :, :], zs[:, b, :, :], -1.0, zs[:, b, :, :], ALU.mult, ALU.min).then_inc(sem("sb_z"), 1)
            sb_logits(0)
            v.wait_ge(sem("gl_mm"), 1)
            for k in range(4):
                e.tensor_scalar(gl[:, k, :], bank[k // 2][:, T * (k % 2):T * (k % 2) + T], col("b_gate", k), None, ALU.add).then_inc(sem("gla_gl"), 1)
            v.wait_ge(sem("gla_gl"), 4)
            glf = gl[:, :, :].rearrange("p k t -> p (k t)")
            e.scalar_tensor_tensor(dif[:, :], glf, -1.0, glf, ALU.mult, ALU.min).then_inc(sem("gla_n"), 1)
            for n in range(SBH // 2):
                b = n % 2
                if n + 1 < SBH // 2:
                    sb_logits(n + 1)
                v.wait_ge(sem("sb_ln"), n + 1)
                if n:
                    v.wait_ge(sem("sb_u"), 2 * n)
                e.scalar_tensor_tensor(sp[:, :, :], zs[:, b, :, :], 0.0, se[:, b, :, :], ALU.max, ALU.add).then_inc(sem("sb_sp"), 1)
                for j in range(2):
                    v.wait_ge(sem("sb_u"), 2 * n + j + 1)
                    if n:
                        v.wait_ge(sem("sb_o"), 2 * n - 1 + j)
                    e.tensor_tensor(sw[:, j, :], m[2 + j][:, 0:384], zs[:, b, j, :], ALU.add).then_inc(sem("sb_ex"), 1)
                if n == 0:
                    v.wait_ge(sem("gla_e"), 2)
                    chain(e.scalar_tensor_tensor(glf, glf, 0.0, dec[:, :], ALU.min, ALU.subtract))
                    v.wait_ge(sem("one_row"), 1)
                    for k in range(4):
                        e.tensor_tensor_scan(cum[:, k, :], one_row[:, :], gl[:, k, :], 0.0, ALU.mult, ALU.add).then_inc(sem("gla_cum"), 1)
            zq = z[:, 24:28, :].rearrange("p k t -> p (k t)")
            zk = z[:, 28:32, :].rearrange("p k t -> p (k t)")
            v.wait_ge(sem("sb_cp"), 8)
            def level_distance(l):
                d = (dif, dif1)[l % 2]
                v.wait_ge(sem("lv_sub"), l + 1)
                e.scalar_tensor_tensor(d[:, :], d[:, :], -1.0, d[:, :], ALU.mult, ALU.min).then_inc(sem("lv_dif"), 1)
            level_distance(0)
            for l in range(LEVELS):
                size = 2 << l
                half = size // 2
                if l + 1 < LEVELS:
                    level_distance(l + 1)
                v.wait_ge(sem("lv_exp"), l + 1)
                for dst, src, second in ((k_lv, zk, False), (q_lv, zq, True)):
                    e.tensor_tensor(dst[:, l, :, :].rearrange("p k c -> p (k c)").rearrange("p (n b) -> p n b", b=half),
                                    tokens(src, size, second), tokens((dec, dec1)[l % 2][:, :], size, second), ALU.mult).then_inc(sem("lv_done"), 1)
            v.wait_ge(sem("masks_loaded"), 16)

            def head_norm(h):
                v.wait_ge(sem("gn_rt"), h + 1)
                if h >= 2:
                    v.wait_ge(sem("gn_o"), h - 1)
                e.reciprocal(o_rstd[:, h % 2, :], o_rms[:, h % 2, :]).then_inc(sem("gn_rs"), 1)
                v.wait_ge(sem("gn_rs"), h + 1)
                e.scalar_tensor_tensor(z[:, 8 + h, :], z[:, 8 + h, :], col("gla_gain", h), o_rstd[:, h % 2, :],
                                       ALU.mult, ALU.mult).then_inc(sem("gn_o"), 1)
            for it in range(24):
                n = 2 if it % 3 == 2 else 4
                s0 = 4 * (it % 3)
                v.wait_ge(sem("gs_mm"), it + 1)
                if it >= 2:
                    v.wait_ge(sem("go_step"), it - 1)
                e.scalar_tensor_tensor(pm[:, it % 2, 0:n, :].rearrange("p n c -> p (n c)"), m[it % 2][:, 0:128 * n], 0.125,
                                       masks[:, s0:s0 + n, :].rearrange("p n c -> p (n c)"), ALU.mult, ALU.mult).then_inc(sem("pm_done"), 1)
                if it % 3 == 2 and it >= 5:
                    head_norm(it // 3 - 1)
            head_norm(7)
            run_phase(v, "out2", lo, store("out2", y))
            norm("post2", y, DT, gain2(0, 1), sq)
        if "ffn0" in plan:
            feed_forward("ffn0", "ffn0", up2, gain2(0, 2), gain2(0, 3))
        if "s5" in plan:
            if "ffn0" not in plan:
                for u in range(24):
                    s5_behind(u)
            norm("s5", res, DT, gain2(1, 0), u5)
            v.wait_ge(sem("c_loaded"), 16)
            v.wait_ge(sem("s5_zero"), 2)
            for r, f in ((0, 1.0), (1, -1.0)):
                for h_ in range(2):
                    e.tensor_scalar(c_lhs[64 * h_:64 * h_ + 64, r, :, 16 * h_:16 * h_ + 16],
                                    c_raw[64 * h_:64 * h_ + 64, r, :, :], f, None, ALU.mult).then_inc(sem("c_done"), 1)

            def y_add(tb):
                for n in range(2):
                    v.wait_ge(sem("y5_mm"), 2 * tb + n + 1)
                    v.wait_ge(sem("y5_skip"), tb + 1)
                    e.tensor_tensor(u5[:, 8 * n:8 * n + 8, 64 * tb:64 * tb + 64], u5[:, 8 * n:8 * n + 8, 64 * tb:64 * tb + 64],
                                    m[4 + n][:, :].rearrange("p (k t) -> p k t", k=8), ALU.add).then_inc(sem("y5_add"), 1)
            def scan(st, t, prev, n):
                for step in range(3):
                    for h in range(2):
                        if not (isinstance(n, int) and n + step == 0):
                            v.wait_ge(scan_step[h], n + step)
                        g = slice(32 * h, 32 * h + 32)
                        now = st[:, t, :, g]
                        if step == 0:
                            ins = e.tensor_tensor(prod[:, h, :, :, :], lam[:, h, :, :, :],
                                                  prev[:, :, g].unsqueeze(1).to_broadcast([P, 2, 2, 32]), ALU.mult)
                        elif step == 1:
                            ins = e.tensor_tensor(now, now, prod[:, h, 0, :, :], ALU.add)
                        else:
                            ins = e.tensor_tensor(now, now, prod[:, h, 1, ::-1, :], ALU.add)
                        ins.then_inc(scan_step[h], 1)
            for tb in range(4):
                st, prev = ((st0, st1), (st1, st0))[tb % 2]
                v.wait_ge(sem("bu_cp"), 16 * tb + 16)
                if tb:
                    scan(st, 0, prev[:, 63, :, :], 3 * (64 * tb - 1))
                for t in range(1, 64):
                    scan(st, t, st[:, t - 1, :, :], 3 * (64 * tb + t - 1))
                if tb:
                    y_add(tb - 1)
            y_add(3)

            def glu(i, w):
                drain(i, w, ev[:, w, :])
                if w == 1:
                    v.wait_ge(drained, 2 * i + 2)
                    v.wait_ge(gate_ready, (i - PH["glu"][0]) + (GATES["glu"] + 1))
                    e.tensor_tensor(y[:, i - PH["glu"][0], :], sg[:, 0, :], ev[:, 1, :], ALU.mult).then_inc(sem("glu_y"), 1)
            run_phase(v, "glu", lo, glu)
            norm("post_s5", y, DT, gain2(1, 1), sq)
        if "ffn1" in plan:
            feed_forward("ffn1", "ffn1", up2, gain2(1, 2), gain2(1, 3))

    @block.gpsimd
    def _(g):
        e = nc.gpsimd
        e.memset(ones[:, :], 1.0).then_inc(setup, 1)
        e.memset(neg_ones[:, :], -1.0).then_inc(setup, 1)
        e.memset(eps_col[:, :], EPS).then_inc(setup, 1)
        e.memset(ident[:, :], 0.0).then_inc(sem("ident0"), 1)
        g.wait_ge(sem("ident0"), 1)
        e.affine_select(out=ident[:, :], in_=ident[:, :], compare_op=ALU.not_equal, fill=1.0, base=0,
                        pattern=[[-1, P]], channel_multiplier=1).then_inc(setup, 1)
        e.memset(fv[:, 0, 0:2], 0.0).then_inc(f_ready, PRIME)
        e.memset(fv[:, 0, 2:4], 0.0).then_inc(y_acc, PRIME)
        e.memset(fv[:, 0, 4:6], 0.0).then_inc(sem("ple_used"), PRIME)

        def act_low(name, src, tiles_=range(DT)):
            for k in tiles_:
                g.wait_ge(act_hi, DT * ACTS[name] + k + 1)
                e.tensor_tensor(act[:, k, T:2 * T], src(k), act[:, k, 0:T].bitcast(F32), ALU.subtract).then_inc(act_ready, 1)

        def add_residual(name):
            for k in range(DT):
                g.wait_ge(scaled, SCALED[name] + k + 1)
                e.tensor_tensor(res[:, k, :], res[:, k, :], sq[:, k, :], ALU.add).then_inc(res_added, 1)

        def s5_zero():
            if "ffn0" in plan:
                g.wait_ge(act_ready, DT * (ACTS["ffn0"] + 1))
            e.memset(b_dia[:, :, :, :], 0.0).then_inc(sem("b_zero"), 1)

        def square_sum(name, begin, ready):
            g.wait_ge(sum_spread, NORM[name])
            e.memset(ssum[:, :], 0.0).then_inc(y_squares, 1)
            for i in range(DT // 2):
                for w in range(2):
                    begin(i, w)
                    g.wait_ge(*ready(i, w))
                    e.tensor_tensor(sq[:, 2 * i + w, :], y[:, 2 * i + w, :], y[:, 2 * i + w, :], ALU.mult).then_inc(y_squares, 1)
                    g.wait_ge(y_squares, 4 * i + (YSQ[name] + 2 * w + 2))
                    e.tensor_tensor(ssum[:, :], ssum[:, :], sq[:, 2 * i + w, :], ALU.add).then_inc(y_squares, 1)

        for k in range(0, DT, 4):
            g.wait_ge(*x_piece(k))
        if "mix1" in plan:
            act_low("in1", lambda k: sq[:, k, :])
            g.wait_ge(sem("lru_sig"), 16)
            e.tensor_tensor(lru_x[:, :, :], lru_x[:, :, :], lru_i[:, :, :], ALU.mult).then_inc(sem("lru_ix"), 1)
            act_low("out1", lambda k: lru_n[:, k, :] if k < 8 else z[:, 16 + k, :])
            square_sum("post1", lambda i, w: None, lambda i, w: (drained, 2 * i + (2 * PH["out1"][0] + w + 1)))
            add_residual("post1")

        def feed_forward(layer, name, paired):
            act_low(name, lambda k: sq[:, k, :])
            for (s_, gr, n, up, down, f0, y0) in GROUPS:
                if s_ != layer:
                    continue

                def f_low(tile, w):
                    g.wait_ge(f_hi, f0 + 1 + tile)
                    e.tensor_tensor(ffn[:, tile, T:2 * T], fv[:, w, :], ffn[:, tile, 0:T].bitcast(F32), ALU.subtract).then_inc(f_ready, 1)
                if name == "ffn0" and gr == 2 and "s5" in plan:
                    s5_zero()
                if paired:
                    with g.Fori(0, n) as i:
                        f_low(i, 0)
                else:
                    with g.Fori(0, n // 2) as i:
                        f_low(2 * i, 0)
                        f_low(2 * i + 1, 1)

                def accumulate(i, w):
                    g.wait_ge(drained, 2 * i + (2 * PH[down][0] + w + 1))
                    e.tensor_tensor(y[:, 2 * i + w, :], y[:, 2 * i + w, :], ev[:, w, :], ALU.add).then_inc(y_acc, 1)
                if y0 + DT == last_y[layer] and gr:
                    square_sum("post_" + name, accumulate, lambda i, w: (y_acc, 2 * i + (PRIME + y0 + w + 1)))
                elif gr:
                    with g.Fori(0, DT // 2) as i:
                        for w in range(2):
                            accumulate(i, w)
            add_residual("post_" + name)
        if "mlp" in plan:
            feed_forward("mlp", "mlp", False)
        if "ple" in plan:
            act_low("gate", lambda k: res[:, k, :])
            with g.Fori(0, DT // 2) as i:
                for w in range(2):
                    g.wait_ge(gate_ready, 2 * i + (GATES["gate"] + w + 1))
                    e.tensor_tensor(y[:, 2 * i + w, :], y[:, 2 * i + w, :], sg[:, w, :], ALU.mult).then_inc(sem("ple_used"), 1)
                    g.wait_ge(sem("ple_used"), 2 * i + (PRIME + w + 1))
                    e.tensor_tensor(res[:, 2 * i + w, :], res[:, 2 * i + w, :], y[:, 2 * i + w, :], ALU.add).then_inc(res_added, 1)
        if "mix2" in plan:
            act_low("in2", lambda k: sq[:, k, :])
            g.wait_ge(drained, 2 * PH["in2"][1])
            e.memset(one_row[:, :], 1.0).then_inc(sem("one_row"), 1)
            g.wait_ge(sem("gla_cum"), 4)
            for l in range(LEVELS):
                size = 2 << l
                if l >= 2:
                    g.wait_ge(sem("lv_exp"), l - 1)
                cv = cum[:, :, :].rearrange("p k t -> p (k t)").rearrange("p (n b) -> p n b", b=size)
                e.tensor_tensor((dif, dif1)[l % 2][:, :].rearrange("p (n b) -> p n b", b=size), cv,
                                cv[:, :, size // 2 - 1:size // 2].to_broadcast([P, 1024 // size, size]), ALU.subtract).then_inc(sem("lv_sub"), 1)
            act_low("out2", lambda k: z[:, k, :], range(8))
            g.wait_ge(sem("lv_done"), 2 * LEVELS)
            g.wait_ge(sem("gn_si"), 1)

            def gate(k):
                g.wait_ge(sem("gn_o"), k + 1)
                e.tensor_tensor(z[:, 8 + k, :], z[:, 8 + k, :], z[:, 40 + k, :], ALU.mult).then_inc(sem("gn_y"), 1)
            for it in range(24):
                h, r = it // 3, it % 3
                if it >= 2:
                    g.wait_ge(sem("gv_mm"), it - 1)
                for n in range(2 if r == 0 else 0, 2 if r == 2 else 4):
                    last = e.tensor_copy(v_first[:, it % 2, n, :].rearrange("p (n b) -> p n b", b=1 << (4 * r + n - 2)),
                                         tokens(z[:, 32 + h, :], 2 << (4 * r + n - 2), False))
                last.then_inc(sem("v_first_ready"), 1)
                if it % 3 == 2 and it >= 8:
                    gate(it // 3 - 2)
            gate(6)
            gate(7)
            act_low("out2", lambda k: z[:, k, :], range(8, 16))
            square_sum("post2", lambda i, w: None, lambda i, w: (drained, 2 * i + (2 * PH["out2"][0] + w + 1)))
            add_residual("post2")
        if "ffn0" in plan:
            feed_forward("ffn0", "ffn0", True)
        if "s5" in plan:
            if before["s5"]:
                g.wait_ge(res_added, before["s5"])
            else:
                s5_zero()
            g.wait_ge(sem("b_done"), 4)
            e.memset(c_lhs[:, 0, :, :], 0.0).then_inc(sem("s5_zero"), 1)
            e.memset(c_lhs[:, 1, :, :], 0.0).then_inc(sem("s5_zero"), 1)
            for tb in range(4):
                g.wait_ge(sem("bu_mm"), 16 * tb + 16)
                e.tensor_tensor(u5[:, :, 64 * tb:64 * tb + 64], u5[:, :, 64 * tb:64 * tb + 64],
                                col("d_skip").unsqueeze(2).to_broadcast([P, DT, 64]), ALU.mult).then_inc(sem("y5_skip"), 1)
            act_low("glu", lambda k: u5[:, k, :])
            square_sum("post_s5", lambda i, w: None, lambda i, w: (sem("glu_y"), 2 * i + (w + 1)))
            add_residual("post_s5")
        if "ffn1" in plan:
            feed_forward("ffn1", "ffn1", True)

    @block.tensor
    def _(pe):
        mm = nc.tensor.matmul

        def unit(i, w, x, kt, n=T, tile_ready=None):
            if not (isinstance(i, int) and i == 0):
                pe.wait_ge(drained, 2 * i + (w - 1))
            hk = kt // 2
            for h in range(2):
                q = 2 * w + h
                pe.wait_ge(lo_ready, 4 * i + (q + 1))
                for k in range(hk):
                    wt = slice(k * P, (k + 1) * P)
                    if tile_ready:
                        pe.wait_ge(*tile_ready(h * hk + k))
                    mm(bank[w][:, 0:2 * n], w_hi[:, q, wt], x(h * hk + k, 0, 2 * n), start=(h == 0 and k == 0), stop=False)
                    last = mm(bank[w][:, n:2 * n], w_lo[:, q, wt], x(h * hk + k, 0, n), start=False,
                              stop=(h == 1 and k == hk - 1))
                last.then_inc(halves_used, 1)

        def gemm(name, x, kt, tile_ready, behind=None):
            start, end = PH[name]
            unit(start, 0, x, kt, tile_ready=tile_ready)
            if behind and start:
                behind(0)
            unit(start, 1, x, kt)
            if behind and start:
                behind(1)
            looped = end if not behind else LT if start == 0 else start + 1
            if looped > start + 1:
                with pe.Fori(start + 1, looped) as i:
                    for w in range(2):
                        unit(i, w, x, kt)
            for i in range(looped, end):
                for w in range(2):
                    unit(i, w, x, kt)
                    behind(2 * (i - start) + w)

        x_act = lambda k, a_, b_: act[:, k, a_:b_]
        x_ffn = lambda k, a_, b_: ffn[:, k, a_:b_]

        def s5_behind(u):
            n = u - 14
            if 0 <= n < 8:
                pe.wait_ge(sem("b_done"), 2 * (n // 4) + 2)
                if n >= 4:
                    pe.wait_ge(sem("blhs_cp"), n - 3)
                for k in range(4):
                    kt = 4 * (n % 4) + k
                    last = nc.tensor.transpose(m[n % 4][:, 128 * k:128 * k + 128],
                                               b_dia[:, n // 4, 4 * kt:4 * kt + 4, :].rearrange("p a c -> p (a c)"), ident[:, :])
                last.then_inc(sem("blhs_mm"), 1)

        def norm(name, squares=None, kt=DT):
            if squares is None:
                pe.wait_ge(y_squares, YSQ[name] + 2 * DT + 1)
                mm(m[5][:, 0:T], ones[:, :], ssum[:, :], start=True, stop=True).then_inc(sum_spread, 1)
                return
            for k in range(kt):
                pe.wait_ge(squared, SQUARED[name] + k + 1)
                last = mm(m[5][:, 0:T], ones[:, :], squares[:, k, :], start=(k == 0), stop=(k == kt - 1))
            last.then_inc(sum_spread, 1)

        def act_tile(name):
            return lambda k: (act_ready, DT * ACTS[name] + k + 1)

        pe.wait_ge(setup, 5)
        pe.wait_ge(consts, NCONST)
        if "mix1" in plan:
            mm(m[0][0:NH, 0:384], rel[:, :], rev_hot[:, :], start=True, stop=True)
            for b in range(2):
                for n in range(NCMP):
                    s0 = 224 + 128 * b - 16 * n
                    last = mm(m[1][:, (b * NCMP + n) * NH:(b * NCMP + n + 1) * NH], fwd_hot[:, s0:s0 + 128], rel[:, :], start=True, stop=True)
            last.then_inc(sem("setup_mm"), 1)
            norm("in1", sq)
            def lru_gates(u):
                j = u - 18
                if not 0 <= j < LT:
                    return
                if j == 0:
                    pe.wait_ge(sem("lru_loaded"), 16)
                pe.wait_ge(sem("lru_conv"), 4 * j + 4)
                if j >= 2:
                    pe.wait_ge(sem("lru_sig"), 2 * (j - 1))
                for wx in range(2):
                    for h in range(2):
                        pr = slice(64 * h, 64 * h + 64)
                        last = mm(m[j % 2][pr, wx * T:(wx + 1) * T], lru_wt[pr, wx, j, :], lru_x[pr, j, :], start=True, stop=True)
                last.then_inc(sem("lru_mm"), 1)
            gemm("in1", x_act, 16, act_tile("in1"), behind=lru_gates)
            pe.wait_ge(drained, 2 * PH["in1"][1])
            for tb in range(2):
                for at_, tile in enumerate((30, 34)):
                    for f in range(2):
                        last = nc.tensor.transpose(m[2 + tb][:, 256 * at_ + 128 * f:256 * at_ + 128 * f + 128],
                                                   z[:, tile + f, 128 * tb:128 * tb + 128], ident[:, :])
            last.then_inc(sem("tok_mm"), 1)
            pe.wait_ge(sem("gate_sig"), 1)
            for tb in range(2):
                last = nc.tensor.transpose(m[4][:, 48 * tb:48 * tb + 48], z[0:48, 36, 128 * tb:128 * tb + 128], ident[0:48, 0:48])
            last.then_inc(sem("tok_mm"), 1)
            for kv in range(2):
                pe.wait_ge(sem("blk_ready"), kv + 1)
                for w in range(2):
                    unit(PH["cmp"][0] + kv, w, lambda k, a_, b_, kv=kv: blk_s[:, kv, k, a_:b_], 16, 60)
            pe.wait_ge(sem("hid_ready"), 4)
            w2k, w2v = COL["w2_k"][0], COL["w2_v"][0]
            for f in range(2):
                mm(m[0][:, 0:60], cols[:, w2k + 128 * f:w2k + 128 * f + 128], hid[:, 0, f, :], start=(f == 0), stop=(f == 1))
            for g_ in range(NG):
                for f in range(2):
                    last = mm(m[1][0:NCMP, 64 * g_:64 * g_ + 64], hid[:, 1, f, g_ * NCMP:(g_ + 1) * NCMP],
                              cols[:, w2v + 64 * f:w2v + 64 * f + 64], start=(f == 0), stop=(f == 1))
            last.then_inc(sem("cmp_mm"), 1)
            pe.wait_ge(sem("cmp_cp"), 2)
            for b in range(2):
                for hh in range(NH):
                    j, h = hh // 2, hh % 2
                    g_ = 2 * (j // 4) + h
                    pr = slice(64 * h, 64 * h + 64)
                    last = mm(m[h][:, (8 * b + j) * NCMP:(8 * b + j + 1) * NCMP], z[pr, 16 + j, 128 * b:128 * b + 128],
                              k_cmp[pr, g_ * NCMP:(g_ + 1) * NCMP], start=True, stop=True)
            last.then_inc(sem("cmp_scores"), 1)
            norm("lru", lru_n, 8)
            pe.wait_ge(sem("cmp_p"), 1)

            def scores(hh):
                j, h = hh // 2, hh % 2
                pr = slice(64 * h, 64 * h + 64)
                for at_ in range(2):
                    kt = (28, 32)[at_] + j // 4
                    if hh:
                        pe.wait_ge(sem("s_bias"), 2 * hh + at_ - 1)
                    mm(m[at_][:, 128:384], z[pr, 16 + j, 128:256], z[pr, kt, :], start=True, stop=True)
                    mm(m[at_][:, 0:128], z[pr, 16 + j, 0:128], z[pr, kt, 0:128], start=True, stop=True).then_inc(sem("s_mm"), 1)

            def cmp_weights(j):
                if j >= 1:
                    pe.wait_ge(sem("pct_cp"), j)
                for h in range(2):
                    for b in range(2):
                        last = nc.tensor.transpose(m[5][0:NCMP, T * h + 128 * b:T * h + 128 * b + 128],
                                                   p_cmp[:, 16 * b + 2 * j + h, :], ident[:, :])
                last.then_inc(sem("pct_mm"), 1)

            def transposes(hh):
                pe.wait_ge(sem("att_p"), 2 * hh + 2)
                for at_ in range(2):
                    if hh:
                        pe.wait_ge(sem("pt_cp"), 2 * hh + at_ - 1)
                    for n in range(3):
                        last = nc.tensor.transpose(m[2 + at_][:, 128 * n:128 * n + 128], s_att[:, hh % 2, at_, 128 * n:128 * n + 128], ident[:, :])
                    last.then_inc(sem("pt_mm"), 1)

            def results(hh):
                j, h = hh // 2, hh % 2
                b, g_ = hh % 2, 2 * (j // 4) + h
                o = (m[4], bank[0])[j % 2][64 * h:64 * h + 64, :]
                if h == 0:
                    pe.wait_ge(sem("pct_cp"), j + 1)
                    if j >= 2:
                        pe.wait_ge(sem("o_cp"), j - 1)
                mm(o[:, 0:T], v_cmp[:, 64 * g_:64 * g_ + 64], pt_cmp[:, j % 2, h, :], start=True, stop=False)
                for at_ in range(2):
                    pe.wait_ge(sem("pt_cp"), 2 * hh + at_ + 1)
                    mm(o[:, 0:T], v_tok[:, 0, at_, 64 * g_:64 * g_ + 64], pt_att[:, b, at_, 0:T], start=False, stop=False)
                    last = mm(o[:, 128:T], v_tok[:, 1, at_, 64 * g_:64 * g_ + 64], pt_att[:, b, at_, T:384], start=False, stop=(at_ == 1))
                last.then_inc(sem("pv_mm"), 1)
            pe.wait_ge(root_taken, NORM["lru"] + 1)
            scores(0)
            for it in range(NH + 2):
                if it + 1 < NH:
                    scores(it + 1)
                if 1 <= it <= NH:
                    if it % 2:
                        cmp_weights(it // 2)
                    transposes(it - 1)
                if it >= 2:
                    results(it - 2)
            norm("nsa", z[:, 24:32, :], 8)
            gemm("out1", x_act, 16, act_tile("out1"))
            norm("post1")

        def feed_forward(layer, name):
            norm(name, sq)
            for (s_, g_, n, up, down, f0, y0) in GROUPS:
                if s_ != layer:
                    continue
                gemm(up, x_act, 16, act_tile(name),
                     behind=s5_behind if s_ == "ffn0" and g_ == 2 and "s5" in plan else None)
                gemm(down, x_ffn, n, lambda k: (f_ready, PRIME + f0 + k + 1))
            norm("post_" + name)
        if "mlp" in plan:
            feed_forward("mlp", "mlp")
        if "ple" in plan:
            pe.wait_ge(sem("p_ready"), 1)
            i0 = PH["proj"][0]
            if i0:
                pe.wait_ge(drained, 2 * i0)
            for mt in range(DT):
                q = mt // 4
                pe.wait_ge(lo_ready, 4 * i0 + q + 1)
                if mt >= 2:
                    if (mt - 2) % 8 == 7:
                        pe.wait_ge(drained, 2 * i0 + 1)
                    else:
                        pe.wait_ge(sem("proj_y"), mt - 1 - (mt >= 9))
                for k in range(2):
                    wt = slice((2 * (mt % 4) + k) * P, (2 * (mt % 4) + k + 1) * P)
                    mm(bank[mt % 2][:, :], w_hi[:, q, wt], p_s[:, k, :], start=(k == 0), stop=False)
                    last = mm(bank[mt % 2][:, T:2 * T], w_lo[:, q, wt], p_s[:, k, 0:T], start=False, stop=(k == 1))
                last.then_inc(halves_used if mt % 4 == 3 else sem("proj_mm"), 1)
            gemm("gate", x_act, 16, act_tile("gate"))
        if "mix2" in plan:
            norm("in2", sq)
            gemm("in2", x_act, 16, act_tile("in2"))
            pe.wait_ge(drained, 2 * PH["in2"][1])
            for n in range(4):
                for k in range(4):
                    last = nc.tensor.transpose(m[n][:, 128 * k:128 * k + 128],
                                               z[:, 16 + 4 * (n % 2) + k, 128 * (n // 2):128 * (n // 2) + 128], ident[:, :])
                last.then_inc(sem("sbv_mm"), 1)
            pe.wait_ge(sem("mix2_loaded"), 32)
            for k in range(4):
                last = mm(bank[k // 2][:, T * (k % 2):T * (k % 2) + T], w_gu[:, 128 * k:128 * k + 128], z[0:16, 48, :], start=True, stop=True)
            last.then_inc(sem("gl_mm"), 1)
            pe.wait_ge(sem("sbv_cp"), 4)

            def sb_scores(n):
                for j in range(2):
                    h = 2 * n + j
                    if n:
                        pe.wait_ge(sem("sb_zs"), h - 1)
                    mm(m[j][:, 0:T], z[:, 8 + h, 0:128], z[:, h, :], start=True, stop=True)
                    mm(m[j][:, T:384], z[:, 8 + h, 128:T], z[:, h, 128:T], start=True, stop=True).then_inc(sem("sb_s"), 1)
            sb_scores(0)
            for n in range(SBH // 2):
                if n + 1 < SBH // 2:
                    sb_scores(n + 1)
                pe.wait_ge(sem("sb_sp"), n + 1)
                for j in range(2):
                    if n:
                        pe.wait_ge(sem("sb_ex"), 2 * n - 1 + j)
                    mm(m[2 + j][:, 0:T], neg_upper[:, :], sp[:, j, 0:T], start=True, stop=False)
                    mm(m[2 + j][:, 128:T], neg_ones[:, :], sp[:, j, T:384], start=False, stop=True)
                    mm(m[2 + j][:, T:384], neg_upper[:, :], sp[:, j, T:384], start=True, stop=True).then_inc(sem("sb_u"), 1)
                pe.wait_ge(sem("sb_w"), n + 1)
                for j in range(2):
                    if n:
                        pe.wait_ge(sem("sb_cp"), 2 * n - 1 + j)
                    hv = slice(128 * (2 * n + j), 128 * (2 * n + j) + 128)
                    mm(m[4 + j][:, 0:T], sb_v[:, 0, hv], sw[:, j, 0:T], start=True, stop=False)
                    mm(m[4 + j][:, 128:T], sb_v[:, 1, hv], sw[:, j, T:384], start=False, stop=True).then_inc(sem("sb_o"), 1)
            pe.wait_ge(sem("sb_cp"), 8)
            pe.wait_ge(sem("lv_done"), 2 * LEVELS)

            def gla_scores(it):
                h, r = it // 3, it % 3
                tl, pr = h // 2, slice(64 * (h % 2), 64 * (h % 2) + 64)
                if it >= 2:
                    pe.wait_ge(sem("pm_done"), it - 1)
                for n in range(2 if r == 2 else 4):
                    o = m[it % 2][:, 128 * n:128 * n + 128]
                    if r == 0 and n < 2:
                        tk = slice(128 * n, 128 * n + 128)
                        last = mm(o, z[pr, 28 + tl, tk], z[pr, 24 + tl, tk], start=True, stop=True)
                    else:
                        l = 4 * r + n - 2
                        last = mm(o, k_lv[pr, l, tl, :], q_lv[pr, l, tl, :], start=True, stop=True)
                last.then_inc(sem("gs_mm"), 1)
                if it >= 2:
                    pe.wait_ge(sem("gv_cp"), it - 1)
                pe.wait_ge(sem("v_first_ready"), it + 1)
                for n in range(2 if r == 2 else 4):
                    o = m[2 + it % 2][:, 128 * n:128 * n + 128]
                    if r == 0 and n < 2:
                        src = z[:, 32 + h, 128 * n:128 * n + 128]
                    else:
                        src = v_first[:, it % 2, n, :]
                    last = nc.tensor.transpose(o, src, ident[:, :])
                last.then_inc(sem("gv_mm"), 1)

            def gla_results(it):
                h, r = it // 3, it % 3
                o = m[4 + h % 2]
                pe.wait_ge(sem("pm_done"), it + 1)
                pe.wait_ge(sem("gv_cp"), it + 1)
                if r == 0 and h >= 2:
                    pe.wait_ge(sem("go_cp"), h - 1)
                for n in range(2 if r == 2 else 4):
                    if r == 0 and n < 2:
                        dst = o[:, 128 * n:128 * n + 128]
                    else:
                        dst = tokens(o[:, 0:T], 2 << (4 * r + n - 2), True)
                    last = mm(dst, v_lv[:, it % 2, n, :], pm[:, it % 2, n, :], start=(r == 0 and n == 0), stop=(r == 2 and n == 1))
                last.then_inc(sem("go_step"), 1)
            def head_squares(h):
                pe.wait_ge(sem("gn_sq"), h + 1)
                mm(bank[h % 2][:, 0:T], ones[:, :], o_rms[:, h % 2, :], start=True, stop=True).then_inc(sem("gn_mm"), 1)
            for it in range(25):
                if it < 24:
                    gla_scores(it)
                if it >= 1:
                    gla_results(it - 1)
                if it % 3 == 1 and it >= 4:
                    head_squares(it // 3 - 1)
            head_squares(7)
            gemm("out2", x_act, 16, act_tile("out2"))
            norm("post2")
        if "ffn0" in plan:
            feed_forward("ffn0", "ffn0")
        if "s5" in plan:
            if "ffn0" not in plan:
                for u in range(24):
                    s5_behind(u)
            norm("s5", u5)
            pe.wait_ge(sem("blhs_cp"), 8)
            pe.wait_ge(scaled, SCALED["s5"] + DT)

            def inputs(tb):
                for n in range(16):
                    bb, i = n // 4, n % 4
                    if tb or n >= 4:
                        pe.wait_ge(sem("bu_cp"), 16 * tb + n - 3)
                    pr = slice(32 * i, 32 * i + 32)
                    for k in range(4):
                        for r in range(2):
                            last = mm(m[i][:, 128 * k + 64 * r:128 * k + 64 * r + 64], b_lhs[pr, r, 4 * bb + k, :],
                                      u5[pr, 4 * bb + k, 64 * tb:64 * tb + 64], start=True, stop=True)
                    last.then_inc(sem("bu_mm"), 1)

            def outputs(tb):
                st = (st0, st1)[tb % 2]
                for h in range(2):
                    pe.wait_ge(scan_step[h], 3 * (64 * tb + 63))
                if tb == 0:
                    pe.wait_ge(sem("c_done"), 4)
                for n in range(2):
                    if tb:
                        pe.wait_ge(sem("y5_add"), 2 * (tb - 1) + n + 1)
                    for k in range(8):
                        for i in range(4):
                            pair = 4 * (8 * n + k) + i
                            for r in range(2):
                                last = mm(m[4 + n][32 * i:32 * i + 32, 64 * k:64 * k + 64], c_lhs[:, r, pair, :],
                                          st[:, :, r, pair], start=(r == 0), stop=(r == 1))
                    last.then_inc(sem("y5_mm"), 1)
            inputs(0)
            for tb in range(4):
                if tb < 3:
                    inputs(tb + 1)
                outputs(tb)
            gemm("glu", x_act, 16, act_tile("glu"))
            norm("post_s5")
        if "ffn1" in plan:
            feed_forward("ffn1", "ffn1")
    ctx.close()


def tiles(w):
    k, n = w.shape
    return w.reshape(k // P, P, n // P, P).transpose(2, 1, 0, 3)


def weight_stream(plan, w):
    table, pairs = phases(plan)
    out = np.zeros((pairs * 4, P, HALF, P), np.float32)

    def put(name, units):
        at = table[name][0] * 4
        for u in units:
            kt = u.shape[1] // 2
            out[at, :, 0:kt] = u[:, :kt]
            out[at + 1, :, 0:kt] = u[:, kt:]
            at += 2
        assert at <= table[name][1] * 4

    def pad(a, n):
        full = np.zeros((a.shape[0], n), np.float32)
        full[:, :a.shape[1]] = a
        return full

    if "mix1" in plan:
        put("in1", tiles(pad(w["in1"], 38 * P)))
        put("cmp", np.concatenate([tiles(w["cmp_k"]), tiles(w["cmp_v"])]))
        put("out1", tiles(w["out1"]))
    if "mlp" in plan:
        up, down = tiles(w["up1"]), tiles(w["down1"])
        for g in range(FF1_GROUPS):
            put(f"up1_{g}", up[16 * g:16 * g + 16])
            put(f"down1_{g}", down[:, :, 16 * g:16 * g + 16])
    if "ple" in plan:
        pj = tiles(w["proj"])
        put("proj", pj.reshape(2, 8, P, 2, P).transpose(0, 2, 1, 3, 4).reshape(2, P, 16, P))
        put("gate", tiles(w["gate"]))
    if "mix2" in plan:
        put("in2", tiles(pad(w["in2"], 50 * P)))
        put("out2", tiles(w["out2"]))
    for s, l in (("ffn0", 0), ("ffn1", 1)):
        if s in plan:
            up, down = tiles(w["up2"][l]), tiles(w["down2"][l])
            n_ff = up.shape[0] // 2
            up = up.reshape(2, n_ff, P, DT, P).transpose(1, 0, 2, 3, 4)
            f = 0
            for g, n in enumerate(FF2_GROUPS):
                put(f"up2_{l}_{g}", up[f:f + n].reshape(2 * n, P, DT, P))
                put(f"down2_{l}_{g}", down[:, :, f:f + n])
                f += n
    if "glu" in table:
        put("glu", tiles(w["glu"]).reshape(2, DT, P, DT, P)[::-1].transpose(1, 0, 2, 3, 4).reshape(2 * DT, P, DT, P))
    return out.reshape(pairs * 4, P, HALF * P)


def bucket(dist):
    n = np.maximum(dist, 0)
    nf = np.maximum(n, 1).astype(np.float32)
    large = 16 + (np.log(nf / 16) / math.log(8) * 16).astype(np.int32)
    return np.where(n < 16, n, np.minimum(large, 31))


def one_hot(dist):
    out = np.zeros((33, len(dist)), np.float32)
    ahead = dist < 0
    out[bucket(dist), np.arange(len(dist))] = ~ahead
    out[32] = ahead
    return out


PLAN = ("mix1", "mlp", "ple", "mix2", "ffn0", "s5", "ffn1")


def kernel(plan=PLAN, **inputs):
    import concourse.bacc as bacc
    from concourse.bass_utils import run_bass_kernel_spmd as run

    a = {k: np.asarray(v) for k, v in inputs.items()}
    heads = [4 * (2 * gp + half) + r for gp in range(2) for r in range(4) for half in range(2)]
    head_cols = np.concatenate([np.arange(64 * h, 64 * h + 64) for h in heads])
    w_in = a["w_in"][0]
    parts = np.split(w_in, np.cumsum([1024, 1024, 1024] + [256] * 6), axis=1)
    gates = parts[9].reshape(D, NH, 3)[:, heads, :].transpose(0, 2, 1).reshape(D, 48)
    w1 = np.concatenate([parts[0], parts[1], parts[2][:, head_cols], *parts[3:9], gates], axis=1)
    w_out = np.concatenate([a["w_out"][0][:1024], a["w_out"][0][1024:][head_cols]], axis=0)
    w = {"in1": w1, "cmp_k": a["cmp_w1_k"][0], "cmp_v": a["cmp_w1_v"][0], "out1": w_out,
         "up1": a["mlp_w1"][0], "down1": a["mlp_w2"][0], "proj": a["ple_proj"][0], "gate": a["ple_gate"][0],
         "in2": a["w_in_2"][0], "out2": a["w_out_2"][0], "glu": a["w_glu_2"][0],
         "up2": a["w_ffn_in_2"], "down2": a["w_ffn_out_2"]}

    cols = np.zeros((P, NCOL), np.float32)

    def put(name, v):
        cols[:, COL[name][0]:COL[name][1]] = v

    by_tile = lambda v: v.reshape(-1, P).T
    for name in ("norm_mix_pre", "norm_mix_post", "norm_mlp_pre", "norm_mlp_post"):
        put(name, by_tile(a[name][0]))
    put("gnorm", by_tile(np.concatenate([a["gnorm_lru"][0], a["gnorm_nsa"][0][head_cols]])))
    put("norms2", by_tile(a["norm_gains_2"].reshape(-1)))
    put("conv_w", by_tile(a["conv_w"][0].reshape(-1)))
    put("conv_b", by_tile(a["conv_b"][0]))
    put("lru_ba", by_tile(a["lru_ba"][0].reshape(-1)))
    put("lru_bx", by_tile(a["lru_bx"][0].reshape(-1)))
    put("lru_lambda", by_tile(a["lru_lambda"][0]))
    put("pe_k", by_tile(a["cmp_pe_k"][0].reshape(-1)))
    put("pe_v", by_tile(a["cmp_pe_v"][0].reshape(-1)))
    w2k = a["cmp_w2_k"][0].reshape(2, P, HD).transpose(1, 0, 2)
    put("w2_k", np.stack([w2k, w2k], axis=2).reshape(P, 256))
    put("w2_v", a["cmp_w2_v"][0].reshape(2, P, HD).transpose(1, 0, 2).reshape(P, 128))
    put("b_gate", by_tile(a["b_gate_2"][0]))
    put("gla_gain", by_tile(a["gla_norm_gain_2"][0]))
    put("d_skip", by_tile(a["s5_d_2"][0]))
    put("any_cmp", (np.arange(P) >= 31).astype(np.float32)[:, None])
    two = lambda v: v.reshape(64, 2, 64).transpose(1, 2, 0).reshape(P, 64)
    put("lam_re", two(a["s5_lambda_re_2"][0]))
    put("lam_im", two(a["s5_lambda_im_2"][0]))
    put("log_step", np.repeat(a["s5_log_step_2"][0].reshape(64, 2).T[:, None, :], 64, axis=1).reshape(P, 64))

    lru = np.stack([a["lru_wa"][0], a["lru_wx"][0]]).reshape(2, LT, 2, HD, HD).transpose(2, 3, 0, 1, 4).reshape(P, 2, LT, HD)
    hot = np.concatenate([one_hot(np.arange(511) - 255), one_hot(255 - np.arange(384))], axis=1)
    key, query = np.arange(P)[:, None], np.arange(P)[None, :]
    strict = np.where(key < query, 0.0, NEG).astype(np.float32)
    sb = np.concatenate([strict, np.zeros((P, P), np.float32), strict, -(key >= query).astype(np.float32)], axis=1)
    eye = np.eye(P, dtype=np.float32)
    gla = np.stack([eye, eye] + [(key // (1 << l) == query // (1 << l)).astype(np.float32) for l in range(LEVELS)], axis=1)
    s5b = np.stack([a[k][0].reshape(64, 2, 64, 16).transpose(1, 2, 0, 3).reshape(P, 64, 16) for k in ("s5_b_re_2", "s5_b_im_2")], axis=1)
    s5c = np.stack([a[k][0].reshape(64, 2, 16, 64).transpose(1, 3, 0, 2).reshape(P, 64, 16) for k in ("s5_c_re_2", "s5_c_im_2")], axis=1)

    arrays = {
        "x_t": a["x"][0].T, "stream": weight_stream(plan, w), "columns": cols, "p_t": a["p"][0, 0].T,
        "lru_w": lru, "onehot": hot, "rel_bias": a["rel_bias"][:, heads], "sb_mask": sb, "gla_masks": gla,
        "gate_up": a["w_gate_up_2"][0], "s5_b": s5b, "s5_c": s5c,
    }
    arrays = {k: np.ascontiguousarray(v) for k, v in arrays.items()}
    nc = bacc.Bacc("TRN2", target_bir_lowering=False, num_devices=1)
    args = {k: nc.dram_tensor(k, v.shape, mybir.dt.from_np(v.dtype), kind="ExternalInput").ap() for k, v in arrays.items()}
    args["toeplitz"] = nc.dram_tensor("toeplitz", (NH, P, 384), F32, kind="Internal").ap()
    out = nc.dram_tensor("out", (D, T), F32, kind="ExternalOutput").ap()
    build(nc, plan, out=out, **args)
    r = run(nc, [arrays], core_ids=[0])
    return np.ascontiguousarray(r.results[0]["out"].T)[None]
```
